# Optimizing a Trainium2 kernel written in Bass

```python
import math, functools
import jax, jax.numpy as jnp
from jax import lax
import numpy as np
import math

D_MODEL = 1024
BATCH = 1
SEQ = 1024
DEPTH = 1

CTX_LEN = 256
GRID_W = 64
ROPE_THETA = 10000.0
NORM_EPS = 1e-6
Q_BLOCK = 128

A_HEADS = 4
A_HEAD_DIM = 64
A_WIDTH = A_HEADS * 2 * A_HEAD_DIM
B_HEADS = 8
B_NOPE = 64
B_ROPE = 32
B_VDIM = 64
B_Q_RANK = 256
B_KV_RANK = 128
B_WIDTH = B_HEADS * B_VDIM
MIX_WIDTH = A_WIDTH + B_WIDTH
IN_WIDTH = 3 * A_WIDTH + B_Q_RANK + B_KV_RANK + B_ROPE
SPLIT_POINTS = (A_WIDTH, 2 * A_WIDTH, 3 * A_WIDTH, 3 * A_WIDTH + B_Q_RANK,
                3 * A_WIDTH + B_Q_RANK + B_KV_RANK)
FFN_HIDDEN = -(-8 * D_MODEL // (3 * 256)) * 256


def _rmsnorm(x, gain=None):
    x32 = x.astype(jnp.float32)
    y = x32 * lax.rsqrt(jnp.mean(x32 * x32, axis=-1, keepdims=True) + NORM_EPS)
    if gain is not None:
        y = y * gain.astype(jnp.float32)
    return y.astype(x.dtype)

def _modulate(h, shift, scale):
    return h * (1 + scale) + shift

def _axial_rope(x, row, col):
    half = x.shape[-1] // 2
    quarter = half // 2
    inv = ROPE_THETA ** (-jnp.arange(quarter, dtype=jnp.float32) / quarter)

    def rot(xa, pos):
        ang = pos.astype(jnp.float32)[:, None] * inv[None, :]
        cos = jnp.concatenate([jnp.cos(ang)] * 2, -1)[None, :, None, :]
        sin = jnp.concatenate([jnp.sin(ang)] * 2, -1)[None, :, None, :]
        xa32 = xa.astype(jnp.float32)
        rotated = jnp.concatenate([-xa32[..., quarter:], xa32[..., :quarter]], -1)
        return (xa32 * cos + rotated * sin).astype(x.dtype)

    return jnp.concatenate([rot(x[..., :half], row), rot(x[..., half:], col)], -1)

def _project(h, w_in, q_a_norm, kv_a_norm, w_q_up, w_kv_up, pos):
    nb, s, _ = h.shape
    qa, ka, va, cq, ckv, krope = jnp.split(h @ w_in, SPLIT_POINTS, axis=-1)
    qa = qa.reshape(nb, s, A_HEADS, 2, A_HEAD_DIM)
    ka = ka.reshape(nb, s, A_HEADS, 2, A_HEAD_DIM)
    q1, q2 = qa[..., 0, :], qa[..., 1, :]
    k1, k2 = ka[..., 0, :], ka[..., 1, :]
    va = va.reshape(nb, s, A_HEADS, 2 * A_HEAD_DIM)
    qb = (_rmsnorm(cq, q_a_norm) @ w_q_up).reshape(nb, s, B_HEADS, B_NOPE + B_ROPE)
    kvb = (_rmsnorm(ckv, kv_a_norm) @ w_kv_up).reshape(nb, s, B_HEADS, B_NOPE + B_VDIM)
    q_nope, q_rope = qb[..., :B_NOPE], qb[..., B_NOPE:]
    k_nope, vb = kvb[..., :B_NOPE], kvb[..., B_NOPE:]
    krope = krope[:, :, None, :]
    if pos is not None:
        row, col = pos
        q1, q2, k1, k2 = (_axial_rope(t, row, col) for t in (q1, q2, k1, k2))
        q_rope = _axial_rope(q_rope, row, col)
        krope = _axial_rope(krope, row, col)
    qb = jnp.concatenate([q_nope, q_rope], -1)
    kb = jnp.concatenate([k_nope, jnp.broadcast_to(krope, (nb, s, B_HEADS, B_ROPE))], -1)
    return q1, q2, k1, k2, va, qb, kb, vb

def _diff_attend(q1, q2, k1, k2, v, lam):
    scale = A_HEAD_DIM ** -0.5
    s1 = jnp.einsum('bqhd,bkhd->bhqk', q1, k1).astype(jnp.float32) * scale
    s2 = jnp.einsum('bqhd,bkhd->bhqk', q2, k2).astype(jnp.float32) * scale
    a = jax.nn.softmax(s1, axis=-1) - lam * jax.nn.softmax(s2, axis=-1)
    return jnp.einsum('bhqk,bkhe->bqhe', a.astype(v.dtype), v)

def _softmax_attend(q, k, v):
    scale = (B_NOPE + B_ROPE) ** -0.5
    s = jnp.einsum('bqhd,bkhd->bhqk', q, k).astype(jnp.float32) * scale
    a = jax.nn.softmax(s, axis=-1)
    return jnp.einsum('bhqk,bkhe->bqhe', a.astype(v.dtype), v)

def _map_query_blocks(fn, *qs):
    nb, s = qs[0].shape[:2]
    n_blk = s // Q_BLOCK
    blocks = tuple(jnp.moveaxis(q.reshape(nb, n_blk, Q_BLOCK, *q.shape[2:]), 1, 0) for q in qs)
    out = lax.map(lambda blk: fn(*blk), blocks)
    out = jnp.moveaxis(out, 0, 1)
    return out.reshape(nb, s, *out.shape[3:])

def _merge_heads(oa, ob, lam_init, diff_subln, w_out):
    nb, s = oa.shape[:2]
    oa = _rmsnorm(oa, diff_subln) * (1 - lam_init)
    cat = jnp.concatenate([oa.reshape(nb, s, A_WIDTH), ob.reshape(nb, s, B_WIDTH)], -1)
    return cat @ w_out

def _swiglu(h, w_ffn_in, w_ffn_out):
    gate, up = jnp.split(h @ w_ffn_in, 2, axis=-1)
    return (jax.nn.silu(gate) * up) @ w_ffn_out

def _layer(x_lat, x_ctx, row, col, c, c_ctx, w_ada, b_ada, w_in, q_a_norm, kv_a_norm,
           w_q_up, w_kv_up, diff_lambda, diff_subln, w_out, w_ffn_in, w_ffn_out,
           layer_idx, update_ctx):
    lam_init = 0.8 - 0.6 * math.exp(-0.3 * layer_idx)
    lp = diff_lambda.astype(jnp.float32)
    lam = jnp.exp(jnp.sum(lp[0] * lp[1])) - jnp.exp(jnp.sum(lp[2] * lp[3])) + lam_init

    sh_a, sc_a, g_a, sh_f, sc_f, g_f = jnp.split((jax.nn.silu(c) @ w_ada + b_ada)[:, None, :], 6, axis=-1)
    csh_a, csc_a, cg_a, csh_f, csc_f, cg_f = jnp.split(jax.nn.silu(c_ctx) @ w_ada + b_ada, 6, axis=-1)

    proj = functools.partial(_project, w_in=w_in, q_a_norm=q_a_norm, kv_a_norm=kv_a_norm,
                             w_q_up=w_q_up, w_kv_up=w_kv_up)
    h_lat = _modulate(_rmsnorm(x_lat), sh_a, sc_a)
    h_ctx = _modulate(_rmsnorm(x_ctx), csh_a, csc_a)
    lq1, lq2, lk1, lk2, lva, lqb, lkb, lvb = proj(h_lat, pos=(row, col))
    cq1, cq2, ck1, ck2, cva, cqb, ckb, cvb = proj(h_ctx, pos=None)

    k1 = jnp.concatenate([ck1, lk1], axis=1)
    k2 = jnp.concatenate([ck2, lk2], axis=1)
    va = jnp.concatenate([cva, lva], axis=1)
    kb = jnp.concatenate([ckb, lkb], axis=1)
    vb = jnp.concatenate([cvb, lvb], axis=1)
    oa = _map_query_blocks(lambda q1, q2: _diff_attend(q1, q2, k1, k2, va, lam), lq1, lq2)
    ob = _map_query_blocks(lambda q: _softmax_attend(q, kb, vb), lqb)
    new_lat = x_lat + g_a * _merge_heads(oa, ob, lam_init, diff_subln, w_out)
    h = _modulate(_rmsnorm(new_lat), sh_f, sc_f)
    new_lat = new_lat + g_f * _swiglu(h, w_ffn_in, w_ffn_out)

    if update_ctx:
        oac = _diff_attend(cq1, cq2, ck1, ck2, cva, lam)
        obc = _softmax_attend(cqb, ckb, cvb)
        new_ctx = x_ctx + cg_a * _merge_heads(oac, obc, lam_init, diff_subln, w_out)
        hc = _modulate(_rmsnorm(new_ctx), csh_f, csc_f)
        new_ctx = new_ctx + cg_f * _swiglu(hc, w_ffn_in, w_ffn_out)
    else:
        new_ctx = x_ctx
    return new_lat, new_ctx

def first_inputs(seed: int = 0) -> dict:
    key = jax.random.key(seed)
    ks = jax.random.split(key, 17)
    f32 = jnp.float32

    def nrm(k, shape, scale):
        return jax.random.normal(k, shape, f32) * scale

    return {
        "x": nrm(ks[0], (BATCH, SEQ, D_MODEL), 1.0),
        "c": nrm(ks[1], (BATCH, D_MODEL), 1.0),
        "ctx": nrm(ks[2], (BATCH, CTX_LEN, D_MODEL), 1.0),
        "c_ctx": nrm(ks[3], (D_MODEL,), 1.0),
        "w_ada": nrm(ks[4], (DEPTH, D_MODEL, 6 * D_MODEL), 0.5 * D_MODEL ** -0.5),
        "b_ada": nrm(ks[5], (DEPTH, 6 * D_MODEL), 0.01),
        "w_in": nrm(ks[6], (DEPTH, D_MODEL, IN_WIDTH), D_MODEL ** -0.5),
        "q_a_norm": 1.0 + nrm(ks[7], (DEPTH, B_Q_RANK), 0.05),
        "kv_a_norm": 1.0 + nrm(ks[8], (DEPTH, B_KV_RANK), 0.05),
        "w_q_up": nrm(ks[9], (DEPTH, B_Q_RANK, B_HEADS * (B_NOPE + B_ROPE)), B_Q_RANK ** -0.5),
        "w_kv_up": nrm(ks[10], (DEPTH, B_KV_RANK, B_HEADS * (B_NOPE + B_VDIM)), B_KV_RANK ** -0.5),
        "diff_lambda": nrm(ks[11], (DEPTH, 4, A_HEAD_DIM), 0.1),
        "diff_subln": 1.0 + nrm(ks[12], (DEPTH, 2 * A_HEAD_DIM), 0.05),
        "w_out": nrm(ks[13], (DEPTH, MIX_WIDTH, D_MODEL), MIX_WIDTH ** -0.5),
        "w_ffn_in": nrm(ks[14], (DEPTH, D_MODEL, 2 * FFN_HIDDEN), D_MODEL ** -0.5),
        "w_ffn_out": nrm(ks[15], (DEPTH, FFN_HIDDEN, D_MODEL), FFN_HIDDEN ** -0.5),
        "final_norm": 1.0 + nrm(ks[16], (D_MODEL,), 0.05),
    }

def first_block(x, c, ctx, c_ctx, w_ada, b_ada, w_in, q_a_norm, kv_a_norm, w_q_up, w_kv_up,
              diff_lambda, diff_subln, w_out, w_ffn_in, w_ffn_out, final_norm):
    seq = x.shape[1]
    rows = seq // GRID_W
    row = jnp.repeat(jnp.arange(rows, dtype=jnp.int32), GRID_W)
    col = jnp.tile(jnp.arange(GRID_W, dtype=jnp.int32), rows)
    x_lat, x_ctx = x, ctx
    for layer in range(DEPTH):
        x_lat, x_ctx = _layer(
            x_lat, x_ctx, row, col, c, c_ctx,
            w_ada[layer], b_ada[layer], w_in[layer], q_a_norm[layer], kv_a_norm[layer],
            w_q_up[layer], w_kv_up[layer], diff_lambda[layer], diff_subln[layer],
            w_out[layer], w_ffn_in[layer], w_ffn_out[layer],
            layer_idx=layer, update_ctx=(layer < DEPTH - 1))
    return _rmsnorm(x_lat, final_norm)


HEAD_DIM = 128
DN_HEADS = D_MODEL // 256
DN_WIDTH = DN_HEADS * HEAD_DIM
CONV_WIDTH = 4
CHUNK = 64
SWA_GROUPS = ((128, 1), (512, 4), (2048, 16))
N_GROUPS = 3
SWA_HEADS = D_MODEL // 256
SWA_WIDTH = SWA_HEADS * HEAD_DIM
ROPE_DIM = HEAD_DIM // 4
ROPE_THETA_2 = 500000.0
N_BRANCHES = 2
EPS = 1e-6
NEG_INF = -1e30

IN_SIZES = (3 * DN_WIDTH, DN_WIDTH, DN_HEADS, DN_HEADS,
            N_GROUPS * SWA_WIDTH, N_GROUPS * SWA_WIDTH, N_GROUPS * SWA_WIDTH, SWA_WIDTH,
            N_BRANCHES * D_MODEL)
IN_COLS = sum(IN_SIZES)


def rms_norm(x, w):
    xf = x.astype(jnp.float32)
    y = xf * lax.rsqrt(jnp.mean(xf * xf, axis=-1, keepdims=True) + EPS)
    return y.astype(x.dtype) * w.astype(x.dtype)

def l2_normalize(x):
    return x * lax.rsqrt(jnp.sum(x * x, axis=-1, keepdims=True) + EPS)

def causal_depthwise_conv(x, w):
    c = x.shape[-1]
    return lax.conv_general_dilated(x, w.astype(x.dtype), window_strides=(1,), padding=[(CONV_WIDTH - 1, 0)],
                                    dimension_numbers=('NWC', 'WIO', 'NWC'), feature_group_count=c)

def partial_rope(x, cos, sin):
    half = ROPE_DIM // 2
    x1, x2, xp = x[..., :half], x[..., half:ROPE_DIM], x[..., ROPE_DIM:]
    c = cos[:, None, None, :].astype(x.dtype)
    s = sin[:, None, None, :].astype(x.dtype)
    return jnp.concatenate([x1 * c - x2 * s, x2 * c + x1 * s, xp], axis=-1)

def gated_delta_rule_chunked(q, k, v, g, beta):
    B, H, T, Dk = q.shape
    Dv = v.shape[-1]
    N = T // CHUNK
    q = q.reshape(B, H, N, CHUNK, Dk)
    k = k.reshape(B, H, N, CHUNK, Dk)
    v = v.reshape(B, H, N, CHUNK, Dv)
    g = g.reshape(B, H, N, CHUNK)
    beta = beta.reshape(B, H, N, CHUNK)
    gc = jnp.cumsum(g, axis=-1)
    idx = jnp.arange(CHUNK)
    causal = idx[:, None] >= idx[None, :]
    strict = idx[:, None] > idx[None, :]
    decay = jnp.exp(jnp.where(causal, gc[..., :, None] - gc[..., None, :], -jnp.inf))
    kb = k * beta[..., None]
    lower = jnp.where(strict, jnp.einsum('bhnid,bhnjd->bhnij', kb, k) * decay, 0.0)
    eye = jnp.eye(CHUNK, dtype=q.dtype)
    tmat = lax.linalg.triangular_solve(eye + lower, jnp.broadcast_to(eye, lower.shape),
                                       left_side=True, lower=True, unit_diagonal=True)
    u = jnp.einsum('bhnij,bhnjd->bhnid', tmat, v * beta[..., None])
    w = jnp.einsum('bhnij,bhnjd->bhnid', tmat, kb * jnp.exp(gc)[..., None])
    a_intra = jnp.where(causal, jnp.einsum('bhnid,bhnjd->bhnij', q, k) * decay, 0.0)

    def step(S, inp):
        qi, ki, ui, wi, ai, gci = inp
        v_new = ui - jnp.einsum('bhck,bhkv->bhcv', wi, S)
        o = jnp.einsum('bhck,bhkv->bhcv', qi * jnp.exp(gci)[..., None], S) + jnp.einsum('bhij,bhjv->bhiv', ai, v_new)
        glast = gci[..., -1]
        S = S * jnp.exp(glast)[..., None, None] + jnp.einsum(
            'bhck,bhcv->bhkv', ki * jnp.exp(glast[..., None] - gci)[..., None], v_new)
        return S, o

    xs = tuple(jnp.moveaxis(a, 2, 0) for a in (q, k, u, w, a_intra, gc))
    s0 = jnp.zeros((B, H, Dk, Dv), q.dtype)
    _, o = lax.scan(step, s0, xs)
    return jnp.moveaxis(o, 0, 2).reshape(B, H, T, Dv)

def dilated_window_attention(q, k, v, window, dilation):
    B, T, H, Dh = q.shape
    L = T // dilation
    blk = window // dilation
    nb = -(-L // blk)
    Lp = nb * blk

    def to_sub(x):
        x = x.astype(jnp.float32).reshape(B, L, dilation, H, Dh).transpose(0, 2, 3, 1, 4)
        return jnp.pad(x, ((0, 0), (0, 0), (0, 0), (0, Lp - L), (0, 0)))

    def windows(x):
        xp = jnp.pad(x, ((0, 0), (0, 0), (0, 0), (blk, 0), (0, 0))).reshape(B, dilation, H, nb + 1, blk, Dh)
        return jnp.concatenate([xp[:, :, :, :-1], xp[:, :, :, 1:]], axis=4)

    qb = to_sub(q).reshape(B, dilation, H, nb, blk, Dh)
    kw = windows(to_sub(k))
    vw = windows(to_sub(v))
    s = jnp.einsum('brhnqd,brhnkd->brhnqk', qb, kw) * (Dh ** -0.5)
    i = jnp.arange(blk)[:, None]
    j = jnp.arange(2 * blk)[None, :]
    dist = blk + i - j
    key_pos = (jnp.arange(nb)[:, None, None] - 1) * blk + j[None]
    valid = (dist >= 0)[None] & (dist <= blk)[None] & (key_pos >= 0)
    s = jnp.where(valid, s, NEG_INF)
    lse = jax.nn.logsumexp(s, axis=-1)
    p = jnp.exp(s - lse[..., None])
    o = jnp.einsum('brhnqk,brhnkd->brhnqd', p, vw)
    o = o.reshape(B, dilation, H, Lp, Dh)[:, :, :, :L].transpose(0, 3, 1, 2, 4).reshape(B, T, H, Dh)
    lse = lse.reshape(B, dilation, H, Lp)[..., :L].transpose(0, 3, 1, 2).reshape(B, T, H)
    return o, lse

def second_inputs(seed: int = 0) -> dict:
    key = jax.random.key(seed)
    ks = jax.random.split(key, 13)
    f32 = jnp.float32
    x = jax.random.normal(ks[0], (BATCH, SEQ, D_MODEL), f32)
    norm_w = 1.0 + 0.02 * jax.random.normal(ks[1], (DEPTH, D_MODEL), f32)
    w_in = jax.random.normal(ks[2], (DEPTH, D_MODEL, IN_COLS), f32) * D_MODEL ** -0.5
    conv_w = jax.random.normal(ks[3], (DEPTH, CONV_WIDTH, 1, 3 * DN_WIDTH), f32) * CONV_WIDTH ** -0.5
    dn_a_log = jnp.log(jax.random.uniform(ks[4], (DEPTH, DN_HEADS), f32, 1.0, 16.0))
    dn_dt_bias = 0.1 * jax.random.normal(ks[5], (DEPTH, DN_HEADS), f32)
    dn_norm_w = 1.0 + 0.02 * jax.random.normal(ks[6], (DEPTH, HEAD_DIM), f32)
    q_norm_w = 1.0 + 0.02 * jax.random.normal(ks[7], (DEPTH, N_GROUPS, HEAD_DIM), f32)
    k_norm_w = 1.0 + 0.02 * jax.random.normal(ks[8], (DEPTH, N_GROUPS, HEAD_DIM), f32)
    w_branch_dn = jax.random.normal(ks[9], (DEPTH, DN_WIDTH, D_MODEL), f32) * DN_WIDTH ** -0.5
    w_branch_swa = jax.random.normal(ks[10], (DEPTH, SWA_WIDTH, D_MODEL), f32) * SWA_WIDTH ** -0.5
    w_out = jax.random.normal(ks[11], (DEPTH, D_MODEL, D_MODEL), f32) * D_MODEL ** -0.5
    return {"x": x, "norm_w": norm_w, "w_in": w_in, "conv_w": conv_w, "dn_a_log": dn_a_log,
            "dn_dt_bias": dn_dt_bias, "dn_norm_w": dn_norm_w, "q_norm_w": q_norm_w, "k_norm_w": k_norm_w,
            "w_branch_dn": w_branch_dn, "w_branch_swa": w_branch_swa, "w_out": w_out}

def second_block(x, norm_w, w_in, conv_w, dn_a_log, dn_dt_bias, dn_norm_w, q_norm_w, k_norm_w,
              w_branch_dn, w_branch_swa, w_out):
    B, T, _ = x.shape
    split_points = [int(p) for p in np.cumsum(IN_SIZES)[:-1]]
    pos = jnp.arange(T, dtype=jnp.float32)
    inv_freq = ROPE_THETA_2 ** (-jnp.arange(0, ROPE_DIM, 2, dtype=jnp.float32) / ROPE_DIM)
    ang = pos[:, None] * inv_freq[None, :]
    cos, sin = jnp.cos(ang), jnp.sin(ang)

    for layer in range(DEPTH):
        h = rms_norm(x, norm_w[layer])
        proj = h @ w_in[layer]
        (dn_qkv, dn_z, dn_b, dn_a, swa_q, swa_k, swa_v, swa_z, gates) = jnp.split(proj, split_points, axis=-1)

        qkv = jax.nn.silu(causal_depthwise_conv(dn_qkv, conv_w[layer]))
        dq, dk, dv = jnp.split(qkv.astype(jnp.float32), 3, axis=-1)
        to_heads = lambda t: t.reshape(B, T, DN_HEADS, HEAD_DIM).transpose(0, 2, 1, 3)
        dq = l2_normalize(to_heads(dq)) * (HEAD_DIM ** -0.5)
        dk = l2_normalize(to_heads(dk))
        dv = to_heads(dv)
        beta = jax.nn.sigmoid(dn_b.astype(jnp.float32)).transpose(0, 2, 1)
        g = (-jnp.exp(dn_a_log[layer].astype(jnp.float32))
             * jax.nn.softplus(dn_a.astype(jnp.float32) + dn_dt_bias[layer].astype(jnp.float32))).transpose(0, 2, 1)
        o_dn = gated_delta_rule_chunked(dq, dk, dv, g, beta).transpose(0, 2, 1, 3).astype(x.dtype)
        o_dn = rms_norm(o_dn, dn_norm_w[layer]) * jax.nn.silu(dn_z.reshape(B, T, DN_HEADS, HEAD_DIM))
        y_dn = o_dn.reshape(B, T, DN_WIDTH) @ w_branch_dn[layer]

        grp = lambda t: t.reshape(B, T, N_GROUPS, SWA_HEADS, HEAD_DIM)
        sq = partial_rope(rms_norm(grp(swa_q), q_norm_w[layer][:, None, :]), cos, sin)
        sk = partial_rope(rms_norm(grp(swa_k), k_norm_w[layer][:, None, :]), cos, sin)
        sv = grp(swa_v)
        outs, lses = [], []
        for gi, (window, dilation) in enumerate(SWA_GROUPS):
            o_g, lse_g = dilated_window_attention(sq[:, :, gi], sk[:, :, gi], sv[:, :, gi], window, dilation)
            outs.append(o_g)
            lses.append(lse_g)
        alpha = jax.nn.softmax(jnp.stack(lses, axis=0), axis=0)
        o_swa = jnp.sum(alpha[..., None] * jnp.stack(outs, axis=0), axis=0).astype(x.dtype)
        o_swa = o_swa * jax.nn.silu(swa_z.reshape(B, T, SWA_HEADS, HEAD_DIM))
        y_swa = o_swa.reshape(B, T, SWA_WIDTH) @ w_branch_swa[layer]

        g_dn, g_swa = jnp.split(gates, 2, axis=-1)
        merged = jax.nn.sigmoid(g_dn) * y_dn + jax.nn.sigmoid(g_swa) * y_swa
        x = x + merged @ w_out[layer]
    return x


def setup_inputs(seed=0):
    out = dict(first_inputs(seed))
    for name, value in second_inputs(seed + 1).items():
        if name != "x":
            out[name + "_2"] = value
    return out


def reference(
    x, c, ctx, c_ctx, w_ada, b_ada, w_in, q_a_norm, kv_a_norm, w_q_up, w_kv_up, diff_lambda,
    diff_subln, w_out, w_ffn_in, w_ffn_out, final_norm, norm_w_2, w_in_2, conv_w_2, dn_a_log_2,
    dn_dt_bias_2, dn_norm_w_2, q_norm_w_2, k_norm_w_2, w_branch_dn_2, w_branch_swa_2, w_out_2,
):
    x = first_block(
        x, c, ctx, c_ctx, w_ada, b_ada, w_in, q_a_norm, kv_a_norm, w_q_up, w_kv_up, diff_lambda,
        diff_subln, w_out, w_ffn_in, w_ffn_out, final_norm,
    )
    return second_block(
        x, norm_w_2, w_in_2, conv_w_2, dn_a_log_2, dn_dt_bias_2, dn_norm_w_2, q_norm_w_2,
        k_norm_w_2, w_branch_dn_2, w_branch_swa_2, w_out_2,
    )


_drawn_inputs = setup_inputs


def setup_inputs(seed=0):
    import zlib

    import numpy as np

    out = dict(_drawn_inputs(seed))
    spreads = {}
    factors = {'b_ada': 4.157,
     'q_a_norm': 8.0,
     'kv_a_norm': 8.0,
     'w_q_up': 2.717,
     'diff_lambda': 4.982,
     'diff_subln': 5.815,
     'norm_w_2': 5.251,
     'dn_dt_bias_2': 8.0,
     'dn_norm_w_2': 8.0,
     'q_norm_w_2': 8.0,
     'k_norm_w_2': 8.0}
    for name, (base, spread) in spreads.items():
        noise = np.random.default_rng([zlib.crc32(name.encode()), seed]).standard_normal(out[name].shape)
        drawn = base * np.exp(spread * noise) if base else spread * noise
        out[name] = __import__('jax').numpy.asarray(drawn.astype(out[name].dtype))
    for name, factor in factors.items():
        out[name] = (out[name] * factor).astype(out[name].dtype)
    return out
```

```python
import math
from contextlib import ExitStack

import numpy as np
import concourse.bass as bass
from concourse import mybir

F32 = mybir.dt.float32
F32R = mybir.dt.float32r
ALU = mybir.AluOpType
ACT = mybir.ActivationFunctionType
AX_X = mybir.AxisListType.X
ds = bass.ds

P = 128
D = 1024
KT = D // P
LAT, CTX = 1024, 256
TOK = LAT + CTX
NQ = LAT // P
NKEY = TOK // P
BANK = 512
EPS = 1e-6
A_HEADS, B_HEADS = 4, 8
QR, KVR = 256, 128
BD, NOPE, ROPE_B = 96, 64, 32
FFN = 2816
FT = FFN // P
LAM_INIT = 0.8 - 0.6 * math.exp(0.0)
SCALE_A = 64.0 ** -0.5
SCALE_B = 96.0 ** -0.5
SCALE_S = 128.0 ** -0.5
DN = 4
GROUPS = ((128, 1), (512, 4), (2048, 16))
PAD = 8
LEVELS = 7
C_Z, C_B, C_SQ = 1536, 2048, 2056
C_SK, C_SV, C_SZ = C_SQ + 1536, C_SQ + 3072, C_SQ + 4608
C_G = C_SZ + 512
ROWS = [("b_ada", 48), ("c", 8), ("c_ctx", 8), ("final_norm", 8), ("norm_w_2", 8), ("q_a_norm", 2),
        ("kv_a_norm", 1), ("diff_subln", 1), ("dn_norm_w_2", 1), ("q_norm_w_2", 3), ("k_norm_w_2", 3)]
ROW_AT = {}
for _name, _n in ROWS:
    ROW_AT[_name] = sum(n for _, n in ROWS[:len(ROW_AT)])
N_ROWS = sum(n for _, n in ROWS)
CONV_AT = 96
M_Q, M_K, M_V, M_C = 0, 2, 4, 6
M_OUT = 8
M_FFN = 12
M_DN = M_FFN + 3 * (FT // 2)
M_SWA = M_DN + 8
M_GATE = M_SWA + 5 * DN
M_BRANCH = M_GATE + 8
M_OUT2 = M_BRANCH + 4
PAIRS = M_OUT2 + 4


def shape_tables():
    eye = np.eye(P, dtype=np.float32)
    i, j = np.arange(P)[:, None], np.arange(P)[None, :]

    def rot(block, lo, hi):
        r = np.zeros((P, P), np.float32)
        for a in range(lo, hi):
            up = (a - lo) % block < block // 2
            r[a, a + block // 2 if up else a - block // 2] = -1.0 if up else 1.0
        return r.T
    mats = [eye, np.full((P, P), 1.0 / P, np.float32), rot(32, 0, 128), rot(16, 64, 96), rot(32, 0, 32),
            (i <= j).astype(np.float32)]
    mats.append(((i // 2 == j // 2) & (i % 2 == 0) & (j % 2 == 1)).astype(np.float32))
    for lv in range(1, LEVELS):
        s = 1 << lv
        mats.append(((i // (2 * s) == j // (2 * s)) & (i // s % 2 == 1) & (j // s % 2 == 0)).astype(np.float32))
    consts = np.concatenate(mats, axis=1).astype(np.float32)

    t = np.arange(LAT)
    row, col = (t // 64).astype(np.float32), (t % 64).astype(np.float32)

    def axial(quarter, lo, n):
        inv = (np.float32(10000.0) ** (-np.arange(quarter, dtype=np.float32) / np.float32(quarter))).astype(np.float32)
        cos, sin = np.ones((P, LAT), np.float32), np.zeros((P, LAT), np.float32)
        for a in range(lo, lo + n):
            b = a - lo
            pos = row if (b // (2 * quarter)) % 2 == 0 else col
            ang = pos * inv[b % quarter]
            cos[a], sin[a] = np.cos(ang), np.sin(ang)
        return np.stack([cos, sin], 1)
    trig_a, trig_b = axial(16, 0, 128), axial(8, 64, 32)
    inv = (np.float32(500000.0) ** (-np.arange(0, 32, 2, dtype=np.float32) / np.float32(32))).astype(np.float32)
    cos, sin = np.ones((P, LAT), np.float32), np.zeros((P, LAT), np.float32)
    for a in range(32):
        ang = t.astype(np.float32) * inv[a % 16]
        cos[a], sin[a] = np.cos(ang), np.sin(ang)
    trig_s = np.stack([cos, sin], 1)
    strips = []
    for window, dil in GROUPS:
        n = min(window // P, NQ - 1)
        for back in range(n, -1, -1):
            dist = back * P + i - j
            ok = (dist >= 0) & (dist <= window) & (dist % dil == 0)
            strips.append(np.where(ok, 0.0, -1e30).astype(np.float32))
    window_mask = np.concatenate(strips, axis=1)
    f = lambda a: np.ascontiguousarray(a, np.float32)
    return dict(consts=f(consts), trig_a=f(trig_a), trig_b=f(trig_b), trig_s=f(trig_s), window_mask=f(window_mask))


SWA_COLS = [C_SQ + g * 512 for g in range(3)] + [C_SK + g * 512 for g in range(3)] + [C_SV + g * 512 for g in range(3)] + [C_SZ]


def window_tiles(n):
    out = []
    for g in range(3):
        for kt in range(max(0, n + 1 - SPAN[g]), n + 1):
            out.append((g, kt, len(out) * P))
    return out


SPAN = [min(w // P, NQ - 1) + 1 for w, _ in GROUPS]
STRIP = [sum(SPAN[:g]) * P for g in range(3)]
MASK_W = sum(SPAN) * P
BATCHES = [-(-len(window_tiles(n)) // 4) for n in range(NQ)]
ALL_BATCHES = sum(BATCHES)


def build(nc, t):
    ctx = ExitStack()
    sem = lambda name: ctx.enter_context(nc.semaphore(name))
    pair = lambda name: [sem(f"{name}_{s}") for s in range(2)]
    base = 16512

    def at(name, off, *shape, dt=F32):
        return nc.alloc_sbuf_tensor_at(name, [P, *shape], dt, offset=base + 4 * off)

    w_raw = at("w_raw", 0, 2, KT, P)
    w_hi = at("w_hi", 2048, 2, KT, P, dt=F32R)
    w_lo = at("w_lo", 4096, 2, KT, P, dt=F32R)
    consts = at("consts", 6144, 6 + LEVELS, P)
    ident, ones_mean, rot_a, rot_b, rot_s, tri = (consts[:, n, :] for n in range(6))
    level = [consts[:, 6 + n, :] for n in range(LEVELS)]
    pcol = at("pcol", 7808, 144)
    ada = at("ada", 7952, 48, 2)
    ada_1 = at("ada_1", 8048, 48, 2)
    lam_in = at("lam_in", 8144, 2, 2, 64)
    lam_prod = at("lam_prod", 8400, 2, 64)
    silu_c = at("silu_c", 8528, KT, 2)
    lam_e = at("lam_e", 8544, 2)
    lam = at("lam", 8552, 1)
    alog = at("alog", 8560, 4)
    dtb = at("dtb", 8568, 4)
    ealog = at("ealog", 8576, 4)
    zero = at("zero", 8584, 1)
    subln = at("subln", 8592, 1)
    A0 = 8704

    x_tile = at("x_tile", A0 + 40000, 2, D)
    param_rows = at("param_rows", A0 + 42048, 2, P)
    ada_w = at("ada_w", A0 + 12288, 2, KT, BANK)
    xt5 = at("xt5", A0, KT, TOK)
    xt = at("xt", A0, KT, LAT)
    h_hi = at("h_hi", A0 + 10240, KT, TOK, dt=F32R)
    h_lo = at("h_lo", A0 + 20480, KT, TOK, dt=F32R)
    n_u = at("n_u", A0 + 30720, KT, BANK)
    n_rs = at("n_rs", A0 + 34816, BANK)
    q_a = at("q_a", A0, A_HEADS, LAT)
    k_a = at("k_a", A0 + 4096, A_HEADS, TOK)
    v_a = at("v_a", A0 + 30720, NKEY, 512)
    cq = at("cq", A0 + 35840, 2, LAT)
    ckv = at("ckv", A0 + 37888, TOK)
    kr = at("kr", A0 + 39168, TOK)
    cos_a = at("cos_a", A0 + 9216, LAT)
    sin_a = at("sin_a", A0 + 40448, LAT)
    rope_tmp = at("rope_tmp", A0 + 41472, 2, LAT)
    v_tmp = at("v_tmp", A0 + 40448, 2, TOK)
    att = at("att", A0 + 10240, NQ, D)
    e_a = at("e_a", A0 + 18432, 2, 2, TOK)
    prob = at("prob", A0 + 23552, 2, TOK)
    pt = at("pt", A0 + 26112, TOK)
    qs = at("qs", A0 + 27392, 2, LAT)
    st_a = at("st_a", A0 + 29440, 32)
    st_m = at("st_m", A0 + 29472, 2, 2)
    st_s = at("st_s", A0 + 29480, 2, 2)
    st_r = at("st_r", A0 + 29488, 2, 2)
    sq_junk = at("sq_junk", A0 + 29504, P)
    q_b = at("q_b", A0, 4, LAT)
    k_b = at("k_b", A0 + 4096, 4, TOK)
    cos_b = at("cos_b", A0 + 9216, LAT)
    cq_hi = at("cq_hi", A0 + 18432, 2, LAT, dt=F32R)
    cq_lo = at("cq_lo", A0 + 20480, 2, LAT, dt=F32R)
    ckv_hi = at("ckv_hi", A0 + 22528, TOK, dt=F32R)
    ckv_lo = at("ckv_lo", A0 + 23808, TOK, dt=F32R)
    e_b = at("e_b", A0 + 25088, 2, TOK)
    tmp_b = at("tmp_b", A0 + 25088, 2, LAT)
    pt_b = at("pt_b", A0 + 27648, TOK)
    st_b = at("st_b", A0 + 29600, 2, 4)
    qs_b = at("qs_b", A0 + 29696, LAT)
    v_b = at("v_b", A0 + 30720, NKEY, 512)
    qup_raw = at("qup_raw", A0, 2, 768)
    kvup_raw = at("kvup_raw", A0 + 1536, 1024)
    qup_hi = at("qup_hi", A0 + 35840, 2, 768, dt=F32R)
    qup_lo = at("qup_lo", A0 + 37376, 2, 768, dt=F32R)
    kvup_hi = at("kvup_hi", A0 + 40448, 1024, dt=F32R)
    kvup_lo = at("kvup_lo", A0 + 41472, 1024, dt=F32R)
    sin_b = at("sin_b", A0 + 42496, LAT)
    nb_u = at("nb_u", A0 + 2560, 2, BANK)
    nb_rs = at("nb_rs", A0 + 3584, BANK)
    cat_hi = at("cat_hi", A0 + 18432, KT, LAT, dt=F32R)
    cat_lo = at("cat_lo", A0 + 26624, KT, LAT, dt=F32R)
    cat_t = at("cat_t", A0 + 36864, 2, LAT)
    h2_hi = at("h2_hi", A0 + 18432, KT, LAT, dt=F32R)
    h2_lo = at("h2_lo", A0 + 26624, KT, LAT, dt=F32R)
    n2_u = at("n2_u", A0 + 8192, KT, BANK)
    n2_rs = at("n2_rs", A0 + 12288, BANK)
    gate_s = at("gate_s", A0 + 34816, 2, LAT)
    hid = at("hid", A0 + 36864, 2, LAT)
    hid_hi = at("hid_hi", A0 + 38912, 2, LAT, dt=F32R)
    hid_lo = at("hid_lo", A0 + 40960, 2, LAT, dt=F32R)

    qkv = at("qkv", A0, 12, LAT)
    conv_in = at("conv_in", A0 + 12288, 2, PAD + LAT)
    sq_d = at("sq_d", A0 + 12288, 2, LAT)
    rs_d = at("rs_d", A0 + 14336, 2, LAT)
    dn = at("dn", A0 + 40400, DN, LAT)
    heads = lambda name, n: at(name, A0 + n, DN, P)
    st_qkv = at("st_qkv", A0 + 12288, 12, P)
    eg, dc, db, u_t, a_t = (heads(n, 13824 + 512 * j) for j, n in enumerate(("eg", "dc", "db", "u_t", "a_t")))
    kbg, ktail, vbeta, qg = (heads(n, 16384 + 512 * j) for j, n in enumerate(("kbg", "ktail", "vbeta", "qg")))
    tt, tm, ym, u_s, w_t, v_new, state, o_n, gx, s_dec = (heads(n, 34816 + 512 * j) for j, n in enumerate(
        ("tt", "tm", "ym", "u_s", "w_t", "v_new", "state", "o_n", "gx", "s_dec")))
    gb = at("gb", A0 + 39936, 8, 8)
    w_ba = at("w_ba", A0 + 40000, 8, 8)
    w_ba_hi = at("w_ba_hi", A0 + 40064, 8, 8, dt=F32R)
    w_ba_lo = at("w_ba_lo", A0 + 40128, 8, 8, dt=F32R)
    beta = at("beta", A0 + 40192, 8, 4)
    g_log = at("g_log", A0 + 40224, 8, 4)
    g_x = at("g_x", A0 + 40256, 8, 4)
    g_e = at("g_e", A0 + 40288, 8, 4)
    g_st = at("g_st", A0 + 40320, 8)
    g_c, e_gc, beta_eg, tail, o_ss = (at(n, A0 + 40328 + 8 * j, 4) for j, n in enumerate(("g_c", "e_gc", "beta_eg", "tail", "o_ss")))
    q_s = at("q_s", A0, 3, LAT)
    k_s = at("k_s", A0 + 3072, 3, LAT)
    v_s = at("v_s", A0 + 6144, 3, NQ, P)
    tmp_s = at("tmp_s", A0 + 9216, 2, LAT)
    sq_s = at("sq_s", A0 + 11264, 2, LAT)
    rs_s = at("rs_s", A0 + 13312, LAT)
    cos_s = at("cos_s", A0 + 14336, LAT)
    sin_s = at("sin_s", A0 + 15360, LAT)
    mask = at("mask", A0 + 16384, MASK_W)
    s_m = at("s_m", A0 + 9216, 2, MASK_W)
    pt_s = at("pt_s", A0 + 13056, 2, BANK)
    sw = at("sw", A0 + 34816, DN, LAT)
    z_s = at("z_s", A0 + 38912, LAT)
    on_s = at("on_s", A0 + 39936, 2, P)
    st_w = at("st_w", A0 + 40192, 2, 8)
    gates = at("gates", A0, 16, LAT)
    m_hi = at("m_hi", A0, KT, LAT, dt=F32R)
    m_lo = at("m_lo", A0 + 8192, KT, LAT, dt=F32R)
    m_t = at("m_t", A0 + 16384, 2, LAT)
    dn_hi = at("dn_hi", A0 + 18432, DN, LAT, dt=F32R)
    dn_lo = at("dn_lo", A0 + 22528, DN, LAT, dt=F32R)
    sw_hi = at("sw_hi", A0 + 26624, DN, LAT, dt=F32R)
    sw_lo = at("sw_lo", A0 + 30720, DN, LAT, dt=F32R)
    x_piece = at("x_piece", A0 + 34816, 2, LAT)
    y_f = at("y_f", A0 + 36864, 2, LAT)
    y_t = at("y_t", A0 + 38912, 2, NQ, P)

    ps = ctx.enter_context(nc.psum_tensor("ps", [P, 8 * BANK], F32))
    bank = lambda b, n=BANK: ps[:, b * BANK:b * BANK + n]

    x_scratch = nc.dram_tensor("x_scratch", [P, KT, LAT], F32, kind="Internal").ap()

    FREE = 1
    phase_end = sem("phase_end")
    w_loaded, w_split, w_done = pair("w_loaded"), pair("w_split"), pair("w_done")
    consts_in, params_in, small_in = sem("consts_in"), sem("params_in"), sem("small_in")
    params_turned, pcol_ready, silu_ready = sem("params_turned"), sem("pcol_ready"), sem("silu_ready")
    x_in, x_turned, xt_dve, xt_act = pair("x_in"), pair("x_turned"), pair("xt_dve"), pair("xt_act")
    ada_in, ada_used, ada_mm = pair("ada_in"), pair("ada_used"), sem("ada_mm")
    dve_step, act_step = sem("dve_step"), sem("act_step")
    spilled, trig_in, xt_back = sem("spilled"), sem("trig_in"), sem("xt_back")

    PHASES = ["input", "norm1", "proj_q", "proj_v", "proj_c", "attn_a", "prep_b", "heads_b0", "attn_b0", "heads_b1", "attn_b1",
              "cat", "out1", "norm2", "ffn", "norm3", "dn_proj", "dn_l2", "delta", "swa", "gates", "split2",
              "branch", "out2", "end"]
    at_end = {p: 3 * (n + 1) for n, p in enumerate(PHASES)}
    order = {}

    def meet(eng, name):
        done = order.setdefault(id(eng), [])
        done.append(name)
        assert PHASES[:len(done)] == done, done
        eng.drain().then_inc(phase_end, 1)
        eng.wait_ge(phase_end, at_end[name])

    def chain(eng, step):
        count = [0, 0, 0]

        def did(ins):
            ins.then_inc(step, 1)
            count[0] += 1

        def link(ins):
            did(ins)
            eng.wait_ge(step, count[1] + count[0])

        def enter(i, per):
            count[1], count[2] = i * per, count[0]

        def leave(per, times):
            assert count[0] - count[2] == per, (count[0] - count[2], per)
            count[0], count[1] = count[2] + per * times, 0
        return did, link, enter, leave

    dve_did, dve_link, dve_enter, dve_leave = chain(nc.vector, dve_step)
    act_did, act_link, act_enter, act_leave = chain(nc.scalar, act_step)

    norm_squared, norm_summed, norm_rooted, norm_scaled, norm_rounded, norm_finished = (
        sem(f"norm_{n}") for n in ("squared", "summed", "rooted", "scaled", "rounded", "finished"))
    norm_pieces = [0, 0]

    def norm(x, nk, pieces, u, rs, gain, shift, hi, lo, out=None):
        before, before_split = norm_pieces
        norm_pieces[0] += len(pieces)
        norm_pieces[1] += 0 if out is not None else len(pieces)

        def view(a, o, n):
            return a[:, :, o:o + n] if nk > 1 else a[:, o:o + n].rearrange("p (k n) -> p k n", k=1)

        def norm_act(act):
            for p, (o, n, which) in enumerate(pieces):
                if p:
                    act.wait_ge(norm_finished, before + p)
                nc.scalar.activation(u[:, 0:nk, 0:n], view(x, o, n), ACT.Square)\
                    .then_inc(norm_squared, 1)
                act.wait_ge(norm_summed, before + p + 1)
                act_link(nc.scalar.activation(rs[:, 0:n], bank(0, n), ACT.Ln, bias=eps_col[:, 0:1], scale=1.0 / nk))
                nc.scalar.activation(rs[:, 0:n], rs[:, 0:n], ACT.Exp, scale=-0.5).then_inc(norm_rooted, 1)
                if out is None:
                    act.wait_ge(norm_scaled, before_split + p + 1)
                    nc.scalar.activation(view(hi, o, n), u[:, 0:nk, 0:n], ACT.Copy)\
                        .then_inc(norm_rounded, 1)

        def norm_pe(pe):
            for p, (o, n, which) in enumerate(pieces):
                pe.wait_ge(norm_squared, before + p + 1)
                if p:
                    pe.wait_ge(norm_rooted, before + p)
                for k in range(nk):
                    last = nc.tensor.matmul(bank(0, n), ones_mean, u[:, k, 0:n], start=k == 0, stop=k == nk - 1)
                last.then_inc(norm_summed, 1)

        def norm_dve(dve):
            for p, (o, n, which) in enumerate(pieces):
                dve.wait_ge(norm_rooted, before + p + 1)
                rs_k = rs[:, 0:n].rearrange("p (k n) -> p k n", k=1).broadcast_to([P, nk, n])
                dve_link(nc.vector.tensor_tensor(u[:, 0:nk, 0:n], view(x, o, n), rs_k, ALU.mult))
                for k in range(nk):
                    dst = u[:, k, 0:n] if out is None else out[:, k, o:o + n]
                    if shift is None:
                        last = nc.vector.tensor_scalar(dst, u[:, k, 0:n], gain(k, which), None, ALU.mult)
                    else:
                        last = nc.vector.tensor_scalar(dst, u[:, k, 0:n], gain(k, which),
                                                       shift(k, which), ALU.mult, ALU.add)
                if out is not None:
                    last.then_inc(norm_finished, 1)
                    continue
                last.then_inc(norm_scaled, 1)
                dve.wait_ge(norm_rounded, before_split + p + 1)
                nc.vector.tensor_tensor(view(lo, o, n), u[:, 0:nk, 0:n],
                                        view(hi, o, n).bitcast(F32), ALU.subtract).then_inc(norm_finished, 1)
        return norm_act, norm_pe, norm_dve, before

    eps_col = at("eps_col", 8600, 1)
    latp = [(0, 512, 0), (512, 512, 0)]
    norm1_act, norm1_pe, norm1_dve, norm1_before = norm(xt5, KT, latp + [(1024, 256, 1)], n_u, n_rs, lambda k, w: ada_1[:, 8 + k, w:w + 1],
                 lambda k, w: ada[:, k, w:w + 1], h_hi, h_lo)
    norm_cq_act, norm_cq_pe, norm_cq_dve, norm_cq_before = norm(cq, 2, latp, nb_u, nb_rs, lambda k, w: pcol[:, ROW_AT["q_a_norm"] + k:ROW_AT["q_a_norm"] + k + 1],
                   None, cq_hi, cq_lo)
    norm_kv_act, norm_kv_pe, norm_kv_dve, norm_kv_before = norm(ckv, 1, latp + [(1024, 256, 0)], nb_u, nb_rs,
                   lambda k, w: pcol[:, ROW_AT["kv_a_norm"]:ROW_AT["kv_a_norm"] + 1], None, ckv_hi, ckv_lo)
    norm2_act, norm2_pe, norm2_dve, norm2_before = norm(xt, KT, latp, n2_u, n2_rs, lambda k, w: ada_1[:, 32 + k, 0:1],
                 lambda k, w: ada[:, 24 + k, 0:1], h2_hi, h2_lo)
    norm_f_act, norm_f_pe, norm_f_dve, norm_f_before = norm(xt, KT, latp, n2_u, n2_rs, lambda k, w: pcol[:, ROW_AT["final_norm"] + k:ROW_AT["final_norm"] + k + 1],
                  None, None, None, out=xt)
    norm3_act, norm3_pe, norm3_dve, norm3_before = norm(xt, KT, latp, n2_u, n2_rs, lambda k, w: pcol[:, ROW_AT["norm_w_2"] + k:ROW_AT["norm_w_2"] + k + 1],
                 None, h2_hi, h2_lo)

    def gemm(pe, m, s, hi, lo, pieces, first=None):
        pe.wait_ge(w_split[s], m + 1)
        for k in range(KT):
            for n_pass, (w, a) in enumerate(((w_hi, hi), (w_hi, lo), (w_lo, hi))):
                for b, o, n in pieces:
                    last = nc.tensor.matmul(bank(b, n), w[:, s, k, :], a[:, k, o:o + n],
                                            start=k == 0 and n_pass == 0, stop=k == KT - 1 and n_pass == 2)
        last.then_inc(w_done[s], 1)

    two = lambda b: [(b, 0, 512), (b + 1, 512, 512)]
    three = lambda b: two(b) + [(b + 2, 1024, 256)]


    tmp_full, rope_done, rot_done = pair("tmp_full"), pair("rope_done"), pair("rot_done")
    v_full, v_turned, v_kept = pair("v_full"), pair("v_turned"), pair("v_kept")
    c_kept = sem("c_kept")
    q_staged, scores_ready, maxed, e_ready = sem("q_staged"), sem("scores_ready"), sem("maxed"), sem("e_ready")
    mixed, turned, pt_dve, pt_act = sem("mixed"), sem("turned"), sem("pt_dve"), sem("pt_act")
    o_kept = sem("o_kept")
    qb_staged, b_scores, b_maxed, b_e, b_turned = sem("qb_staged"), sem("b_scores"), sem("b_maxed"), sem("b_e"), sem("b_turned")
    b_pt0, b_pt1, b_pt2, b_av, b_kept = sem("b_pt0"), sem("b_pt1"), sem("b_pt2"), sem("b_av"), sem("b_kept")
    up_in, up_hi, up_split = sem("up_in"), sem("up_hi"), sem("up_split")
    kr_rot, vb_mm, vb_kept = sem("kr_rot"), sem("vb_mm"), sem("vb_kept")
    qb_mm, qb_tmp, qb_rot, qb_done, kb_mm, kb_kept = (sem(n) for n in ("qb_mm", "qb_tmp", "qb_rot", "qb_done", "kb_mm", "kb_kept"))
    cat_scaled, cat_turned, cat_taken, cat_rounded = sem("cat_scaled"), pair("cat_turned"), pair("cat_taken"), pair("cat_rounded")
    added = pair("added")
    gated, up_mixed, hid_rounded, hid_split = pair("gated"), pair("up_mixed"), pair("hid_rounded"), pair("hid_split")
    down_mm, down_added = pair("down_mm"), pair("down_added")

    w_in_v = t["w_in"].rearrange("l (k p) n -> p (l k) n", p=P)
    w_out_v = t["w_out"].rearrange("l (k p) n -> p (l k) n", p=P)
    w_ada_v = t["w_ada"].rearrange("l (k p) n -> p (l k) n", p=P)
    w_f_v = t["w_ffn_in"].rearrange("l (k p) n -> p (l k) n", p=P)
    w_fo_v = t["w_ffn_out"].rearrange("l (k p) n -> p (l k) n", p=P)
    w_in2_v = t["w_in_2"].rearrange("l (k p) n -> p (l k) n", p=P)
    w_br_v = t["w_branch"].rearrange("(k p) n -> p k n", p=P)
    w_out2_v = t["w_out_2"].rearrange("l (k p) n -> p (l k) n", p=P)
    x_rows, ctx_rows = t["x"].rearrange("b n d -> (b n) d"), t["ctx"].rearrange("b n d -> (b n) d")

    lam_summed, lam_exp, o_mm, att_ready = sem("lam_summed"), sem("lam_exp"), sem("o_mm"), sem("att_ready")
    S = lambda *names: [sem(n) for n in names]
    spilled2, ba_in, ba_mm, ba_hi, ba_split, gb_exp = S("spilled2", "ba_in", "ba_mm", "ba_hi", "ba_split", "gb_exp")
    ba_kept, g_abs, g_one = S("ba_kept", "g_abs", "g_one")
    staged, g_staged, gc_mm, gx_ready, eg_ready, e_done, kk_mm, kv_turned = S(
        "staged", "g_staged", "gc_mm", "gx_ready", "eg_ready", "e_done", "kk_mm", "kv_turned")
    tt_first, t_turned, t_kept, ops_ready = S("tt_first", "t_turned", "t_kept", "ops_ready")
    od_mm, state_mm, state_new = S("od_mm", "state_mm", "state_new")
    od_rooted, on_ready, on_turned, dn_kept = S("od_rooted", "on_ready", "on_turned", "dn_kept")
    win_in, zs_in, pt_even, pt_odd = S("win_in", "zs_in", "pt_even", "pt_odd")
    split_hi = sem("split_hi")
    xp_in, y_stored = pair("xp_in"), pair("y_stored")
    A_TILES = A_HEADS * NQ
    y_mm, y_masked, z_mm, tt_new, t_new, uw_mm, uw_kept, ws_mm, v_new_ready = (
        scores_ready, maxed, e_ready, mixed, turned, pt_dve, pt_act, o_mm, o_kept)
    B_TILES = B_HEADS * NQ
    s_mm, s_masked, s_exp, so_mm, so_kept, so_scaled, so_turned, s_turned = (
        b_scores, b_maxed, b_e, b_av, b_kept, b_pt0, b_pt1, b_pt2)
    qk_in, qk_mm, qk_rooted, qk_done, vs_in, vs_turned, vs_done = (
        qb_mm, qb_rot, qb_tmp, qb_done, kb_mm, kb_kept, qb_staged)
    CAT_PAIRS = KT // 2
    y_added, conv_full, conv_done, z_kept = (
        added, cat_turned, cat_taken, cat_rounded)
    FFN_PAIRS = FT // 2
    gate_kept, merged, merged_hi, y_kept = (
        gated, up_mixed, hid_rounded, hid_split)
    DOWNS = FT // 2 * KT // 2
    y_turned = down_added
    V_PAIRS = A_HEADS // 2
    d_squared, d_summed, d_rooted = (
        v_full, v_turned, v_kept)
    ROPES = 2 * A_HEADS // 2
    d_scaled = tmp_full
    zeroed, w_rounded = sem("zeroed"), pair("w_rounded")

    block = ctx.enter_context(nc.Block())

    @block.sync
    def _(sp):
        def chunk(m, s, src, n=P):
            sp.wait_ge(w_split[s], m)
            sp.dma_start(w_raw[:, s, :, 0:n], src).then_inc(w_loaded[s], 16)

        def chunk_rows(m, s, src):
            sp.wait_ge(w_split[s], m)
            sp.dma_start(w_raw[:, s, :, :].rearrange("p k n -> p (k n)"), src).then_inc(w_loaded[s], 16)

        sp.dma_start(consts[:, :, :], t["consts"].rearrange("p (m n) -> p m n", n=P)).then_inc(consts_in, 16)
        for s in range(2):
            sp.dma_start(x_tile[:, s, :], x_rows[s * P:(s + 1) * P, :]).then_inc(x_in[s], 16)
        for name, n in ROWS:
            src = t[name]
            src = src.rearrange("(a n) -> a n", n=P) if len(src.shape) == 1 else src.rearrange("l (a n) -> (l a) n", n=P) \
                if len(src.shape) == 2 else src.rearrange("l a n -> (l a) n")
            sp.dma_start(param_rows[ROW_AT[name]:ROW_AT[name] + n, 0, :], src).then_inc(params_in, 16)
        sp.dma_start(param_rows[0:48, 1, :], t["conv_w_2"].rearrange("l j o (f n) -> (l j o f) n", n=P)).then_inc(params_in, 16)
        sp.dma_start(lam_in[:, :, :, :].rearrange("p a b n -> p (a b n)"),
                     t["diff_lambda"].rearrange("l a n -> l (a n)").broadcast_to([P, 256])).then_inc(small_in, 16)
        sp.dma_start(alog[:, :], t["dn_a_log_2"].broadcast_to([P, 4])).then_inc(small_in, 16)
        sp.dma_start(dtb[:, :], t["dn_dt_bias_2"].broadcast_to([P, 4])).then_inc(small_in, 16)
        for s in range(2):
            sp.dma_start(ada_w[:, s, :, :], w_ada_v[:, :, s * BANK:(s + 1) * BANK]).then_inc(ada_in[s], 16)
        with sp.Fori(1, 4) as i:
            for s in range(2):
                sp.wait_ge(x_turned[s], i)
                sp.dma_start(x_tile[:, s, :], x_rows[ds(i * 256 + s * P, P), :]).then_inc(x_in[s], 16)
        for s in range(2):
            sp.wait_ge(x_turned[s], 4)
            sp.dma_start(x_tile[:, s, :], ctx_rows[s * P:(s + 1) * P, :]).then_inc(x_in[s], 16)
        with sp.Fori(1, 6) as i:
            for s in range(2):
                sp.wait_ge(ada_used[s], i)
                sp.dma_start(ada_w[:, s, :, :], w_ada_v[:, :, ds(i * 1024 + s * BANK, BANK)]).then_inc(ada_in[s], 16)
        sp.wait_ge(phase_end, at_end["input"])
        sp.dma_start(x_scratch, xt5[:, :, 0:LAT]).then_inc(spilled, 16)
        for m, c in ((M_Q, 0), (M_K, 512)):
            for j in range(2):
                for s in range(2):
                    chunk(m + j, s, w_in_v[:, :, c + (2 * j + s) * P:c + (2 * j + s + 1) * P])
            if m == M_Q:
                sp.wait_ge(phase_end, at_end["norm1"])
                sp.wait_ge(spilled, 16)
                sp.dma_start(cos_a[:, :], t["trig_a"][:, 0, :]).then_inc(trig_in, 16)
                sp.dma_start(sin_a[:, :], t["trig_a"][:, 1, :]).then_inc(trig_in, 16)
        with sp.Fori(0, 2) as i:
            for s in range(2):
                chunk(M_V + i, s, w_in_v[:, :, ds(i * 256 + 1024 + s * P, P)])
        for s in range(2):
            chunk(M_C, s, w_in_v[:, :, 1536 + s * P:1536 + (s + 1) * P])
        chunk(M_C + 1, 0, w_in_v[:, :, 1792:1920])
        chunk(M_C + 1, 1, w_in_v[:, :, 1856:1952], BD)
        for s in range(2):
            chunk(M_OUT, s, w_out_v[:, :, s * P:(s + 1) * P])
        sp.wait_ge(phase_end, at_end["attn_a"])
        sp.dma_start(qup_raw[:, :, :], t["w_q_up"].rearrange("l (k p) n -> p (l k) n", p=P)).then_inc(up_in, 16)
        sp.dma_start(kvup_raw[:, :], t["w_kv_up"].rearrange("l p n -> p (l n)")).then_inc(up_in, 16)
        sp.dma_start(cos_b[:, :], t["trig_b"][:, 0, :]).then_inc(up_in, 16)
        sp.dma_start(sin_b[:, :], t["trig_b"][:, 1, :]).then_inc(up_in, 16)
        sp.wait_ge(phase_end, at_end["attn_b1"])
        sp.dma_start(xt[:, :, :], x_scratch).then_inc(xt_back, 16)
        with sp.Fori(1, 4) as i:
            for s in range(2):
                chunk(M_OUT + i, s, w_out_v[:, :, ds(i * 256 + s * P, P)])
        for s in range(2):
            chunk(M_FFN, s, w_f_v[:, :, s * P:(s + 1) * P])
        for s in range(2):
            chunk(M_FFN + 1, s, w_f_v[:, :, FFN + s * P:FFN + (s + 1) * P])
        with sp.Fori(1, FT // 2) as i:
            for s in range(2):
                chunk(M_FFN - 1 + i * 3, s, w_f_v[:, :, ds(i * 256 + s * P, P)])
            for s in range(2):
                chunk_rows(M_FFN + i * 3, s, w_fo_v[:, ds(i * 2 - 2 + s, 1), :].rearrange("p k n -> p (k n)"))
            for s in range(2):
                chunk(M_FFN + 1 + i * 3, s, w_f_v[:, :, ds(i * 256 + FFN + s * P, P)])
        for s in range(2):
            chunk_rows(M_FFN + 2 + 3 * (FT // 2 - 1), s, w_fo_v[:, FT - 2 + s, :])
        sp.wait_ge(phase_end, at_end["norm3"])
        sp.dma_start(x_scratch, xt[:, :, :]).then_inc(spilled2, 16)
        sp.dma_start(w_ba[:, :, :], w_in2_v[:, :, C_B:C_B + 8]).then_inc(ba_in, 16)
        with sp.Fori(0, 8) as i:
            for s in range(2):
                chunk(i + M_DN, s, w_in2_v[:, :, ds(i * 256 + s * P, P)])
        for s in range(2):
            chunk(M_SWA, s, w_in2_v[:, :, C_SQ + s * 512:C_SQ + s * 512 + P])
        sp.wait_ge(phase_end, at_end["delta"])
        sp.dma_start(cos_s[:, :], t["trig_s"][:, 0, :]).then_inc(win_in, 16)
        sp.dma_start(sin_s[:, :], t["trig_s"][:, 1, :]).then_inc(win_in, 16)
        sp.dma_start(mask[:, :], t["window_mask"]).then_inc(win_in, 16)
        for c in range(2, 10):
            chunk(M_SWA + c // 2, c % 2, w_in2_v[:, :, SWA_COLS[c]:SWA_COLS[c] + P])
        with sp.Fori(1, DN) as h:
            for c in range(10):
                chunk(h * 5 + M_SWA + c // 2, c % 2, w_in2_v[:, :, ds(h * P + SWA_COLS[c], P)])
        with sp.Fori(0, 8) as i:
            for s in range(2):
                chunk(i + M_GATE, s, w_in2_v[:, :, ds(i * 256 + C_G + s * P, P)])
        with sp.Fori(0, 4) as i:
            for s in range(2):
                chunk(i + M_BRANCH, s, w_br_v[:, :, ds(i * 256 + s * P, P)])
        sp.wait_ge(phase_end, at_end["branch"])
        sp.wait_ge(spilled2, 16)
        with sp.Fori(0, 4) as i:
            for s in range(2):
                chunk(i + M_OUT2, s, w_out2_v[:, :, ds(i * 256 + s * P, P)])
                sp.wait_ge(y_added[s], i + CAT_PAIRS + FREE)
                sp.dma_start(x_piece[:, s, :], x_scratch[:, ds(i * 2 + s, 1), :].rearrange("p k n -> p (k n)")).then_inc(xp_in[s], 16)

    @block.gpsimd
    def _(pool):
        for freed in (*rope_done, *v_kept, kv_turned, ops_ready, dn_kept, state_new, *y_stored, o_mm, b_kept, e_ready,
                      o_kept, b_e, *added):
            pool.sem_inc(freed, FREE)
        nc.gpsimd.memset(zero[:, :], 0.0).then_inc(zeroed, 1)
        pool.wait_ge(zeroed, 1)

        def split(m):
            for s in range(2):
                flat = lambda w: w[:, s, :, :].rearrange("p k n -> p (k n)")
                pool.wait_ge(w_loaded[s], m * 16 + 16)
                pool.wait_ge(w_done[s], m)
                nc.gpsimd.tensor_tensor(flat(w_hi), flat(w_raw), zero[:, 0:1].broadcast_to([P, KT * P]), ALU.add)\
                    .then_inc(w_rounded[s], 1)
                pool.wait_ge(w_rounded[s], m + 1)
                nc.gpsimd.tensor_tensor(flat(w_lo), flat(w_raw), flat(w_hi).bitcast(F32), ALU.subtract)\
                    .then_inc(w_split[s], 1)

        split(0)
        with pool.Fori(1, PAIRS) as m:
            split(m)

    @block.scalar
    def _(act):
        act.wait_ge(lam_summed, 1)
        nc.scalar.activation(lam_e[:, :], lam_e[:, :], ACT.Exp).then_inc(lam_exp, 1)
        act.wait_ge(params_turned, 2)
        nc.scalar.activation(pcol[:, 0:N_ROWS], bank(6, N_ROWS), ACT.Copy)
        nc.scalar.activation(pcol[:, CONV_AT:CONV_AT + 48], bank(7, 48), ACT.Copy).then_inc(pcol_ready, 1)
        act.wait_ge(pcol_ready, 1)
        nc.scalar.activation(silu_c[:, :, :].rearrange("p k w -> p w k"),
                             pcol[:, 48:64].rearrange("p (w k) -> p w k", w=2), ACT.Silu).then_inc(silu_ready, 1)
        with act.Fori(0, 5) as i:
            for s in range(2):
                act.wait_ge(x_turned[s], i + 1)
                nc.scalar.activation(xt5[:, 0:4, ds(i * 256 + s * P, P)],
                                     bank(2 * s).rearrange("p (k n) -> p k n", k=4), ACT.Copy).then_inc(xt_act[s], 1)
        meet(act, "input")
        norm1_act(act)
        meet(act, "norm1")
        act.wait_ge(spilled, 16)
        for m, keys, n0 in ((M_Q, False, 0), (M_K, True, 2)):
            with act.Fori(0, 2) as i:
                for s in range(2):
                    act.wait_ge(w_done[s], i + m + 1)
                    act.wait_ge(rope_done[s], i + n0 + FREE)
                    if keys:
                        nc.scalar.activation(k_a[:, ds(i * 2 + s, 1), LAT:TOK], bank(3 * s + 2, CTX).rearrange("p (k n) -> p k n", k=1), ACT.Copy)
                    nc.scalar.activation(rope_tmp[:, s, :], bank(3 * s, LAT), ACT.Copy).then_inc(tmp_full[s], 1)
        meet(act, "proj_q")
        with act.Fori(0, 2) as i:
            for s in range(2):
                act.wait_ge(w_done[s], i + M_V + 1)
                nc.scalar.activation(v_tmp[:, s, :], bank(3 * s, TOK), ACT.Copy).then_inc(v_full[s], 1)
        meet(act, "proj_v")
        for s in range(2):
            act.wait_ge(w_done[s], M_C + 1)
            nc.scalar.activation(cq[:, s, :], bank(3 * s, LAT), ACT.Copy).then_inc(c_kept, 1)
        for s, dst in enumerate((ckv[:, :], kr[0:BD, :])):
            act.wait_ge(w_done[s], M_C + 2)
            nc.scalar.activation(dst, ps[0:BD if s else P, 3 * s * BANK:3 * s * BANK + TOK], ACT.Copy)
        meet(act, "proj_c")
        def square_output(h, qt):
            act.wait_ge(o_kept, h * NQ + qt + 1 + FREE)
            nc.scalar.activation(sq_junk[:, :], att[:, qt, ds(h * P, P)], ACT.Square, accum_out=st_a[:, ds(h * NQ + qt, 1)])

        with act.Fori(0, A_HEADS) as h:
            for qt in range(NQ):
                act.wait_ge(maxed, h * NQ + qt + 1)
                for w in range(2):
                    last = nc.scalar.activation(e_a[:, qt % 2, w, :], ps[:, w * TOK:(w + 1) * TOK], ACT.Exp,
                                                bias=st_m[:, qt % 2, w:w + 1], scale=SCALE_A,
                                                accum_out=st_s[:, qt % 2, w:w + 1])
                last.then_inc(e_ready, 1)
                if qt:
                    square_output(h, qt - 1)
                act.wait_ge(turned, h * NQ + qt + 1)
                nc.scalar.activation(pt[:, 512:1024], bank(6), ACT.Copy).then_inc(pt_act, 1)
            square_output(h, NQ - 1)
        meet(act, "attn_a")
        act.wait_ge(up_in, 64)
        norm_cq_act(act)
        act.wait_ge(norm_finished, norm_cq_before + 2)
        norm_kv_act(act)
        act.wait_ge(norm_finished, norm_kv_before + 3)
        nc.scalar.activation(qup_hi[:, :, :], qup_raw[:, :, :], ACT.Copy)
        nc.scalar.activation(kvup_hi[:, :], kvup_raw[:, :], ACT.Copy).then_inc(up_hi, 1)
        meet(act, "prep_b")
        for g in range(2):
            for h in range(4):
                n = g * 4 + h
                act.wait_ge(qb_mm, n + 1)
                if n:
                    act.wait_ge(qb_done, n)
                nc.scalar.activation(tmp_b[0:BD, h % 2, :], ps[0:BD, 0:LAT], ACT.Copy).then_inc(qb_tmp, 1)
                act.wait_ge(kb_mm, n + 1)
                nc.scalar.activation(k_b[0:NOPE, h, :], ps[0:NOPE, 4 * BANK:4 * BANK + TOK], ACT.Copy).then_inc(kb_kept, 1)
            meet(act, f"heads_b{g}")
            with act.Fori(0, 4) as h:
                act.wait_ge(b_kept, h * NQ + g * 32 + FREE)
                nc.scalar.activation(qs_b[0:BD, :], q_b[0:BD, ds(h, 1), :].rearrange("p k n -> p (k n)"), ACT.Copy)\
                    .then_inc(qb_staged, 1)
                for qt in range(NQ):
                    n = h * NQ + g * 32 + qt
                    act.wait_ge(b_maxed, n + 1)
                    b = 3 * (qt % 2)
                    nc.scalar.activation(e_b[:, qt % 2, :], bank(b, TOK), ACT.Exp, bias=st_b[:, qt % 2, 0:1],
                                         scale=SCALE_B, accum_out=st_b[:, qt % 2, 1:2]).then_inc(b_e, 1)
                    act.wait_ge(b_turned, n * 3 + 2)
                    nc.scalar.activation(pt_b[:, 512:1024], bank(7), ACT.Copy).then_inc(b_pt1, 1)
            meet(act, f"attn_b{g}")
        act_link(nc.scalar.activation(st_a[:, :], st_a[:, :], ACT.Ln, bias=eps_col[:, 0:1], scale=1.0 / P))
        nc.scalar.activation(st_a[:, :], st_a[:, :], ACT.Exp, scale=-0.5).then_inc(cat_scaled, 1)
        for f in range(KT):
            s = f % 2
            act.wait_ge(cat_taken[s], f // 2 + 1)
            nc.scalar.activation(cat_hi[:, f, :], cat_t[:, s, :], ACT.Copy).then_inc(cat_rounded[s], 1)
        meet(act, "cat")
        meet(act, "out1")
        norm2_act(act)
        meet(act, "norm2")
        def gate_and_round(i, gates, downs):
            for s in range(2):
                act.wait_ge(w_done[s], gates)
                act.wait_ge(up_mixed[s], i)
                nc.scalar.activation(gate_s[:, s, :], bank(2 * s, LAT), ACT.Silu).then_inc(gated[s], 1)
            for s in range(2):
                act.wait_ge(w_done[1], downs)
                act.wait_ge(up_mixed[s], i + 1)
                nc.scalar.activation(hid_hi[:, s, :], hid[:, s, :], ACT.Copy).then_inc(hid_rounded[s], 1)

        gate_and_round(0, M_FFN + 1, M_FFN + 1)
        with act.Fori(1, FT // 2) as i:
            gate_and_round(i, i * 3 + M_FFN, i * 3 + M_FFN + 1)
        meet(act, "ffn")
        norm_f_act(act)
        act.wait_ge(norm_finished, norm_f_before + 2)
        norm3_act(act)
        meet(act, "norm3")
        act.wait_ge(spilled2, 16)
        with act.Fori(0, 6) as i:
            for s in range(2):
                act.wait_ge(w_done[s], i + M_DN + 1)
                act.wait_ge(conv_done[s], i + CAT_PAIRS)
                nc.scalar.activation(conv_in[:, s, PAD:PAD + LAT], bank(2 * s, LAT), ACT.Copy).then_inc(conv_full[s], 1)
            for s in range(2):
                act.wait_ge(conv_done[s], i + 1 + CAT_PAIRS)
                y = qkv[:, ds(i * 2 + s, 1), :].rearrange("p k n -> p (k n)")
                nc.scalar.activation(y, y, ACT.Silu)
        with act.Fori(0, 2) as i:
            for s in range(2):
                act.wait_ge(w_done[s], i + M_DN + 7)
                nc.scalar.activation(dn[:, ds(i * 2 + s, 1), :].rearrange("p k n -> p (k n)"), bank(2 * s, LAT), ACT.Silu)\
                    .then_inc(z_kept[s], 1)
        act.wait_ge(ba_in, 16)
        nc.scalar.activation(w_ba_hi[:, :, :], w_ba[:, :, :], ACT.Copy).then_inc(ba_hi, 1)
        meet(act, "dn_proj")
        with act.Fori(0, 4) as i:
            act_enter(i, 2)
            for s in range(2):
                act.wait_ge(d_scaled[s], i + ROPES)
                nc.scalar.activation(sq_d[:, s, :], qkv[:, ds(i * 2 + s, 1), :].rearrange("p k n -> p (k n)"), ACT.Square)\
                    .then_inc(d_squared[s], 1)
            for s in range(2):
                act.wait_ge(d_summed[s], i + 1 + V_PAIRS)
                act_link(nc.scalar.activation(rs_d[:, s, :], bank(2 * s, LAT), ACT.Ln, bias=eps_col[:, 0:1], scale=float(P)))
                nc.scalar.activation(rs_d[:, s, :], rs_d[:, s, :], ACT.Exp, scale=-0.5).then_inc(d_rooted[s], 1)
            act_leave(2, 4)
        act.wait_ge(ba_kept, 1)
        nc.scalar.activation(beta[:, :, :], gb[:, :, 0:4], ACT.Exp, scale=-1.0)
        nc.scalar.activation(ealog[:, :], alog[:, :], ACT.Exp)
        act.wait_ge(g_abs, 1)
        nc.scalar.activation(g_e[:, :, :], g_e[:, :, :], ACT.Exp, scale=-1.0).then_inc(gb_exp, 1)
        act.wait_ge(g_one, 1)
        nc.scalar.activation(g_e[:, :, :], g_e[:, :, :], ACT.Ln).then_inc(gb_exp, 1)
        meet(act, "dn_l2")
        flat = lambda a: a[:, :, :].rearrange("p h n -> p (h n)")
        with act.Fori(0, NQ) as c:
            act_enter(c, 2)
            act.wait_ge(kv_turned, c + FREE)
            act.wait_ge(ops_ready, c + FREE)
            nc.scalar.activation(st_qkv[:, :, :], qkv[:, :, ds(c * P, P)], ACT.Copy).then_inc(staged, 1)
            act.wait_ge(gx_ready, c + 1)
            nc.scalar.activation(flat(eg), bank(0), ACT.Exp)
            nc.scalar.activation(e_gc[:, :], g_c[:, :], ACT.Exp)
            nc.scalar.activation(tail[:, :], tail[:, :], ACT.Exp).then_inc(eg_ready, 1)
            nc.scalar.activation(flat(dc), flat(gx), ACT.Exp).then_inc(e_done, 1)
            act.wait_ge(t_turned, c + 1)
            nc.scalar.activation(flat(tm), bank(7), ACT.Copy).then_inc(t_kept, 1)
            act.wait_ge(uw_mm, c + 1 + A_TILES)
            nc.scalar.activation(flat(u_s), bank(3), ACT.Copy)
            nc.scalar.activation(flat(w_t), bank(4), ACT.Copy).then_inc(uw_kept, 1)
            act.wait_ge(od_mm, c + 1)
            for h in range(DN):
                last = nc.scalar.activation(u_s[:, h, :], bank(6)[:, h * P:(h + 1) * P], ACT.Square, accum_out=o_ss[:, h:h + 1])
            act_link(last)
            act_link(nc.scalar.activation(o_ss[:, :], o_ss[:, :], ACT.Ln, bias=eps_col[:, 0:1], scale=1.0 / P))
            nc.scalar.activation(o_ss[:, :], o_ss[:, :], ACT.Exp, scale=-0.5).then_inc(od_rooted, 1)
            act_leave(2, NQ)
        meet(act, "delta")
        with act.Fori(0, DN) as h:
            act_enter(h, 6)

            def root(j):
                act.wait_ge(qk_mm, h * 6 + j + 1 + B_HEADS)
                act.wait_ge(qk_done, h * 6 + j + B_HEADS)
                act_link(nc.scalar.activation(rs_s[:, :], bank(4, LAT), ACT.Ln, bias=eps_col[:, 0:1]))
                nc.scalar.activation(rs_s[:, :], rs_s[:, :], ACT.Exp, scale=-0.5).then_inc(qk_rooted, 1)

            act.wait_ge(so_kept, h * NQ + B_TILES + FREE)
            for c in range(10):
                s = c % 2
                act.wait_ge(w_done[s], h * 5 + M_SWA + c // 2 + 1)
                if c < 6:
                    if c >= 2:
                        act.wait_ge(qk_done, h * 6 + c - 1 + B_HEADS)
                    norm_w = ROW_AT["q_norm_w_2"] + c
                    nc.scalar.activation(tmp_s[:, s, :], bank(2 * s, LAT), ACT.Copy, scale=pcol[:, norm_w:norm_w + 1])
                    nc.scalar.activation(sq_s[:, s, :], bank(2 * s, LAT), ACT.Square).then_inc(qk_in, 1)
                elif c < 9:
                    if c < 8:
                        act.wait_ge(qk_done, h * 6 + c - 1 + B_HEADS)
                    else:
                        act.wait_ge(vs_turned, h * 3 + 1 + B_HEADS)
                    nc.scalar.activation(tmp_s[:, s, :], bank(2 * s, LAT), ACT.Copy).then_inc(vs_in, 1)
                else:
                    nc.scalar.activation(z_s[:, :], bank(2 * s, LAT), ACT.Silu).then_inc(zs_in, 1)
                if 1 <= c <= 6:
                    root(c - 1)
            act.wait_ge(vs_done, h * 3 + 3 + B_HEADS)
            for n in range(NQ):
                s = n % 2
                width = len(window_tiles(n)) * P
                act.wait_ge(s_masked, h * NQ + n + 1 + B_TILES)
                nc.scalar.activation(s_m[:, s, 0:width], s_m[:, s, 0:width], ACT.Exp, bias=st_w[:, s, 4:5],
                                     accum_out=st_w[:, s, 5:6]).then_inc(s_exp, 1)
                for b in range(1, BATCHES[n], 2):
                    act.wait_ge(s_turned, h * ALL_BATCHES + sum(BATCHES[:n]) + b + 1 + B_TILES)
                    w = min(BANK, width - b * BANK)
                    nc.scalar.activation(pt_s[:, 1, 0:w], bank(5, w), ACT.Copy).then_inc(pt_odd, 1)
            act_leave(6, DN)
        meet(act, "swa")
        with act.Fori(0, 8) as i:
            for s in range(2):
                act.wait_ge(w_done[s], i + M_GATE + 1)
                nc.scalar.activation(gates[:, ds(i * 2 + s, 1), :].rearrange("p k n -> p (k n)"), bank(2 * s, LAT), ACT.Sigmoid)\
                    .then_inc(gate_kept[s], 1)
        meet(act, "gates")
        nc.scalar.activation(dn_hi[:, :, :], dn[:, :, :], ACT.Copy).then_inc(split_hi, 1)
        nc.scalar.activation(sw_hi[:, :, :], sw[:, :, :], ACT.Copy).then_inc(split_hi, 1)
        meet(act, "split2")
        with act.Fori(0, 4) as i:
            for s in range(2):
                act.wait_ge(merged[s], i + 1 + FFN_PAIRS)
                nc.scalar.activation(m_hi[:, ds(i * 2 + s, 1), :].rearrange("p k n -> p (k n)"), m_t[:, s, :], ACT.Copy)\
                    .then_inc(merged_hi[s], 1)
        meet(act, "branch")
        out_v = t["out"].rearrange("b (q p) n -> p (b q) n", p=P)
        with act.Fori(0, 4) as i:
            for s in range(2):
                act.wait_ge(y_turned[s], i + 1 + DOWNS)
                act.wait_ge(y_stored[s], i * 16 + FREE)
                nc.scalar.activation(y_t[:, s, :, :].rearrange("p q n -> p (q n)"), bank(4 + 2 * s, LAT), ACT.Copy)\
                    .then_inc(y_kept[s], 1)
                act.wait_ge(y_kept[s], i + 1 + FFN_PAIRS)
                act.dma_start(out_v[:, :, ds(i * 256 + s * P, P)], y_t[:, s, :, :]).then_inc(y_stored[s], 16)
        for s in range(2):
            act.wait_ge(y_stored[s], 64 + FREE)

    @block.vector
    def _(dve):
        nc.vector.memset(eps_col[:, :], EPS)
        dve.wait_ge(small_in, 48)
        dve_link(nc.vector.tensor_tensor(lam_prod[:, :, :], lam_in[:, :, 0, :], lam_in[:, :, 1, :], ALU.mult))
        nc.vector.tensor_reduce(lam_e[:, :], lam_prod[:, :, :], AX_X, ALU.add).then_inc(lam_summed, 1)
        with dve.Fori(0, 5) as i:
            for s in range(2):
                dve.wait_ge(x_turned[s], i + 1)
                nc.vector.tensor_copy(xt5[:, 4:8, ds(i * 256 + s * P, P)],
                                      bank(2 * s + 1).rearrange("p (k n) -> p k n", k=4)).then_inc(xt_dve[s], 1)
        dve.wait_ge(ada_mm, 1)
        dve.wait_ge(pcol_ready, 1)
        dve_link(nc.vector.tensor_tensor(ada[:, :, :], bank(6, 96).rearrange("p (m w) -> p m w", w=2),
                                           pcol[:, 0:48].rearrange("p (m w) -> p m w", w=1).broadcast_to([P, 48, 2]), ALU.add))
        nc.vector.tensor_scalar(ada_1[:, :, :], ada[:, :, :], 1.0, None, ALU.add)
        nc.vector.tensor_scalar(subln[:, :], pcol[:, ROW_AT["diff_subln"]:ROW_AT["diff_subln"] + 1], 1.0 - LAM_INIT, None, ALU.mult)
        meet(dve, "input")
        norm1_dve(dve)
        meet(dve, "norm1")
        dve.wait_ge(trig_in, 32)
        for m, dst, n0 in ((M_Q, q_a, 0), (M_K, k_a, 2)):
            with dve.Fori(0, 2) as i:
                dve_enter(i, 4)
                for s in range(2):
                    out = dst[:, ds(i * 2 + s, 1), 0:LAT].rearrange("p k n -> p (k n)")
                    dve.wait_ge(tmp_full[s], i + n0 + 1)
                    dve_link(nc.vector.tensor_tensor(out, rope_tmp[:, s, :], cos_a[:, :], ALU.mult))
                    dve.wait_ge(rot_done[s], i + n0 + 1)
                    dve_link(nc.vector.tensor_tensor(rope_tmp[:, s, :], bank(3 * s, LAT), sin_a[:, :], ALU.mult))
                    nc.vector.tensor_tensor(out, out, rope_tmp[:, s, :], ALU.add).then_inc(rope_done[s], 1)
                dve_leave(4, 2)
        meet(dve, "proj_q")
        with dve.Fori(0, 2) as i:
            for s in range(2):
                dve.wait_ge(v_turned[s], i + 1)
                nc.vector.tensor_copy(v_a[:, :, ds(i * 256 + s * P, P)],
                                      bank(3 * s, TOK).rearrange("p (t n) -> p t n", n=P)).then_inc(v_kept[s], 1)
        meet(dve, "proj_v")
        dve.wait_ge(lam_exp, 1)
        nc.vector.scalar_tensor_tensor(lam[:, :], lam_e[:, 0:1], LAM_INIT, lam_e[:, 1:2], ALU.add, ALU.subtract)
        meet(dve, "proj_c")
        nc.vector.memset(qs[64:128, 0, :], 0.0)
        nc.vector.memset(qs[0:64, 1, :], 0.0)
        with dve.Fori(0, A_HEADS) as h:
            dve_enter(h, 3 * NQ)
            dve.wait_ge(o_mm, h * NQ + FREE)
            for w in range(2):
                a, b = 64 * w, 64 * w + 64
                last = nc.vector.tensor_copy(qs[a:b, w, :], q_a[a:b, ds(h, 1), :].rearrange("p k n -> p (k n)"))
            last.then_inc(q_staged, 1)

            def take_output(qt):
                dve.wait_ge(o_mm, h * NQ + qt + 1 + FREE)
                nc.vector.tensor_copy(att[:, qt, ds(h * P, P)], ps[:, 7 * BANK + 256:7 * BANK + 384]).then_inc(o_kept, 1)

            for qt in range(NQ):
                s, n = qt % 2, h * NQ + qt
                dve.wait_ge(scores_ready, n + 1)
                dve_link(nc.vector.tensor_reduce(st_r[:, s, :], ps[:, 0:2 * TOK].rearrange("p (w n) -> p w n", w=2), AX_X, ALU.max))
                nc.vector.tensor_scalar(st_m[:, s, :], st_r[:, s, :], -SCALE_A, None, ALU.mult).then_inc(maxed, 1)
                if qt:
                    take_output(qt - 1)
                dve.wait_ge(e_ready, n + 1 + FREE)
                dve_link(nc.vector.reciprocal(st_r[:, s, :], st_s[:, s, :]))
                dve_link(nc.vector.tensor_scalar(prob[:, s, :], e_a[:, s, 1, :], st_r[:, s, 1:2], lam[:, 0:1], ALU.mult, ALU.mult))
                nc.vector.scalar_tensor_tensor(prob[:, s, :], e_a[:, s, 0, :], st_r[:, s, 0:1], prob[:, s, :],
                                               ALU.mult, ALU.subtract).then_inc(mixed, 1)
                dve.wait_ge(turned, n + 1)
                nc.vector.tensor_copy(pt[:, 0:512], bank(5))
                nc.vector.tensor_copy(pt[:, 1024:1280], bank(7, 256)).then_inc(pt_dve, 1)
            take_output(NQ - 1)
            dve_leave(3 * NQ, A_HEADS)
        meet(dve, "attn_a")
        dve.wait_ge(up_in, 64)
        norm_cq_dve(dve)
        norm_kv_dve(dve)
        dve.wait_ge(up_hi, 1)
        nc.vector.tensor_tensor(qup_lo[:, :, :], qup_raw[:, :, :], qup_hi[:, :, :].bitcast(F32), ALU.subtract)
        nc.vector.tensor_tensor(kvup_lo[:, :], kvup_raw[:, :], kvup_hi[:, :].bitcast(F32), ALU.subtract).then_inc(up_split, 1)
        dve.wait_ge(kr_rot, 1)
        r = slice(NOPE, BD)
        dve_did(nc.vector.tensor_tensor(tmp_b[r, 0, :], ps[r, 4 * BANK:6 * BANK], sin_b[r, :], ALU.mult))
        dve_link(nc.vector.tensor_tensor(kr[r, 0:LAT], kr[r, 0:LAT], cos_b[r, :], ALU.mult))
        dve_link(nc.vector.tensor_tensor(kr[r, 0:LAT], kr[r, 0:LAT], tmp_b[r, 0, :], ALU.add))
        for kt in range(NKEY):
            dve.wait_ge(vb_mm, kt + 1)
            nc.vector.tensor_copy(v_b[:, kt, :], bank(kt % 2)).then_inc(vb_kept, 1)
        meet(dve, "prep_b")
        for g in range(2):
            for h in range(4):
                n = g * 4 + h
                nc.vector.tensor_copy(k_b[r, h, :], kr[r, :])
                dve.wait_ge(qb_tmp, n + 1)
                dve_link(nc.vector.tensor_tensor(q_b[0:BD, h, :], tmp_b[0:BD, h % 2, :], cos_b[0:BD, :], ALU.mult))
                dve.wait_ge(qb_rot, n + 1)
                dve_link(nc.vector.tensor_tensor(tmp_b[0:BD, h % 2, :], ps[0:BD, 2 * BANK:4 * BANK], sin_b[0:BD, :], ALU.mult))
                nc.vector.tensor_tensor(q_b[0:BD, h, :], q_b[0:BD, h, :], tmp_b[0:BD, h % 2, :], ALU.add).then_inc(qb_done, 1)
            meet(dve, f"heads_b{g}")
            with dve.Fori(0, 4) as h:
                dve_enter(h, 2 * NQ)

                def take_output(qt):
                    s = qt % 2
                    dve_link(nc.vector.reciprocal(st_b[:, s, 3:4], st_b[:, s, 1:2]))
                    dve.wait_ge(b_av, h * NQ + g * 32 + qt + 1)
                    nc.vector.tensor_scalar(att[:, qt, ds(h * 64 + 512 + g * 256, 64)], bank(7, 64), st_b[:, s, 3:4], None, ALU.mult)\
                        .then_inc(b_kept, 1)

                for qt in range(NQ):
                    s, n = qt % 2, h * NQ + g * 32 + qt
                    dve.wait_ge(b_scores, n + 1)
                    dve_link(nc.vector.tensor_reduce(st_b[:, s, 2:3], bank(3 * s, TOK), AX_X, ALU.max))
                    nc.vector.tensor_scalar(st_b[:, s, 0:1], st_b[:, s, 2:3], -SCALE_B, None, ALU.mult).then_inc(b_maxed, 1)
                    if qt:
                        take_output(qt - 1)
                    dve.wait_ge(b_turned, n * 3 + 1)
                    nc.vector.tensor_copy(pt_b[:, 0:512], bank(6)).then_inc(b_pt0, 1)
                    dve.wait_ge(b_turned, n * 3 + 3)
                    nc.vector.tensor_copy(pt_b[:, 1024:1280], bank(6, 256)).then_inc(b_pt2, 1)
                take_output(NQ - 1)
                dve_leave(2 * NQ, 4)
            meet(dve, f"attn_b{g}")
        dve.wait_ge(cat_scaled, 1)
        for qt in range(NQ):
            a = att[:, qt, 0:512].rearrange("p (h n) -> p h n", h=A_HEADS)
            last = nc.vector.tensor_tensor(a, a, st_a[:, :].rearrange("p (h q w) -> p h q w", q=NQ, w=1)[:, :, qt, :]
                                           .broadcast_to([P, A_HEADS, P]), ALU.mult)
        last.then_inc(att_ready, 1)
        for f in range(KT):
            s = f % 2
            dve.wait_ge(cat_turned[s], f // 2 + 1)
            if f < 4:
                nc.vector.tensor_scalar(cat_t[:, s, :], bank(2 * s, LAT), subln[:, 0:1], None, ALU.mult).then_inc(cat_taken[s], 1)
            else:
                nc.vector.tensor_copy(cat_t[:, s, :], bank(2 * s, LAT)).then_inc(cat_taken[s], 1)
            dve.wait_ge(cat_rounded[s], f // 2 + 1)
            nc.vector.tensor_tensor(cat_lo[:, f, :], cat_t[:, s, :], cat_hi[:, f, :].bitcast(F32), ALU.subtract)
        meet(dve, "cat")
        dve.wait_ge(xt_back, 16)
        with dve.Fori(0, 4) as i:
            for s in range(2):
                dve.wait_ge(w_done[s], i + M_OUT + 1)
                x = xt[:, ds(i * 2 + s, 1), :].rearrange("p k n -> p (k n)")
                nc.vector.scalar_tensor_tensor(x, bank(2 * s, LAT), ada[:, ds(i * 2 + s + 16, 1), 0], x, ALU.mult, ALU.add)\
                    .then_inc(added[s], 1)
        meet(dve, "out1")
        norm2_dve(dve)
        meet(dve, "norm2")

        def add_down(i, m):
            for f in range(KT):
                s = f % 2
                if f == KT - 1:
                    dve.wait_ge(w_done[1], m + 1)
                else:
                    dve.wait_ge(down_mm[s], i * (4 - s) + f // 2 + 1)
                nc.vector.scalar_tensor_tensor(xt[:, f, :], bank(4 + 2 * s, LAT), ada[:, 40 + f, 0:1], xt[:, f, :],
                                               ALU.mult, ALU.add).then_inc(down_added[s], 1)

        def mix_up(i):
            for s in range(2):
                dve.wait_ge(gated[s], i + 1)
                dve.wait_ge(w_done[s], i * 3 + M_FFN + 2)
                nc.vector.tensor_tensor(hid[:, s, :], bank(4 + 2 * s, LAT), gate_s[:, s, :], ALU.mult).then_inc(up_mixed[s], 1)
            for s in range(2):
                dve.wait_ge(hid_rounded[s], i + 1)
                nc.vector.tensor_tensor(hid_lo[:, s, :], hid[:, s, :], hid_hi[:, s, :].bitcast(F32), ALU.subtract)\
                    .then_inc(hid_split[s], 1)

        mix_up(0)
        with dve.Fori(1, FT // 2) as i:
            add_down(i - 1, i * 3 + M_FFN)
            mix_up(i)
        add_down(FT // 2 - 1, M_FFN + 32)
        meet(dve, "ffn")
        norm_f_dve(dve)
        dve.wait_ge(norm_finished, norm_f_before + 2)
        norm3_dve(dve)
        meet(dve, "norm3")
        dve.wait_ge(spilled2, 16)
        for s in range(2):
            last = nc.vector.memset(conv_in[:, s, 0:PAD], 0.0)
        dve_link(last)
        with dve.Fori(0, 6) as i:
            dve_enter(i, 6)
            for s in range(2):
                y = qkv[:, ds(i * 2 + s, 1), :].rearrange("p k n -> p (k n)")
                dve.wait_ge(conv_full[s], i + 1 + CAT_PAIRS)
                tap = lambda j: pcol[:, ds(i * 2 + s + CONV_AT + 12 * j, 1)]
                dve_link(nc.vector.tensor_scalar(y, conv_in[:, s, PAD - 3:PAD - 3 + LAT], tap(0), None, ALU.mult))
                for j in (1, 2, 3):
                    ins = nc.vector.scalar_tensor_tensor(y, conv_in[:, s, PAD - 3 + j:PAD - 3 + j + LAT], tap(j), y, ALU.mult, ALU.add)
                    if j < 3:
                        dve_link(ins)
                    else:
                        ins.then_inc(conv_done[s], 1)
            dve_leave(6, 6)
        dve.wait_ge(ba_hi, 1)
        nc.vector.tensor_tensor(w_ba_lo[:, :, :], w_ba[:, :, :], w_ba_hi[:, :, :].bitcast(F32), ALU.subtract).then_inc(ba_split, 1)
        dve.wait_ge(ba_mm, 1)
        nc.vector.tensor_copy(gb[:, :, :], bank(7, 64).rearrange("p (c n) -> p c n", n=8)).then_inc(ba_kept, 1)
        meet(dve, "dn_proj")
        for f0, scale in ((0, SCALE_S), (2, 1.0)):
            with dve.Fori(0, 2) as i:
                for s in range(2):
                    dve.wait_ge(d_rooted[s], i + f0 + 1 + V_PAIRS + FREE)
                    x = qkv[:, ds(i * 2 + 2 * f0 + s, 1), :].rearrange("p k n -> p (k n)")
                    nc.vector.scalar_tensor_tensor(x, x, scale, rs_d[:, s, :], ALU.mult, ALU.mult).then_inc(d_scaled[s], 1)
        per_head = lambda a: a[:, :].rearrange("p (c n) -> p c n", c=1).broadcast_to([P, 8, 4])
        dve.wait_ge(ba_kept, 1)
        dve_link(nc.vector.tensor_tensor(g_x[:, :, :], gb[:, :, 4:8], per_head(dtb), ALU.add))
        nc.vector.scalar_tensor_tensor(g_e[:, :, :], g_x[:, :, :], -1.0, g_x[:, :, :], ALU.mult, ALU.max).then_inc(g_abs, 1)
        dve.wait_ge(gb_exp, 1)
        nc.vector.tensor_scalar(g_e[:, :, :], g_e[:, :, :], 1.0, None, ALU.add).then_inc(g_one, 1)
        dve_link(nc.vector.tensor_scalar(beta[:, :, :], beta[:, :, :], 1.0, None, ALU.add))
        nc.vector.reciprocal(beta[:, :, :], beta[:, :, :])
        dve.wait_ge(gb_exp, 2)
        dve_link(nc.vector.scalar_tensor_tensor(g_x[:, :, :], g_x[:, :, :], 0.0, g_e[:, :, :], ALU.max, ALU.add))
        nc.vector.scalar_tensor_tensor(g_log[:, :, :], g_x[:, :, :], -1.0, per_head(ealog), ALU.mult, ALU.mult)
        nc.vector.memset(state[:, :, :], 0.0)
        meet(dve, "dn_l2")
        flat = lambda a: a[:, :, :].rearrange("p h n -> p (h n)")
        over_heads = lambda m: m.rearrange("p (h n) -> p h n", h=1).broadcast_to([P, DN, P])
        over_cols = lambda a: a.rearrange("p (h n) -> p h n", n=1).broadcast_to([P, DN, P])
        in_heads = lambda b: bank(b).rearrange("p (h n) -> p h n", h=DN)
        tt_ = nc.vector.tensor_tensor
        with dve.Fori(0, NQ) as c:
            dve_enter(c, 8)
            dve.wait_ge(kv_turned, c + FREE)
            nc.vector.tensor_copy(g_st[:, 0:4], g_log[:, ds(c, 1), :].rearrange("p c n -> p (c n)"))
            nc.vector.tensor_copy(g_st[:, 4:8], beta[:, ds(c, 1), :].rearrange("p c n -> p (c n)")).then_inc(g_staged, 1)
            dve.wait_ge(gc_mm, c + 1)
            dve_link(nc.vector.tensor_copy(g_c[:, :], bank(2, 4)))
            dve_did(tt_(tail[:, :], in_heads(0)[:, :, P - 1], g_c[:, :], ALU.subtract))
            dve_link(tt_(gx[:, :, :], over_cols(g_c[:, :]), in_heads(0), ALU.subtract))
            nc.vector.tensor_scalar(flat(gx), flat(gx), 0.0, -1.0, ALU.max, ALU.mult).then_inc(gx_ready, 1)
            dve.wait_ge(e_done, c + 1)
            dve_link(tt_(dc[:, :, :], dc[:, :, :], over_heads(tri), ALU.mult))
            dve_did(tt_(beta_eg[:, :], g_st[:, 4:8], e_gc[:, :], ALU.mult))
            dve_link(tt_(flat(db), bank(1), flat(dc), ALU.mult))
            dve.wait_ge(kk_mm, c + 1)
            dve_link(tt_(flat(u_t), bank(3), flat(db), ALU.mult))
            dve_link(tt_(ym[:, :, :], u_t[:, :, :], over_heads(level[0]), ALU.mult))
            tt_(tt[:, :, :], over_heads(ident), ym[:, :, :], ALU.subtract).then_inc(tt_first, 1)
            tt_(flat(a_t), bank(4), flat(dc), ALU.mult)
            dve.wait_ge(kv_turned, c + 1 + FREE)
            tt_(kbg[:, :, :], in_heads(5), over_cols(beta_eg[:, :]), ALU.mult)
            tt_(ktail[:, :, :], in_heads(5), over_cols(tail[:, :]), ALU.mult)
            tt_(vbeta[:, :, :], in_heads(6), over_cols(g_st[:, 4:8]), ALU.mult)
            tt_(qg[:, :, :], st_qkv[:, 0:4, :], eg[:, :, :], ALU.mult).then_inc(ops_ready, 1)
            for lv in range(1, LEVELS):
                n = c * (LEVELS - 1) + lv
                dve.wait_ge(y_mm, n + A_TILES)
                tt_(ym[:, :, :], in_heads(0), over_heads(level[lv]), ALU.mult).then_inc(y_masked, 1)
                dve.wait_ge(z_mm, n + A_TILES + FREE)
                tt_(flat(tt), flat(tt), bank(1), ALU.subtract).then_inc(tt_new, 1)
                if lv < LEVELS - 1:
                    tt_(flat(tm), flat(tm), bank(2), ALU.subtract).then_inc(t_new, 1)
            tt_(s_dec[:, :, :], state[:, :, :], over_cols(eg[:, :, P - 1]), ALU.mult)
            dve.wait_ge(uw_kept, c + 1 + A_TILES)
            dve.wait_ge(ws_mm, c + 1 + A_TILES + FREE)
            tt_(flat(v_new), flat(u_s), bank(5), ALU.subtract).then_inc(v_new_ready, 1)
            dve.wait_ge(state_mm, c + 1)
            tt_(flat(state), flat(s_dec), bank(7), ALU.add).then_inc(state_new, 1)
            dve.wait_ge(od_rooted, c + 1)
            tt_(o_n[:, :, :], in_heads(6), over_cols(o_ss[:, :]), ALU.mult).then_inc(on_ready, 1)
            dve.wait_ge(on_turned, c + 1)
            z = dn[:, :, ds(c * P, P)]
            norm_w = pcol[:, ROW_AT["dn_norm_w_2"]:ROW_AT["dn_norm_w_2"] + 1]
            nc.vector.scalar_tensor_tensor(z, in_heads(5), norm_w, z, ALU.mult, ALU.mult).then_inc(dn_kept, 1)
            dve_leave(8, NQ)
        meet(dve, "delta")
        dve.wait_ge(win_in, 48)
        with dve.Fori(0, DN) as h:
            dve_enter(h, 6 * 3 + NQ * 3)

            def rotate(j):
                dst, s = (q_s if j < 3 else k_s)[:, j % 3, :], j % 2
                dve.wait_ge(qk_mm, h * 6 + j + 1 + B_HEADS)
                dve_link(nc.vector.tensor_tensor(dst, tmp_s[:, s, :], cos_s[:, :], ALU.mult))
                dve_link(nc.vector.tensor_tensor(sq_s[:, s, :], bank(6, LAT), sin_s[:, :], ALU.mult))
                dve_link(nc.vector.tensor_tensor(dst, dst, sq_s[:, s, :], ALU.add))
                dve.wait_ge(qk_rooted, h * 6 + j + 1 + B_HEADS)
                nc.vector.tensor_tensor(dst, dst, rs_s[:, :], ALU.mult).then_inc(qk_done, 1)

            for j in range(6):
                rotate(j)
            for j in range(3):
                dve.wait_ge(vs_turned, h * 3 + j + 1 + B_HEADS)
                nc.vector.tensor_copy(v_s[:, j, :, :].rearrange("p q n -> p (q n)"), bank(4, LAT)).then_inc(vs_done, 1)

            def take_output(n):
                s, m = n % 2, h * NQ + n
                dve.wait_ge(s_exp, m + 1 + B_TILES + FREE)
                dve_link(nc.vector.reciprocal(st_w[:, s, 6:7], st_w[:, s, 5:6]))
                dve.wait_ge(so_mm, m + 1 + B_TILES)
                nc.vector.tensor_scalar(on_s[:, s, :], bank(6, P), st_w[:, s, 6:7], None, ALU.mult).then_inc(so_scaled, 1)
                dve.wait_ge(so_turned, m + 1 + B_TILES)
                nc.vector.tensor_tensor(sw[:, ds(h, 1), n * P:(n + 1) * P].rearrange("p h n -> p (h n)"), bank(7, P),
                                        z_s[:, n * P:(n + 1) * P], ALU.mult).then_inc(so_kept, 1)

            dve.wait_ge(zs_in, h + 1)
            for n in range(NQ):
                s, width = n % 2, len(window_tiles(n)) * P
                dve.wait_ge(s_mm, h * NQ + n + 1 + B_TILES)
                nc.vector.memset(st_w[:, s, 7:8], 0.0)
                col = 0
                for g in range(3):
                    w = min(n + 1, SPAN[g]) * P
                    m0 = STRIP[g] + SPAN[g] * P - w
                    last = nc.vector.tensor_tensor_reduce(
                        out=s_m[:, s, col:col + w], in0=ps[:, col:col + w], in1=mask[:, m0:m0 + w], scale=SCALE_S,
                        scalar=-3.0e38, op0=ALU.add, op1=ALU.max, accum_out=st_w[:, s, g:g + 1])
                    col += w
                dve_link(last)
                dve_link(nc.vector.tensor_reduce(st_w[:, s, 3:4], st_w[:, s, 0:3], AX_X, ALU.max))
                nc.vector.tensor_scalar(st_w[:, s, 4:5], st_w[:, s, 3:4], -1.0, None, ALU.mult).then_inc(s_masked, 1)
                if n:
                    take_output(n - 1)
                for b in range(0, BATCHES[n], 2):
                    dve.wait_ge(s_turned, h * ALL_BATCHES + sum(BATCHES[:n]) + b + 1 + B_TILES)
                    w = min(BANK, width - b * BANK)
                    nc.vector.tensor_copy(pt_s[:, 0, 0:w], bank(4, w)).then_inc(pt_even, 1)
            take_output(NQ - 1)
            dve_leave(6 * 3 + NQ * 3, DN)
        meet(dve, "swa")
        meet(dve, "gates")
        for k, (lo, src, hi) in enumerate(((dn_lo, dn, dn_hi), (sw_lo, sw, sw_hi))):
            dve.wait_ge(split_hi, k + 1)
            nc.vector.tensor_tensor(lo[:, :, :], src[:, :, :], hi[:, :, :].bitcast(F32), ALU.subtract)
        meet(dve, "split2")
        row = lambda a, i: a[:, ds(i, 1), :].rearrange("p k n -> p (k n)")
        with dve.Fori(0, 4) as i:
            dve_enter(i, 4)
            for s in range(2):
                f = i * 2 + s
                dve.wait_ge(w_done[s], i + M_BRANCH + 1)
                dve_did(nc.vector.tensor_tensor(m_t[:, s, :], bank(4 * s, LAT), row(gates, f), ALU.mult))
                dve_link(nc.vector.tensor_tensor(row(gates, f + 8), bank(4 * s + 2, LAT), row(gates, f + 8), ALU.mult))
                nc.vector.tensor_tensor(m_t[:, s, :], m_t[:, s, :], row(gates, f + 8), ALU.add).then_inc(merged[s], 1)
                dve.wait_ge(merged_hi[s], i + 1 + FFN_PAIRS)
                nc.vector.tensor_tensor(row(m_lo, f), m_t[:, s, :], row(m_hi, f).bitcast(F32), ALU.subtract)
            dve_leave(4, 4)
        meet(dve, "branch")
        with dve.Fori(0, 4) as i:
            for s in range(2):
                dve.wait_ge(w_done[s], i + M_OUT2 + 1)
                dve.wait_ge(xp_in[s], i * 16 + 16)
                dve.wait_ge(y_turned[s], i + DOWNS)
                nc.vector.tensor_tensor(y_f[:, s, :], bank(2 * s, LAT), x_piece[:, s, :], ALU.add).then_inc(y_added[s], 1)

    @block.tensor
    def _(pe):
        def turn(dst, src, n=P):
            return nc.tensor.transpose(dst, src, ident[0:n, 0:n])

        pe.wait_ge(consts_in, 16)
        pe.wait_ge(params_in, 16 * (len(ROWS) + 1))
        turn(bank(6, N_ROWS), param_rows[0:N_ROWS, 0, :], N_ROWS).then_inc(params_turned, 1)
        turn(bank(7, 48), param_rows[0:48, 1, :], 48).then_inc(params_turned, 1)

        def turn_x(i):
            for s in range(2):
                pe.wait_ge(x_in[s], i * 16 + 16)
                pe.wait_ge(xt_act[s], i)
                pe.wait_ge(xt_dve[s], i)
                for k in range(KT):
                    last = turn(ps[:, 2 * s * BANK + k * P:2 * s * BANK + (k + 1) * P], x_tile[:, s, k * P:(k + 1) * P])
                last.then_inc(x_turned[s], 1)

        turn_x(0)
        with pe.Fori(1, 5) as i:
            turn_x(i)
        pe.wait_ge(silu_ready, 1)
        with pe.Fori(0, 6) as i:
            for s in range(2):
                pe.wait_ge(ada_in[s], i * 16 + 16)
                for m in range(4):
                    for k in range(KT):
                        last = nc.tensor.matmul(ps[:, ds(i * 16 + 6 * BANK + s * 8 + m * 2, 2)], ada_w[:, s, k, m * P:(m + 1) * P],
                                                silu_c[:, k, :], start=k == 0, stop=k == KT - 1)
                last.then_inc(ada_used[s], 1)
        pe.wait_ge(ada_used[1], 6)
        nc.tensor.matmul(bank(7, 2), ident, ident[:, 0:2], start=True, stop=True).then_inc(ada_mm, 1)
        meet(pe, "input")
        norm1_pe(pe)
        meet(pe, "norm1")
        for m, pieces, n0 in ((M_Q, two, 0), (M_K, three, 2)):
            with pe.Fori(0, 2) as i:
                for s in range(2):
                    pe.wait_ge(rope_done[s], i + n0 + FREE)
                    gemm(pe, i + m, s, h_hi, h_lo, pieces(3 * s))
                for s in range(2):
                    pe.wait_ge(tmp_full[s], i + n0 + 1)
                    for b in range(2):
                        last = nc.tensor.matmul(bank(3 * s + b), rot_a, rope_tmp[:, s, b * BANK:(b + 1) * BANK], start=True, stop=True)
                    last.then_inc(rot_done[s], 1)
        meet(pe, "proj_q")
        with pe.Fori(0, 2) as i:
            for s in range(2):
                pe.wait_ge(v_kept[s], i + FREE)
                gemm(pe, i + M_V, s, h_hi, h_lo, three(3 * s))
            for s in range(2):
                pe.wait_ge(v_full[s], i + 1)
                for kt in range(NKEY):
                    last = turn(ps[:, 3 * s * BANK + kt * P:3 * s * BANK + (kt + 1) * P], v_tmp[:, s, kt * P:(kt + 1) * P])
                last.then_inc(v_turned[s], 1)
        meet(pe, "proj_v")
        for s in range(2):
            gemm(pe, M_C, s, h_hi, h_lo, two(3 * s))
        pe.wait_ge(c_kept, 2)
        for s in range(2):
            gemm(pe, M_C + 1, s, h_hi, h_lo, three(3 * s))
        meet(pe, "proj_c")
        with pe.Fori(0, A_HEADS) as h:
            def scores(qt):
                pe.wait_ge(e_ready, h * NQ + qt + FREE)
                for w in range(2):
                    o = 0
                    while o < TOK:
                        c = w * TOK + o
                        n = min(TOK - o, BANK - c % BANK)
                        last = nc.tensor.matmul(ps[:, c:c + n], qs[:, w, qt * P:(qt + 1) * P], k_a[:, ds(h, 1), o:o + n],
                                                start=True, stop=True)
                        o += n
                last.then_inc(scores_ready, 1)

            def attend(qt):
                n = h * NQ + qt
                pe.wait_ge(mixed, n + 1)
                pe.wait_ge(o_kept, n + FREE)
                for kt in range(NKEY):
                    last = turn(ps[:, 5 * BANK + kt * P:5 * BANK + (kt + 1) * P], prob[:, qt % 2, kt * P:(kt + 1) * P])
                last.then_inc(turned, 1)
                pe.wait_ge(pt_dve, n + 1)
                pe.wait_ge(pt_act, n + 1)
                for kt in range(NKEY):
                    last = nc.tensor.matmul(ps[:, 7 * BANK + 256:7 * BANK + 384], pt[:, kt * P:(kt + 1) * P],
                                            v_a[:, kt, ds(h * P, P)], start=kt == 0, stop=kt == NKEY - 1)
                last.then_inc(o_mm, 1)

            pe.wait_ge(q_staged, h + 1)
            scores(0)
            for qt in range(1, NQ):
                scores(qt)
                attend(qt - 1)
            attend(NQ - 1)
        meet(pe, "attn_a")
        norm_cq_pe(pe)
        pe.wait_ge(norm_rooted, norm_cq_before + 2)
        norm_kv_pe(pe)
        for b in range(2):
            last = nc.tensor.matmul(ps[0:BD, (4 + b) * BANK:(5 + b) * BANK], rot_b[0:BD, 0:BD], kr[0:BD, b * BANK:(b + 1) * BANK],
                                    start=True, stop=True)
        last.then_inc(kr_rot, 1)
        pe.wait_ge(up_split, 1)
        pe.wait_ge(norm_finished, norm_kv_before + 3)
        kv_v = lambda w: w[:, :].rearrange("p (h a n) -> p h a n", h=B_HEADS, a=2)[:, :, 1, :]
        for kt in range(NKEY):
            if kt >= 2:
                pe.wait_ge(vb_kept, kt - 1)
            for n_pass, (a, w) in enumerate(((ckv_hi, kvup_hi), (ckv_lo, kvup_hi), (ckv_hi, kvup_lo))):
                last = nc.tensor.matmul(bank(kt % 2), a[:, kt * P:(kt + 1) * P], kv_v(w), start=n_pass == 0, stop=n_pass == 2)
            last.then_inc(vb_mm, 1)
        meet(pe, "prep_b")
        for g in range(2):
            for h in range(4):
                n = g * 4 + h
                if n:
                    pe.wait_ge(qb_tmp, n)
                for k in range(2):
                    for n_pass, (w, a) in enumerate(((qup_hi, cq_hi), (qup_hi, cq_lo), (qup_lo, cq_hi))):
                        for b in range(2):
                            last = nc.tensor.matmul(ps[0:BD, b * BANK:(b + 1) * BANK], w[:, k, n * BD:(n + 1) * BD],
                                                    a[:, k, b * BANK:(b + 1) * BANK],
                                                    start=k == 0 and n_pass == 0, stop=k == 1 and n_pass == 2)
                last.then_inc(qb_mm, 1)
                if n:
                    pe.wait_ge(kb_kept, n)
                for n_pass, (w, a) in enumerate(((kvup_hi, ckv_hi), (kvup_hi, ckv_lo), (kvup_lo, ckv_hi))):
                    for b, o, w_n in three(4):
                        last = nc.tensor.matmul(bank(b, w_n), w[:, n * P:(n + 1) * P], a[:, o:o + w_n],
                                                start=n_pass == 0, stop=n_pass == 2)
                last.then_inc(kb_mm, 1)
                pe.wait_ge(qb_tmp, n + 1)
                if n:
                    pe.wait_ge(qb_done, n)
                for b in range(2):
                    last = nc.tensor.matmul(ps[0:BD, (2 + b) * BANK:(3 + b) * BANK], rot_b[0:BD, 0:BD],
                                            tmp_b[0:BD, h % 2, b * BANK:(b + 1) * BANK], start=True, stop=True)
                last.then_inc(qb_rot, 1)
            meet(pe, f"heads_b{g}")
            with pe.Fori(0, 4) as h:
                def scores_b(qt):
                    pe.wait_ge(b_e, h * NQ + g * 32 + max(qt - 1, 0) + FREE)
                    for b, o in enumerate(range(0, TOK, BANK)):
                        n = min(BANK, TOK - o)
                        last = nc.tensor.matmul(bank(3 * (qt % 2) + b, n), qs_b[0:BD, qt * P:(qt + 1) * P],
                                                k_b[0:BD, ds(h, 1), o:o + n], start=True, stop=True)
                    last.then_inc(b_scores, 1)

                def attend_b(qt):
                    n = h * NQ + g * 32 + qt
                    pe.wait_ge(b_e, n + 1 + FREE)
                    pe.wait_ge(b_kept, n + FREE)
                    for j, (b, k0, k1) in enumerate(((6, 0, 4), (7, 4, 8), (6, 8, 10))):
                        if j == 2:
                            pe.wait_ge(b_pt0, n + 1)
                        for kt in range(k0, k1):
                            last = turn(ps[:, b * BANK + (kt - k0) * P:b * BANK + (kt - k0 + 1) * P],
                                        e_b[:, qt % 2, kt * P:(kt + 1) * P])
                        last.then_inc(b_turned, 1)
                    pe.wait_ge(b_pt1, n + 1)
                    for kt in range(NKEY):
                        if kt == 8:
                            pe.wait_ge(b_pt2, n + 1)
                        last = nc.tensor.matmul(bank(7, 64), pt_b[:, kt * P:(kt + 1) * P],
                                                v_b[:, kt, ds(h * 64 + g * 256, 64)], start=kt == 0, stop=kt == NKEY - 1)
                    last.then_inc(b_av, 1)

                pe.wait_ge(qb_staged, h + g * 4 + 1)
                scores_b(0)
                for qt in range(1, NQ):
                    scores_b(qt)
                    attend_b(qt - 1)
                attend_b(NQ - 1)
            meet(pe, f"attn_b{g}")
        pe.wait_ge(att_ready, 1)
        for f in range(KT):
            s = f % 2
            pe.wait_ge(cat_taken[s], f // 2)
            for qt in range(NQ):
                last = turn(ps[:, 2 * s * BANK + qt * P:2 * s * BANK + (qt + 1) * P], att[:, qt, f * P:(f + 1) * P])
            last.then_inc(cat_turned[s], 1)
        meet(pe, "cat")
        with pe.Fori(0, 4) as i:
            for s in range(2):
                pe.wait_ge(added[s], i + FREE)
                gemm(pe, i + M_OUT, s, cat_hi, cat_lo, two(2 * s))
        meet(pe, "out1")
        norm2_pe(pe)
        meet(pe, "norm2")

        def gate(i, m):
            for s in range(2):
                pe.wait_ge(gated[s], i)
                gemm(pe, m, s, h2_hi, h2_lo, two(2 * s))

        def up(i, m):
            for s in range(2):
                pe.wait_ge(down_added[s], i * 4)
                gemm(pe, m, s, h2_hi, h2_lo, two(4 + 2 * s))

        def down(i, m):
            for s in range(2):
                pe.wait_ge(hid_split[s], i + 1)
                pe.wait_ge(w_split[s], m + 1)
            for f in range(KT):
                fs = f % 2
                pe.wait_ge(down_added[fs], i * 4 + f // 2)
                for s in range(2):
                    for n_pass, (w, a) in enumerate(((w_hi, hid_hi), (w_hi, hid_lo), (w_lo, hid_hi))):
                        for b in range(2):
                            last = nc.tensor.matmul(bank(4 + 2 * fs + b), w[:, s, f, :], a[:, s, b * BANK:(b + 1) * BANK],
                                                    start=s == 0 and n_pass == 0, stop=s == 1 and n_pass == 2)
                    if f == KT - 1:
                        last.then_inc(w_done[s], 1)
                    elif s == 1:
                        last.then_inc(down_mm[fs], 1)

        gate(0, M_FFN)
        up(0, M_FFN + 1)
        with pe.Fori(1, FT // 2) as i:
            gate(i, i * 3 + M_FFN - 1)
            down(i - 1, i * 3 + M_FFN)
            up(i, i * 3 + M_FFN + 1)
        down(FT // 2 - 1, M_FFN + 32)
        meet(pe, "ffn")
        norm_f_pe(pe)
        pe.wait_ge(norm_rooted, norm_f_before + 2)
        norm3_pe(pe)
        meet(pe, "norm3")
        pe.wait_ge(norm_finished, norm3_before + 2)
        with pe.Fori(0, 6) as i:
            for s in range(2):
                pe.wait_ge(conv_full[s], i + CAT_PAIRS)
                gemm(pe, i + M_DN, s, h2_hi, h2_lo, two(2 * s))
        with pe.Fori(0, 2) as i:
            for s in range(2):
                pe.wait_ge(conv_full[s], CAT_PAIRS + 6)
                pe.wait_ge(z_kept[s], i + CAT_PAIRS)
                gemm(pe, i + M_DN + 6, s, h2_hi, h2_lo, two(2 * s))
        pe.wait_ge(ba_split, 1)
        for qt in range(NQ):
            for k in range(KT):
                for n_pass, (w, a) in enumerate(((w_ba_hi, h2_hi), (w_ba_hi, h2_lo), (w_ba_lo, h2_hi))):
                    last = nc.tensor.matmul(ps[:, 7 * BANK + qt * 8:7 * BANK + qt * 8 + 8], a[:, k, qt * P:(qt + 1) * P],
                                            w[:, k, :], start=k == 0 and n_pass == 0, stop=k == KT - 1 and n_pass == 2)
        last.then_inc(ba_mm, 1)
        meet(pe, "dn_proj")
        with pe.Fori(0, 4) as i:
            for s in range(2):
                pe.wait_ge(d_squared[s], i + 1 + V_PAIRS)
                pe.wait_ge(d_rooted[s], i + V_PAIRS + FREE)
                for b in range(2):
                    last = nc.tensor.matmul(bank(2 * s + b), ones_mean, sq_d[:, s, b * BANK:(b + 1) * BANK], start=True, stop=True)
                last.then_inc(d_summed[s], 1)
        meet(pe, "dn_l2")

        def per_head(b, lhs, rhs, start=True, stop=True):
            for h in range(DN):
                last = nc.tensor.matmul(bank(b)[:, h * P:(h + 1) * P], lhs(h), rhs(h), start=start, stop=stop)
            return last

        of = lambda a: lambda h: a[:, h, :]
        with pe.Fori(0, NQ) as c:
            pe.wait_ge(g_staged, c + 1)
            pe.wait_ge(y_masked, c * (LEVELS - 1) + A_TILES)
            per_head(0, lambda h: g_st[:, h:h + 1].broadcast_to([P, P]), lambda h: tri)
            per_head(1, lambda h: g_st[:, 4 + h:5 + h].broadcast_to([P, P]), lambda h: ident)
            nc.tensor.matmul(bank(2, 4), tri, g_st[:, 0:4], start=True, stop=True).then_inc(gc_mm, 1)
            pe.wait_ge(staged, c + 1)
            key = lambda h: st_qkv[:, 4 + h, :]
            per_head(3, key, key)
            per_head(4, key, lambda h: st_qkv[:, h, :]).then_inc(kk_mm, 1)
            pe.wait_ge(dn_kept, c + FREE)
            for b, g in ((5, 4), (6, 8)):
                for h in range(DN):
                    last = turn(bank(b)[:, h * P:(h + 1) * P], st_qkv[:, g + h, :])
            last.then_inc(kv_turned, 1)
            pe.wait_ge(tt_first, c + 1)
            pe.wait_ge(state_new, c + FREE)
            for h in range(DN):
                last = turn(bank(7)[:, h * P:(h + 1) * P], tt[:, h, :])
            last.then_inc(t_turned, 1)
            for lv in range(1, LEVELS):
                n = c * (LEVELS - 1) + lv
                if lv == 1:
                    pe.wait_ge(t_kept, c + 1)
                else:
                    pe.wait_ge(t_new, c * (LEVELS - 2) + lv - 1 + A_TILES)
                if lv == 1:
                    pe.wait_ge(ops_ready, c + 1 + FREE)
                per_head(0, of(u_t), of(tm)).then_inc(y_mm, 1)
                pe.wait_ge(y_masked, n + A_TILES)
                last = per_head(1, of(ym), of(tt))
                if lv < LEVELS - 1:
                    last = per_head(2, of(tt), of(ym))
                last.then_inc(z_mm, 1)
            pe.wait_ge(tt_new, c * (LEVELS - 1) + LEVELS - 1 + A_TILES)
            per_head(3, of(tt), of(vbeta))
            per_head(4, of(kbg), of(tt)).then_inc(uw_mm, 1)
            pe.wait_ge(uw_kept, c + 1 + A_TILES)
            per_head(5, of(w_t), of(state)).then_inc(ws_mm, 1)
            pe.wait_ge(v_new_ready, c + 1 + A_TILES + FREE)
            for h in range(DN):
                nc.tensor.matmul(bank(6)[:, h * P:(h + 1) * P], qg[:, h, :], state[:, h, :], start=True, stop=False)
                last = nc.tensor.matmul(bank(6)[:, h * P:(h + 1) * P], a_t[:, h, :], v_new[:, h, :], start=False, stop=True)
            last.then_inc(od_mm, 1)
            per_head(7, of(ktail), of(v_new)).then_inc(state_mm, 1)
            pe.wait_ge(on_ready, c + 1)
            for h in range(DN):
                last = turn(bank(5)[:, h * P:(h + 1) * P], o_n[:, h, :])
            last.then_inc(on_turned, 1)
        meet(pe, "delta")
        with pe.Fori(0, DN) as h:
            def after(c):
                s = c % 2
                if c < 6:
                    pe.wait_ge(qk_in, h * 6 + c + 1 + B_HEADS)
                    pe.wait_ge(qk_done, h * 6 + c + B_HEADS)
                    for b in range(2):
                        nc.tensor.matmul(bank(4 + b), ones_mean, sq_s[:, s, b * BANK:(b + 1) * BANK], start=True, stop=True)
                    for b in range(2):
                        last = nc.tensor.matmul(bank(6 + b), rot_s, tmp_s[:, s, b * BANK:(b + 1) * BANK], start=True, stop=True)
                    last.then_inc(qk_mm, 1)
                elif c < 9:
                    pe.wait_ge(vs_in, h * 3 + c - 5 + B_HEADS)
                    pe.wait_ge(qk_done, h * 6 + 6 + B_HEADS)
                    pe.wait_ge(vs_done, h * 3 + c - 6 + B_HEADS)
                    for q in range(NQ):
                        last = turn(ps[:, 4 * BANK + q * P:4 * BANK + (q + 1) * P], tmp_s[:, s, q * P:(q + 1) * P])
                    last.then_inc(vs_turned, 1)

            pe.wait_ge(so_kept, h * NQ + B_TILES + FREE)
            for c in range(10):
                if 2 <= c < 8:
                    pe.wait_ge(qk_in, h * 6 + c - 1 + B_HEADS)
                elif c >= 8:
                    pe.wait_ge(vs_in, h * 3 + c - 7 + B_HEADS)
                gemm(pe, h * 5 + M_SWA + c // 2, c % 2, h2_hi, h2_lo, two(2 * (c % 2)))
                if c:
                    after(c - 1)

            def scores(n):
                pe.wait_ge(s_masked, h * NQ + n + B_TILES)
                for g, kt, col in window_tiles(n):
                    last = nc.tensor.matmul(ps[:, col:col + P], q_s[:, g, n * P:(n + 1) * P], k_s[:, g, kt * P:(kt + 1) * P],
                                            start=True, stop=True)
                last.then_inc(s_mm, 1)

            def attend(n):
                m, tiles = h * NQ + n, window_tiles(n)
                pe.wait_ge(s_exp, m + 1 + B_TILES + FREE)
                pe.wait_ge(so_kept, m + B_TILES + FREE)

                def turn_batch(b):
                    for j in range(4 * b, min(4 * b + 4, len(tiles))):
                        last = turn(ps[:, (4 + b % 2) * BANK + (j % 4) * P:(4 + b % 2) * BANK + (j % 4 + 1) * P],
                                    s_m[:, n % 2, j * P:(j + 1) * P])
                    last.then_inc(s_turned, 1)

                def weigh_batch(b):
                    even = sum((x + 1) // 2 for x in BATCHES)
                    odd = sum(x // 2 for x in BATCHES)
                    if b % 2 == 0:
                        pe.wait_ge(pt_even, h * even + sum((x + 1) // 2 for x in BATCHES[:n]) + b // 2 + 1)
                    else:
                        pe.wait_ge(pt_odd, h * odd + sum(x // 2 for x in BATCHES[:n]) + b // 2 + 1)
                    for j in range(4 * b, min(4 * b + 4, len(tiles))):
                        g, kt, _ = tiles[j]
                        last = nc.tensor.matmul(bank(6, P), pt_s[:, b % 2, (j % 4) * P:(j % 4 + 1) * P], v_s[:, g, kt, :],
                                                start=j == 0, stop=j == len(tiles) - 1)
                    return last

                turn_batch(0)
                for b in range(1, BATCHES[n]):
                    turn_batch(b)
                    weigh_batch(b - 1)
                weigh_batch(BATCHES[n] - 1).then_inc(so_mm, 1)
                pe.wait_ge(so_scaled, m + 1 + B_TILES)
                turn(bank(7, P), on_s[:, n % 2, :]).then_inc(so_turned, 1)

            pe.wait_ge(vs_done, h * 3 + 3 + B_HEADS)
            pe.wait_ge(zs_in, h + 1)
            scores(0)
            for n in range(1, NQ):
                scores(n)
                attend(n - 1)
            attend(NQ - 1)
        meet(pe, "swa")
        with pe.Fori(0, 8) as i:
            for s in range(2):
                pe.wait_ge(gate_kept[s], i + FFN_PAIRS)
                gemm(pe, i + M_GATE, s, h2_hi, h2_lo, two(2 * s))
        meet(pe, "gates")
        meet(pe, "split2")
        with pe.Fori(0, 4) as i:
            for s in range(2):
                pe.wait_ge(w_split[s], i + M_BRANCH + 1)
                pe.wait_ge(merged[s], i + FFN_PAIRS)
                for k in range(KT):
                    hi, lo = (dn_hi, dn_lo) if k < 4 else (sw_hi, sw_lo)
                    for n_pass, (w, a) in enumerate(((w_hi, hi), (w_hi, lo), (w_lo, hi))):
                        for b in range(2):
                            last = nc.tensor.matmul(bank(4 * s + 2 * (k // 4) + b), w[:, s, k, :], a[:, k % 4, b * BANK:(b + 1) * BANK],
                                                    start=k % 4 == 0 and n_pass == 0, stop=k % 4 == 3 and n_pass == 2)
                last.then_inc(w_done[s], 1)
        meet(pe, "branch")
        with pe.Fori(0, 4) as i:
            for s in range(2):
                pe.wait_ge(y_added[s], i + CAT_PAIRS + FREE)
                gemm(pe, i + M_OUT2, s, m_hi, m_lo, two(2 * s))
            for s in range(2):
                pe.wait_ge(y_added[s], i + 1 + CAT_PAIRS + FREE)
                pe.wait_ge(y_kept[s], i + FFN_PAIRS)
                for q in range(NQ):
                    last = turn(ps[:, (4 + 2 * s) * BANK + q * P:(4 + 2 * s) * BANK + (q + 1) * P], y_f[:, s, q * P:(q + 1) * P])
                last.then_inc(y_turned[s], 1)

    ctx.close()


_INS = ["x", "c", "ctx", "c_ctx", "w_ada", "b_ada", "w_in", "q_a_norm", "kv_a_norm", "w_q_up", "w_kv_up", "diff_lambda",
        "diff_subln", "w_out", "w_ffn_in", "w_ffn_out", "final_norm", "norm_w_2", "w_in_2", "conv_w_2", "dn_a_log_2",
        "dn_dt_bias_2", "dn_norm_w_2", "q_norm_w_2", "k_norm_w_2", "w_branch_dn_2", "w_branch_swa_2", "w_out_2"]


def kernel(**inputs):
    import concourse.bacc as bacc
    from concourse.bass_utils import run_bass_kernel_spmd

    nc = bacc.Bacc("TRN2", target_bir_lowering=False, num_devices=1)
    arrays = {name: np.ascontiguousarray(inputs[name]) for name in _INS}
    arrays["w_branch"] = np.concatenate([arrays.pop("w_branch_dn_2")[0], arrays.pop("w_branch_swa_2")[0]], axis=0)
    arrays.update(shape_tables())
    tensors = {name: nc.dram_tensor(name, a.shape, F32, kind="ExternalInput").ap() for name, a in arrays.items()}
    tensors["out"] = nc.dram_tensor("out", [1, LAT, D], F32, kind="ExternalOutput").ap()
    build(nc, tensors)
    return run_bass_kernel_spmd(nc, [arrays], core_ids=[0]).results[0]["out"]
```

```python
import math
from contextlib import ExitStack

import numpy as np
import concourse.bass as bass
from concourse import mybir

F32 = mybir.dt.float32
F32R = mybir.dt.float32r
ALU = mybir.AluOpType
ACT = mybir.ActivationFunctionType
AX_X = mybir.AxisListType.X
ds = bass.ds

P = 128
D = 1024
KT = D // P
LAT, CTX = 1024, 256
TOK = LAT + CTX
NQ = LAT // P
NKEY = TOK // P
BANK = 512
EPS = 1e-6
A_HEADS, B_HEADS = 4, 8
QR, KVR = 256, 128
BD, NOPE, ROPE_B = 96, 64, 32
FFN = 2816
FT = FFN // P
LAM_INIT = 0.8 - 0.6 * math.exp(0.0)
SCALE_A = 64.0 ** -0.5
SCALE_B = 96.0 ** -0.5
SCALE_S = 128.0 ** -0.5
DN = 4
GROUPS = ((128, 1), (512, 4), (2048, 16))
PAD = 8
LEVELS = 7
C_Z, C_B, C_SQ = 1536, 2048, 2056
C_SK, C_SV, C_SZ = C_SQ + 1536, C_SQ + 3072, C_SQ + 4608
C_G = C_SZ + 512
ROWS = [("b_ada", 48), ("c", 8), ("c_ctx", 8), ("final_norm", 8), ("norm_w_2", 8), ("q_a_norm", 2),
        ("kv_a_norm", 1), ("diff_subln", 1), ("dn_norm_w_2", 1), ("q_norm_w_2", 3), ("k_norm_w_2", 3)]
ROW_AT = {}
for _name, _n in ROWS:
    ROW_AT[_name] = sum(n for _, n in ROWS[:len(ROW_AT)])
N_ROWS = sum(n for _, n in ROWS)
CONV_AT = 96
M_Q, M_K, M_V, M_C = 0, 2, 4, 6
M_OUT = 8
M_FFN = 12
M_DN = M_FFN + 2 * (FT // 2)
M_SWA = M_DN + 8
M_GATE = M_SWA + 5 * DN
M_BRANCH = M_GATE + 8
M_OUT2 = M_BRANCH + 4
PAIRS = M_OUT2 + 4


def shape_tables():
    eye = np.eye(P, dtype=np.float32)
    i, j = np.arange(P)[:, None], np.arange(P)[None, :]

    def rot(block, lo, hi):
        r = np.zeros((P, P), np.float32)
        for a in range(lo, hi):
            up = (a - lo) % block < block // 2
            r[a, a + block // 2 if up else a - block // 2] = -1.0 if up else 1.0
        return r.T
    mats = [eye, np.full((P, P), 1.0 / P, np.float32), rot(32, 0, 128), rot(16, 64, 96), rot(32, 0, 32),
            (i <= j).astype(np.float32)]
    mats.append(((i // 2 == j // 2) & (i % 2 == 0) & (j % 2 == 1)).astype(np.float32))
    for lv in range(1, LEVELS):
        s = 1 << lv
        mats.append(((i // (2 * s) == j // (2 * s)) & (i // s % 2 == 1) & (j // s % 2 == 0)).astype(np.float32))
    consts = np.concatenate(mats, axis=1).astype(np.float32)

    t = np.arange(LAT)
    row, col = (t // 64).astype(np.float32), (t % 64).astype(np.float32)

    def axial(quarter, lo, n):
        inv = (np.float32(10000.0) ** (-np.arange(quarter, dtype=np.float32) / np.float32(quarter))).astype(np.float32)
        cos, sin = np.ones((P, LAT), np.float32), np.zeros((P, LAT), np.float32)
        for a in range(lo, lo + n):
            b = a - lo
            pos = row if (b // (2 * quarter)) % 2 == 0 else col
            ang = pos * inv[b % quarter]
            cos[a], sin[a] = np.cos(ang), np.sin(ang)
        return np.stack([cos, sin], 1)
    trig_a, trig_b = axial(16, 0, 128), axial(8, 64, 32)
    inv = (np.float32(500000.0) ** (-np.arange(0, 32, 2, dtype=np.float32) / np.float32(32))).astype(np.float32)
    cos, sin = np.ones((P, LAT), np.float32), np.zeros((P, LAT), np.float32)
    for a in range(32):
        ang = t.astype(np.float32) * inv[a % 16]
        cos[a], sin[a] = np.cos(ang), np.sin(ang)
    trig_s = np.stack([cos, sin], 1)
    strips = []
    for window, dil in GROUPS:
        n = min(window // P, NQ - 1)
        for back in range(n, -1, -1):
            dist = back * P + i - j
            ok = (dist >= 0) & (dist <= window) & (dist % dil == 0)
            strips.append(np.where(ok, 0.0, -1e30).astype(np.float32))
    window_mask = np.concatenate(strips, axis=1)
    f = lambda a: np.ascontiguousarray(a, np.float32)
    return dict(consts=f(consts), trig_a=f(trig_a), trig_b=f(trig_b), trig_s=f(trig_s), window_mask=f(window_mask))


SWA_COLS = [C_SQ + g * 512 for g in range(3)] + [C_SK + g * 512 for g in range(3)] + [C_SV + g * 512 for g in range(3)] + [C_SZ]


def window_tiles(n):
    out = []
    for g in range(3):
        for kt in range(max(0, n + 1 - SPAN[g]), n + 1):
            out.append((g, kt, len(out) * P))
    return out


SPAN = [min(w // P, NQ - 1) + 1 for w, _ in GROUPS]
STRIP = [sum(SPAN[:g]) * P for g in range(3)]
MASK_W = sum(SPAN) * P
BATCHES = [-(-len(window_tiles(n)) // 4) for n in range(NQ)]
ALL_BATCHES = sum(BATCHES)


def build(nc, t):
    ctx = ExitStack()
    sem = lambda name: ctx.enter_context(nc.semaphore(name))
    pair = lambda name: [sem(f"{name}_{s}") for s in range(2)]
    base = 16512

    def at(name, off, *shape, dt=F32):
        return nc.alloc_sbuf_tensor_at(name, [P, *shape], dt, offset=base + 4 * off)

    w_raw = at("w_raw", 0, 2, KT, P)
    w_hi = at("w_hi", 2048, 2, KT, P, dt=F32R)
    w_lo = at("w_lo", 4096, 2, KT, P, dt=F32R)
    consts = at("consts", 6144, 6 + LEVELS, P)
    ident, ones_mean, rot_a, rot_b, rot_s, tri = (consts[:, n, :] for n in range(6))
    level = [consts[:, 6 + n, :] for n in range(LEVELS)]
    pcol = at("pcol", 7808, 144)
    ada = at("ada", 7952, 48, 2)
    ada_1 = at("ada_1", 8048, 48, 2)
    lam_in = at("lam_in", 8144, 2, 2, 64)
    lam_prod = at("lam_prod", 8400, 2, 64)
    silu_c = at("silu_c", 8528, KT, 2)
    lam_e = at("lam_e", 8544, 2)
    minus_lam = at("minus_lam", 8552, 1)
    alog = at("alog", 8560, 4)
    dtb = at("dtb", 8568, 4)
    ealog = at("ealog", 8576, 4)
    zero = at("zero", 8584, 1)
    subln = at("subln", 8592, 1)
    A0 = 8704

    x_tile = at("x_tile", A0 + 40000, 2, D)
    param_rows = at("param_rows", A0 + 42048, 2, P)
    ada_w = at("ada_w", A0 + 12288, 4, KT, BANK)
    ada_w2 = at("ada_w2", A0 + 40448, 2, KT, P)
    xt5 = at("xt5", A0, KT, TOK)
    xt = at("xt", A0, KT, LAT)
    h_hi = at("h_hi", A0 + 10240, KT, TOK, dt=F32R)
    h_lo = at("h_lo", A0 + 20480, KT, TOK, dt=F32R)
    n_u = at("n_u", A0 + 30720, 2, KT, BANK)
    n_rs = at("n_rs", A0 + 38912, 2, BANK)
    q_a = at("q_a", A0, A_HEADS, LAT)
    k_a = at("k_a", A0 + 4096, A_HEADS, TOK)
    v_a = at("v_a", A0 + 30720, NKEY, 512)
    cq = at("cq", A0 + 35840, 2, LAT)
    ckv = at("ckv", A0 + 37888, TOK)
    kr = at("kr", A0 + 39168, TOK)
    cos_a = at("cos_a", A0 + 9216, LAT)
    sin_a = at("sin_a", A0 + 40448, LAT)
    rope_tmp = at("rope_tmp", A0 + 41472, 2, LAT)
    v_tmp = at("v_tmp", A0 + 40448, 2, TOK)
    att = at("att", A0 + 10240, NQ, D)
    e_a = at("e_a", A0 + 18432, 2, 2, TOK)
    prob = at("prob", A0 + 23552, 2, TOK)
    pt = at("pt", A0 + 26112, TOK)
    qs = at("qs", A0 + 27392, 2, LAT)
    st_a = at("st_a", A0 + 29440, 32)
    st_m = at("st_m", A0 + 29472, 2, 2)
    st_s = at("st_s", A0 + 29480, 2, 2)
    st_r = at("st_r", A0 + 29488, 2, 2)
    st_c = at("st_c", A0 + 29632, 2, 1)
    st_x = at("st_x", A0 + 29640, 2, 2)
    sq_junk = at("sq_junk", A0 + 29696, 2, P)
    q_b = at("q_b", A0, 4, LAT)
    k_b = at("k_b", A0 + 4096, 4, TOK)
    cos_b = at("cos_b", A0 + 9216, LAT)
    cq_hi = at("cq_hi", A0 + 18432, 2, LAT, dt=F32R)
    cq_lo = at("cq_lo", A0 + 20480, 2, LAT, dt=F32R)
    ckv_hi = at("ckv_hi", A0 + 22528, TOK, dt=F32R)
    ckv_lo = at("ckv_lo", A0 + 23808, TOK, dt=F32R)
    e_b = at("e_b", A0 + 25088, 2, TOK)
    tmp_b = at("tmp_b", A0 + 25088, 2, LAT)
    pt_b = at("pt_b", A0 + 27648, TOK)
    st_b = at("st_b", A0 + 29600, 2, 4)
    qs_b = at("qs_b", A0 + 29696, LAT)
    v_b = at("v_b", A0 + 30720, NKEY, 512)
    qup_raw = at("qup_raw", A0, 2, 768)
    kvup_raw = at("kvup_raw", A0 + 1536, 1024)
    qup_hi = at("qup_hi", A0 + 35840, 2, 768, dt=F32R)
    qup_lo = at("qup_lo", A0 + 37376, 2, 768, dt=F32R)
    kvup_hi = at("kvup_hi", A0 + 40448, 1024, dt=F32R)
    kvup_lo = at("kvup_lo", A0 + 41472, 1024, dt=F32R)
    sin_b = at("sin_b", A0 + 42496, LAT)
    nb_u = at("nb_u", A0 + 2560, 2, 2, BANK)
    nb_rs = at("nb_rs", A0 + 4608, 2, BANK)
    cat_hi = at("cat_hi", A0 + 18432, KT, LAT, dt=F32R)
    cat_lo = at("cat_lo", A0 + 26624, KT, LAT, dt=F32R)
    cat_t = at("cat_t", A0 + 36864, 2, LAT)
    h2_hi = at("h2_hi", A0 + 18432, KT, LAT, dt=F32R)
    h2_lo = at("h2_lo", A0 + 26624, KT, LAT, dt=F32R)
    n2_u = at("n2_u", A0 + 8192, 2, KT, BANK)
    n2_rs = at("n2_rs", A0 + 16384, 2, BANK)
    wd_raw = at("wd_raw", A0 + 8192, 2, KT, P)
    wd_hi = at("wd_hi", A0 + 10240, 2, KT, P, dt=F32R)
    wd_lo = at("wd_lo", A0 + 12288, 2, KT, P, dt=F32R)
    gate_s = at("gate_s", A0 + 34816, 2, LAT)
    hid = at("hid", A0 + 36864, 2, LAT)
    hid_hi = at("hid_hi", A0 + 38912, 2, LAT, dt=F32R)
    hid_lo = at("hid_lo", A0 + 40960, 2, LAT, dt=F32R)

    qkv = at("qkv", A0, 12, LAT)
    conv_in = at("conv_in", A0 + 12288, 2, PAD + LAT)
    sq_d = at("sq_d", A0 + 12288, 2, LAT)
    rs_d = at("rs_d", A0 + 14336, 2, LAT)
    dn = at("dn", A0 + 40400, DN, LAT)
    heads = lambda name, n: at(name, A0 + n, DN, P)
    st_qkv = at("st_qkv", A0 + 12288, 12, P)
    eg, dc, db, u_t, a_t = (heads(n, 13824 + 512 * j) for j, n in enumerate(("eg", "dc", "db", "u_t", "a_t")))
    kbg, ktail, vbeta, qg = (heads(n, 16384 + 512 * j) for j, n in enumerate(("kbg", "ktail", "vbeta", "qg")))
    tt, tm, ym, u_s, w_t, v_new, state, o_n, gx, s_dec = (heads(n, 34816 + 512 * j) for j, n in enumerate(
        ("tt", "tm", "ym", "u_s", "w_t", "v_new", "state", "o_n", "gx", "s_dec")))
    gb = at("gb", A0 + 39936, 8, 8)
    w_ba = at("w_ba", A0 + 40000, 8, 8)
    w_ba_hi = at("w_ba_hi", A0 + 40064, 8, 8, dt=F32R)
    w_ba_lo = at("w_ba_lo", A0 + 40128, 8, 8, dt=F32R)
    beta = at("beta", A0 + 40192, 8, 4)
    g_log = at("g_log", A0 + 40224, 8, 4)
    g_x = at("g_x", A0 + 40256, 8, 4)
    g_e = at("g_e", A0 + 40288, 8, 4)
    g_st = at("g_st", A0 + 40320, 8)
    g_c, e_gc, beta_eg, tail, o_ss = (at(n, A0 + 40328 + 8 * j, 4) for j, n in enumerate(("g_c", "e_gc", "beta_eg", "tail", "o_ss")))
    q_s = at("q_s", A0, 3, LAT)
    k_s = at("k_s", A0 + 3072, 3, LAT)
    v_s = at("v_s", A0 + 6144, 3, NQ, P)
    tmp_s = at("tmp_s", A0 + 9216, 2, LAT)
    sq_s = at("sq_s", A0 + 11264, 2, LAT)
    rs_s = at("rs_s", A0 + 13312, LAT)
    cos_s = at("cos_s", A0 + 14336, LAT)
    sin_s = at("sin_s", A0 + 15360, LAT)
    mask = at("mask", A0 + 16384, MASK_W)
    s_m = at("s_m", A0 + 9216, 2, MASK_W)
    pt_s = at("pt_s", A0 + 13056, 2, BANK)
    sw = at("sw", A0 + 34816, DN, LAT)
    z_s = at("z_s", A0 + 38912, LAT)
    on_s = at("on_s", A0 + 39936, 2, P)
    st_w = at("st_w", A0 + 40192, 2, 8)
    gates = at("gates", A0, 16, LAT)
    m_hi = at("m_hi", A0, KT, LAT, dt=F32R)
    m_lo = at("m_lo", A0 + 8192, KT, LAT, dt=F32R)
    m_t = at("m_t", A0 + 16384, 2, LAT)
    dn_hi = at("dn_hi", A0 + 18432, DN, LAT, dt=F32R)
    dn_lo = at("dn_lo", A0 + 22528, DN, LAT, dt=F32R)
    sw_hi = at("sw_hi", A0 + 26624, DN, LAT, dt=F32R)
    sw_lo = at("sw_lo", A0 + 30720, DN, LAT, dt=F32R)
    x_piece = at("x_piece", A0 + 34816, 2, LAT)
    y_f = at("y_f", A0 + 36864, 2, LAT)
    y_t = at("y_t", A0 + 38912, 2, NQ, P)

    ps = ctx.enter_context(nc.psum_tensor("ps", [P, 8 * BANK], F32))
    bank = lambda b, n=BANK: ps[:, b * BANK:b * BANK + n]

    x_scratch = nc.dram_tensor("x_scratch", [P, KT, LAT], F32, kind="Internal").ap()

    FREE = 1
    phase_end = sem("phase_end")
    w_loaded, w_split, w_done = pair("w_loaded"), pair("w_split"), pair("w_done")
    wd_loaded, wd_split, wd_done = pair("wd_loaded"), pair("wd_split"), pair("wd_done")
    consts_in, params_in, small_in = sem("consts_in"), sem("params_in"), sem("small_in")
    params_turned, pcol_ready, silu_ready = sem("params_turned"), sem("pcol_ready"), sem("silu_ready")
    x_in, x_turned, xt_dve, xt_act = pair("x_in"), pair("x_turned"), pair("xt_dve"), pair("xt_act")
    ada_in, ada_in_2, ada_used, ada_mm = pair("ada_in"), pair("ada_in_2"), pair("ada_used"), sem("ada_mm")
    dve_step, act_step = sem("dve_step"), sem("act_step")
    spilled, trig_in, xt_back = sem("spilled"), sem("trig_in"), sem("xt_back")

    PHASES = ["input", "norm1", "proj_q", "proj_v", "proj_c", "attn_a", "prep_b", "heads_b0", "attn_b0", "heads_b1", "attn_b1",
              "cat", "out1", "norm2", "ffn", "norm3", "dn_proj", "dn_l2", "delta", "swa", "gates", "split2",
              "branch", "out2", "end"]
    at_end = {p: 3 * (n + 1) for n, p in enumerate(PHASES)}
    order = {}

    def meet(eng, name):
        done = order.setdefault(id(eng), [])
        done.append(name)
        assert PHASES[:len(done)] == done, done
        eng.drain().then_inc(phase_end, 1)
        eng.wait_ge(phase_end, at_end[name])

    def chain(eng, step):
        count = [0, 0, 0]

        def did(ins):
            ins.then_inc(step, 1)
            count[0] += 1

        def link(ins):
            did(ins)
            eng.wait_ge(step, count[1] + count[0])

        def enter(i, per):
            count[1], count[2] = i * per, count[0]

        def leave(per, times):
            assert count[0] - count[2] == per, (count[0] - count[2], per)
            count[0], count[1] = count[2] + per * times, 0
        return did, link, enter, leave, lambda: count[0]

    dve_did, dve_link, dve_enter, dve_leave, _ = chain(nc.vector, dve_step)
    act_did, act_link, act_enter, act_leave, act_count = chain(nc.scalar, act_step)

    norm_squared, norm_summed, norm_rooted, norm_scaled, norm_rounded, norm_finished = (
        sem(f"norm_{n}") for n in ("squared", "summed", "rooted", "scaled", "rounded", "finished"))
    norm_pieces = [0, 0]

    def norm(x, nk, pieces, u, rs, gain, shift, hi, lo, out=None):
        before, before_split = norm_pieces
        norm_pieces[0] += len(pieces)
        norm_pieces[1] += 0 if out is not None else len(pieces)

        def view(a, o, n):
            return a[:, :, o:o + n] if nk > 1 else a[:, o:o + n].rearrange("p (k n) -> p k n", k=1)

        def norm_act(act):
            def square(p):
                o, n, which = pieces[p]
                if p >= 2:
                    act.wait_ge(norm_finished, before + p - 1)
                nc.scalar.activation(u[:, p % 2, 0:nk, 0:n], view(x, o, n), ACT.Square).then_inc(norm_squared, 1)

            square(0)
            for p, (o, n, which) in enumerate(pieces):
                act.wait_ge(norm_summed, before + p + 1)
                act_link(nc.scalar.activation(rs[:, p % 2, 0:n], bank(p % 2, n), ACT.Ln, bias=eps_col[:, 0:1], scale=1.0 / nk))
                nc.scalar.activation(rs[:, p % 2, 0:n], rs[:, p % 2, 0:n], ACT.Exp, scale=-0.5).then_inc(norm_rooted, 1)
                if p + 1 < len(pieces):
                    square(p + 1)
                if out is None:
                    act.wait_ge(norm_scaled, before_split + p + 1)
                    if shift is None:
                        last = nc.scalar.activation(view(hi, o, n), u[:, p % 2, 0:nk, 0:n], ACT.Copy)
                    else:
                        for k in range(nk):
                            last = nc.scalar.activation(hi[:, k, o:o + n], u[:, p % 2, k, 0:n], ACT.Identity, bias=shift(k, which))
                    last.then_inc(norm_rounded, 1)

        def norm_pe(pe):
            for p, (o, n, which) in enumerate(pieces):
                pe.wait_ge(norm_squared, before + p + 1)
                if p >= 2:
                    pe.wait_ge(norm_rooted, before + p - 1)
                for k in range(nk):
                    last = nc.tensor.matmul(bank(p % 2, n), ones_mean, u[:, p % 2, k, 0:n], start=k == 0, stop=k == nk - 1)
                last.then_inc(norm_summed, 1)

        def norm_dve(dve):
            for p, (o, n, which) in enumerate(pieces):
                dve.wait_ge(norm_rooted, before + p + 1)
                for k in range(nk):
                    dst = u[:, p % 2, k, 0:n] if out is None else out[:, k, o:o + n]
                    last = nc.vector.scalar_tensor_tensor(dst, view(x, o, n)[:, k, :], gain(k, which), rs[:, p % 2, 0:n],
                                                          ALU.mult, ALU.mult)
                if out is not None:
                    last.then_inc(norm_finished, 1)
                    continue
                last.then_inc(norm_scaled, 1)
                dve.wait_ge(norm_rounded, before_split + p + 1)
                if shift is None:
                    last = nc.vector.tensor_tensor(view(lo, o, n), u[:, p % 2, 0:nk, 0:n], view(hi, o, n).bitcast(F32), ALU.subtract)
                else:
                    for k in range(nk):
                        last = nc.vector.scalar_tensor_tensor(lo[:, k, o:o + n], u[:, p % 2, k, 0:n], shift(k, which),
                                                              hi[:, k, o:o + n].bitcast(F32), ALU.add, ALU.subtract)
                last.then_inc(norm_finished, 1)
        return norm_act, norm_pe, norm_dve, before

    eps_col = at("eps_col", 8600, 1)
    latp = [(0, 512, 0), (512, 512, 0)]
    norm1_act, norm1_pe, norm1_dve, norm1_before = norm(xt5, KT, latp + [(1024, 256, 1)], n_u, n_rs, lambda k, w: ada_1[:, 8 + k, w:w + 1],
                 lambda k, w: ada[:, k, w:w + 1], h_hi, h_lo)
    norm_cq_act, norm_cq_pe, norm_cq_dve, norm_cq_before = norm(cq, 2, latp, nb_u, nb_rs, lambda k, w: pcol[:, ROW_AT["q_a_norm"] + k:ROW_AT["q_a_norm"] + k + 1],
                   None, cq_hi, cq_lo)
    norm_kv_act, norm_kv_pe, norm_kv_dve, norm_kv_before = norm(ckv, 1, latp + [(1024, 256, 0)], nb_u, nb_rs,
                   lambda k, w: pcol[:, ROW_AT["kv_a_norm"]:ROW_AT["kv_a_norm"] + 1], None, ckv_hi, ckv_lo)
    norm2_act, norm2_pe, norm2_dve, norm2_before = norm(xt, KT, latp, n2_u, n2_rs, lambda k, w: ada_1[:, 32 + k, 0:1],
                 lambda k, w: ada[:, 24 + k, 0:1], h2_hi, h2_lo)
    norm_f_act, norm_f_pe, norm_f_dve, norm_f_before = norm(xt, KT, latp, n2_u, n2_rs, lambda k, w: pcol[:, ROW_AT["final_norm"] + k:ROW_AT["final_norm"] + k + 1],
                  None, None, None, out=xt)
    norm3_act, norm3_pe, norm3_dve, norm3_before = norm(xt, KT, latp, n2_u, n2_rs, lambda k, w: pcol[:, ROW_AT["norm_w_2"] + k:ROW_AT["norm_w_2"] + k + 1],
                 None, h2_hi, h2_lo)

    def gemm(pe, m, s, hi, lo, pieces, first=None):
        pe.wait_ge(w_split[s], m + 1)
        for k in range(KT):
            for n_pass, (w, a) in enumerate(((w_hi, hi), (w_hi, lo), (w_lo, hi))):
                for b, o, n in pieces:
                    last = nc.tensor.matmul(bank(b, n), w[:, s, k, :], a[:, k, o:o + n],
                                            start=k == 0 and n_pass == 0, stop=k == KT - 1 and n_pass == 2)
        last.then_inc(w_done[s], 1)

    two = lambda b: [(b, 0, 512), (b + 1, 512, 512)]
    three = lambda b: two(b) + [(b + 2, 1024, 256)]


    tmp_full, rope_done, rot_done = pair("tmp_full"), pair("rope_done"), pair("rot_done")
    v_full, v_turned, v_kept = pair("v_full"), pair("v_turned"), pair("v_kept")
    c_kept = sem("c_kept")
    q_staged, scores_ready, maxed, e_ready = sem("q_staged"), sem("scores_ready"), sem("maxed"), sem("e_ready")
    mixed, turned, pt_act = sem("mixed"), sem("turned"), sem("pt_act")
    o_kept = sem("o_kept")
    qb_staged, b_scores, b_maxed, b_e, b_turned = sem("qb_staged"), sem("b_scores"), sem("b_maxed"), sem("b_e"), sem("b_turned")
    b_pt0, b_pt1, b_pt2, b_av, b_kept = sem("b_pt0"), sem("b_pt1"), sem("b_pt2"), sem("b_av"), sem("b_kept")
    up_in, up_hi, up_split = sem("up_in"), sem("up_hi"), sem("up_split")
    kr_rot, vb_mm, vb_kept = sem("kr_rot"), sem("vb_mm"), sem("vb_kept")
    qb_mm, qb_tmp, qb_rot, qb_done, kb_mm, kb_kept = (sem(n) for n in ("qb_mm", "qb_tmp", "qb_rot", "qb_done", "kb_mm", "kb_kept"))
    cat_scaled, cat_turned, cat_taken, cat_rounded = sem("cat_scaled"), pair("cat_turned"), pair("cat_taken"), pair("cat_rounded")
    added = pair("added")
    gated, up_mixed, hid_rounded, hid_split = pair("gated"), pair("up_mixed"), pair("hid_rounded"), pair("hid_split")
    down_mm, down_added = pair("down_mm"), pair("down_added")

    w_in_v = t["w_in"].rearrange("l (k p) n -> p (l k) n", p=P)
    w_out_v = t["w_out"].rearrange("l (k p) n -> p (l k) n", p=P)
    w_ada_v = t["w_ada"].rearrange("l (k p) n -> p (l k) n", p=P)
    w_f_v = t["w_ffn_in"].rearrange("l (k p) n -> p (l k) n", p=P)
    w_fo_v = t["w_ffn_out"].rearrange("l (k p) n -> p (l k) n", p=P)
    w_in2_v = t["w_in_2"].rearrange("l (k p) n -> p (l k) n", p=P)
    w_br_v = t["w_branch"].rearrange("(k p) n -> p k n", p=P)
    w_out2_v = t["w_out_2"].rearrange("l (k p) n -> p (l k) n", p=P)
    x_rows, ctx_rows = t["x"].rearrange("b n d -> (b n) d"), t["ctx"].rearrange("b n d -> (b n) d")

    lam_summed, lam_exp, o_mm, att_ready = sem("lam_summed"), sem("lam_exp"), sem("o_mm"), sem("att_ready")
    S = lambda *names: [sem(n) for n in names]
    spilled2, ba_in, ba_mm, ba_hi, ba_split, gb_exp = S("spilled2", "ba_in", "ba_mm", "ba_hi", "ba_split", "gb_exp")
    ba_kept, g_abs, g_one = S("ba_kept", "g_abs", "g_one")
    staged, g_staged, gc_mm, gx_ready, e_done, kk_mm, kv_turned = S(
        "staged", "g_staged", "gc_mm", "gx_ready", "e_done", "kk_mm", "kv_turned")
    tt_first, t_turned, t_kept, ops_ready = S("tt_first", "t_turned", "t_kept", "ops_ready")
    uw_mm, od_mm, state_mm, state_new = S("uw_mm", "od_mm", "state_mm", "state_new")
    od_rooted, on_ready, on_turned, dn_kept = S("od_rooted", "on_ready", "on_turned", "dn_kept")
    win_in, zs_in, pt_even, pt_odd = S("win_in", "zs_in", "pt_even", "pt_odd")
    split_hi = sem("split_hi")
    xp_in, y_stored = pair("xp_in"), pair("y_stored")
    A_TILES = A_HEADS * NQ
    y_mm, y_masked, z_mm, tt_new, t_new, uw_kept, ws_mm, v_new_ready = (
        scores_ready, maxed, e_ready, mixed, turned, pt_act, o_mm, o_kept)
    B_TILES = B_HEADS * NQ
    s_mm, s_masked, s_exp, so_mm, so_kept, so_scaled, so_turned, s_turned = (
        b_scores, b_maxed, b_e, b_av, b_kept, b_pt0, b_pt1, b_pt2)
    qk_in, qk_mm, qk_rooted, qk_done, vs_in, vs_turned, vs_done = (
        qb_mm, qb_rot, qb_tmp, qb_done, kb_mm, kb_kept, qb_staged)
    CAT_PAIRS = KT // 2
    y_added, conv_full, conv_done, z_kept = (
        added, cat_turned, cat_taken, cat_rounded)
    FFN_PAIRS = FT // 2
    gate_kept, merged, merged_hi, y_kept = (
        gated, up_mixed, hid_rounded, hid_split)
    DOWNS = FT // 2 * KT // 2
    y_turned = down_added
    V_PAIRS = A_HEADS // 2
    d_squared, d_summed, d_rooted = (
        v_full, v_turned, v_kept)
    ROPES = 2 * A_HEADS // 2
    d_scaled = tmp_full
    zeroed, w_rounded, wd_rounded = sem("zeroed"), pair("w_rounded"), pair("wd_rounded")

    block = ctx.enter_context(nc.Block())

    @block.sync
    def _(sp):
        def chunk(m, s, src, n=P):
            sp.wait_ge(w_split[s], m)
            sp.dma_start(w_raw[:, s, :, 0:n], src).then_inc(w_loaded[s], 16)

        def chunk_down(n, s, src):
            sp.wait_ge(wd_split[s], n)
            sp.dma_start(wd_raw[:, s, :, :].rearrange("p k n -> p (k n)"), src).then_inc(wd_loaded[s], 16)

        sp.dma_start(consts[:, :, :], t["consts"].rearrange("p (m n) -> p m n", n=P)).then_inc(consts_in, 16)
        for s in range(2):
            sp.dma_start(x_tile[:, s, :], x_rows[s * P:(s + 1) * P, :]).then_inc(x_in[s], 16)
        for name, n in ROWS:
            src = t[name]
            src = src.rearrange("(a n) -> a n", n=P) if len(src.shape) == 1 else src.rearrange("l (a n) -> (l a) n", n=P) \
                if len(src.shape) == 2 else src.rearrange("l a n -> (l a) n")
            sp.dma_start(param_rows[ROW_AT[name]:ROW_AT[name] + n, 0, :], src).then_inc(params_in, 16)
        sp.dma_start(param_rows[0:48, 1, :], t["conv_w_2"].rearrange("l j o (f n) -> (l j o f) n", n=P)).then_inc(params_in, 16)
        sp.dma_start(lam_in[:, :, :, :].rearrange("p a b n -> p (a b n)"),
                     t["diff_lambda"].rearrange("l a n -> l (a n)").broadcast_to([P, 256])).then_inc(small_in, 16)
        sp.dma_start(alog[:, :], t["dn_a_log_2"].broadcast_to([P, 4])).then_inc(small_in, 16)
        sp.dma_start(dtb[:, :], t["dn_dt_bias_2"].broadcast_to([P, 4])).then_inc(small_in, 16)
        for s in range(4):
            sp.dma_start(ada_w[:, s, :, :], w_ada_v[:, :, s * BANK:(s + 1) * BANK]).then_inc((*ada_in, *ada_in_2)[s], 16)
        with sp.Fori(1, 4) as i:
            for s in range(2):
                sp.wait_ge(x_turned[s], i)
                sp.dma_start(x_tile[:, s, :], x_rows[ds(i * 256 + s * P, P), :]).then_inc(x_in[s], 16)
        for s in range(2):
            sp.wait_ge(x_turned[s], 4)
            sp.dma_start(x_tile[:, s, :], ctx_rows[s * P:(s + 1) * P, :]).then_inc(x_in[s], 16)
        sp.wait_ge(phase_end, at_end["input"])
        sp.dma_start(x_scratch, xt5[:, :, 0:LAT]).then_inc(spilled, 16)
        for m, c in ((M_Q, 0), (M_K, 512)):
            for j in range(2):
                for s in range(2):
                    chunk(m + j, s, w_in_v[:, :, c + (2 * j + s) * P:c + (2 * j + s + 1) * P])
            if m == M_Q:
                sp.wait_ge(phase_end, at_end["norm1"])
                sp.wait_ge(spilled, 16)
                sp.dma_start(cos_a[:, :], t["trig_a"][:, 0, :]).then_inc(trig_in, 16)
                sp.dma_start(sin_a[:, :], t["trig_a"][:, 1, :]).then_inc(trig_in, 16)
        with sp.Fori(0, 2) as i:
            for s in range(2):
                chunk(M_V + i, s, w_in_v[:, :, ds(i * 256 + 1024 + s * P, P)])
        for s in range(2):
            chunk(M_C, s, w_in_v[:, :, 1536 + s * P:1536 + (s + 1) * P])
        chunk(M_C + 1, 0, w_in_v[:, :, 1792:1920])
        chunk(M_C + 1, 1, w_in_v[:, :, 1856:1952], BD)
        for s in range(2):
            chunk(M_OUT, s, w_out_v[:, :, s * P:(s + 1) * P])
        sp.wait_ge(phase_end, at_end["proj_v"])
        with sp.Fori(0, A_HEADS) as h:
            for qt in range(NQ):
                s = qt % 2
                sp.wait_ge(ada_used[s], h * 4 + qt // 2 + 2)
                sp.dma_start(ada_w2[:, s, :, :], w_ada_v[:, :, ds(h * 1024 + 2048 + qt * P, P)]).then_inc(ada_in[s], 16)
        sp.wait_ge(phase_end, at_end["attn_a"])
        sp.dma_start(qup_raw[:, :, :], t["w_q_up"].rearrange("l (k p) n -> p (l k) n", p=P)).then_inc(up_in, 16)
        sp.dma_start(kvup_raw[:, :], t["w_kv_up"].rearrange("l p n -> p (l n)")).then_inc(up_in, 16)
        sp.dma_start(cos_b[:, :], t["trig_b"][:, 0, :]).then_inc(up_in, 16)
        sp.dma_start(sin_b[:, :], t["trig_b"][:, 1, :]).then_inc(up_in, 16)
        sp.wait_ge(phase_end, at_end["attn_b1"])
        sp.dma_start(xt[:, :, :], x_scratch).then_inc(xt_back, 16)
        with sp.Fori(1, 4) as i:
            for s in range(2):
                chunk(M_OUT + i, s, w_out_v[:, :, ds(i * 256 + s * P, P)])
        for s in range(2):
            chunk(M_FFN, s, w_f_v[:, :, s * P:(s + 1) * P])
        for s in range(2):
            chunk(M_FFN + 1, s, w_f_v[:, :, FFN + s * P:FFN + (s + 1) * P])
        sp.wait_ge(phase_end, at_end["norm2"])
        for s in range(2):
            chunk_down(0, s, w_fo_v[:, s, :])
        with sp.Fori(1, FT // 2) as i:
            for half in range(2):
                for s in range(2):
                    chunk(M_FFN + half + i * 2, s, w_f_v[:, :, ds(i * 256 + half * FFN + s * P, P)])
            for s in range(2):
                chunk_down(i, s, w_fo_v[:, ds(i * 2 + s, 1), :].rearrange("p k n -> p (k n)"))
        for s in range(2):
            chunk(M_DN, s, w_in2_v[:, :, s * P:(s + 1) * P])
        sp.wait_ge(norm_finished, norm_f_before + 2)
        sp.dma_start(x_scratch, xt[:, :, :]).then_inc(spilled2, 16)
        sp.dma_start(w_ba[:, :, :], w_in2_v[:, :, C_B:C_B + 8]).then_inc(ba_in, 16)
        with sp.Fori(1, 8) as i:
            for s in range(2):
                chunk(i + M_DN, s, w_in2_v[:, :, ds(i * 256 + s * P, P)])
        for s in range(2):
            chunk(M_SWA, s, w_in2_v[:, :, C_SQ + s * 512:C_SQ + s * 512 + P])
        sp.wait_ge(phase_end, at_end["delta"])
        sp.dma_start(cos_s[:, :], t["trig_s"][:, 0, :]).then_inc(win_in, 16)
        sp.dma_start(sin_s[:, :], t["trig_s"][:, 1, :]).then_inc(win_in, 16)
        sp.dma_start(mask[:, :], t["window_mask"]).then_inc(win_in, 16)
        for c in range(2, 10):
            chunk(M_SWA + c // 2, c % 2, w_in2_v[:, :, SWA_COLS[c]:SWA_COLS[c] + P])
        with sp.Fori(1, DN) as h:
            for c in range(10):
                chunk(h * 5 + M_SWA + c // 2, c % 2, w_in2_v[:, :, ds(h * P + SWA_COLS[c], P)])
        with sp.Fori(0, 8) as i:
            for s in range(2):
                chunk(i + M_GATE, s, w_in2_v[:, :, ds(i * 256 + C_G + s * P, P)])
        with sp.Fori(0, 4) as i:
            for s in range(2):
                chunk(i + M_BRANCH, s, w_br_v[:, :, ds(i * 256 + s * P, P)])
        sp.wait_ge(phase_end, at_end["branch"])
        sp.wait_ge(spilled2, 16)
        with sp.Fori(0, 4) as i:
            for s in range(2):
                chunk(i + M_OUT2, s, w_out2_v[:, :, ds(i * 256 + s * P, P)])
                sp.wait_ge(y_added[s], i + CAT_PAIRS + FREE)
                sp.dma_start(x_piece[:, s, :], x_scratch[:, ds(i * 2 + s, 1), :].rearrange("p k n -> p (k n)")).then_inc(xp_in[s], 16)

    @block.gpsimd
    def _(pool):
        for freed in (*rope_done, *v_kept, kv_turned, ops_ready, dn_kept, state_new, *y_stored, o_mm, b_kept, e_ready,
                      o_kept, b_e, *added):
            pool.sem_inc(freed, FREE)
        nc.gpsimd.memset(zero[:, :], 0.0).then_inc(zeroed, 1)
        pool.wait_ge(zeroed, 1)

        def split_chunk(m, s, raw, hi, lo, loaded, used, rounded, split):
            flat = lambda w: w[:, s, :, :].rearrange("p k n -> p (k n)")
            pool.wait_ge(loaded[s], m * 16 + 16)
            pool.wait_ge(used[s], m)
            nc.gpsimd.tensor_tensor(flat(hi), flat(raw), zero[:, 0:1].broadcast_to([P, KT * P]), ALU.add)\
                .then_inc(rounded[s], 1)
            pool.wait_ge(rounded[s], m + 1)
            nc.gpsimd.tensor_tensor(flat(lo), flat(raw), flat(hi).bitcast(F32), ALU.subtract)\
                .then_inc(split[s], 1)

        def split(m):
            for s in range(2):
                split_chunk(m, s, w_raw, w_hi, w_lo, w_loaded, w_done, w_rounded, w_split)

        def split_down(n):
            for s in range(2):
                split_chunk(n, s, wd_raw, wd_hi, wd_lo, wd_loaded, wd_done, wd_rounded, wd_split)

        split(0)
        with pool.Fori(1, M_FFN + 2) as m:
            split(m)
        split_down(0)
        with pool.Fori(1, FT // 2) as i:
            split(i * 2 + M_FFN)
            split(i * 2 + M_FFN + 1)
            split_down(i)
        with pool.Fori(M_DN, PAIRS) as m:
            split(m)

    @block.scalar
    def _(act):
        act.wait_ge(lam_summed, 1)
        nc.scalar.activation(lam_e[:, :], lam_e[:, :], ACT.Exp).then_inc(lam_exp, 1)
        act.wait_ge(params_turned, 2)
        nc.scalar.activation(pcol[:, 0:N_ROWS], bank(6, N_ROWS), ACT.Copy)
        nc.scalar.activation(pcol[:, CONV_AT:CONV_AT + 48], bank(7, 48), ACT.Copy).then_inc(pcol_ready, 1)
        act.wait_ge(pcol_ready, 1)
        nc.scalar.activation(silu_c[:, :, :].rearrange("p k w -> p w k"),
                             pcol[:, 48:64].rearrange("p (w k) -> p w k", w=2), ACT.Silu).then_inc(silu_ready, 1)
        with act.Fori(0, 5) as i:
            for s in range(2):
                act.wait_ge(x_turned[s], i + 1)
                nc.scalar.activation(xt5[:, 0:4, ds(i * 256 + s * P, P)],
                                     bank(2 * s).rearrange("p (k n) -> p k n", k=4), ACT.Copy).then_inc(xt_act[s], 1)
        meet(act, "input")
        norm1_act(act)
        meet(act, "norm1")
        act.wait_ge(spilled, 16)
        for m, keys, n0 in ((M_Q, False, 0), (M_K, True, 2)):
            with act.Fori(0, 2) as i:
                for s in range(2):
                    act.wait_ge(w_done[s], i + m + 1)
                    act.wait_ge(rope_done[s], i + n0 + FREE)
                    if keys:
                        nc.scalar.activation(k_a[:, ds(i * 2 + s, 1), LAT:TOK], bank(3 * s + 2, CTX).rearrange("p (k n) -> p k n", k=1), ACT.Copy)
                    nc.scalar.activation(rope_tmp[:, s, :], bank(3 * s, LAT), ACT.Copy).then_inc(tmp_full[s], 1)
        meet(act, "proj_q")
        with act.Fori(0, 2) as i:
            for s in range(2):
                act.wait_ge(w_done[s], i + M_V + 1)
                nc.scalar.activation(v_tmp[:, s, :], bank(3 * s, TOK), ACT.Copy).then_inc(v_full[s], 1)
        meet(act, "proj_v")
        for s in range(2):
            act.wait_ge(w_done[s], M_C + 1)
            nc.scalar.activation(cq[:, s, :], bank(3 * s, LAT), ACT.Copy).then_inc(c_kept, 1)
        for s, dst in enumerate((ckv[:, :], kr[0:BD, :])):
            act.wait_ge(w_done[s], M_C + 2)
            nc.scalar.activation(dst, ps[0:BD if s else P, 3 * s * BANK:3 * s * BANK + TOK], ACT.Copy)
        meet(act, "proj_c")
        def square_output(h, qt):
            act.wait_ge(o_kept, h * NQ + qt + 1 + FREE)
            nc.scalar.activation(sq_junk[:, qt % 2, :], att[:, qt, ds(h * P, P)], ACT.Square, accum_out=st_a[:, ds(h * NQ + qt, 1)])

        with act.Fori(0, A_HEADS) as h:
            def take_transposes(qt):
                act.wait_ge(turned, h * NQ + qt + 1)
                nc.scalar.activation(pt[:, :], ps[:, 5 * BANK:5 * BANK + TOK], ACT.Copy).then_inc(pt_act, 1)

            for qt in range(NQ):
                if qt:
                    take_transposes(qt - 1)
                act.wait_ge(maxed, h * NQ + qt + 1)
                for w in range(2):
                    last = nc.scalar.activation(e_a[:, qt % 2, w, :], ps[:, w * TOK:(w + 1) * TOK], ACT.Exp,
                                                bias=st_m[:, qt % 2, w:w + 1], scale=SCALE_A,
                                                accum_out=st_s[:, qt % 2, w:w + 1])
                last.then_inc(e_ready, 1)
                if qt >= 2:
                    square_output(h, qt - 2)
            take_transposes(NQ - 1)
            for qt in range(NQ - 2, NQ):
                square_output(h, qt)
        meet(act, "attn_a")
        norm_cq_act(act)
        act.wait_ge(norm_finished, norm_cq_before + 2)
        norm_kv_act(act)
        act.wait_ge(norm_finished, norm_kv_before + 3)
        act.wait_ge(up_in, 64)
        nc.scalar.activation(qup_hi[:, :, :], qup_raw[:, :, :], ACT.Copy)
        nc.scalar.activation(kvup_hi[:, :], kvup_raw[:, :], ACT.Copy).then_inc(up_hi, 1)
        meet(act, "prep_b")
        for g in range(2):
            for h in range(4):
                n = g * 4 + h
                act.wait_ge(qb_mm, n + 1)
                if n:
                    act.wait_ge(qb_done, n)
                nc.scalar.activation(tmp_b[0:BD, h % 2, :], ps[0:BD, 0:LAT], ACT.Copy).then_inc(qb_tmp, 1)
                act.wait_ge(kb_mm, n + 1)
                nc.scalar.activation(k_b[0:NOPE, h, :], ps[0:NOPE, 4 * BANK:4 * BANK + TOK], ACT.Copy).then_inc(kb_kept, 1)
            meet(act, f"heads_b{g}")
            with act.Fori(0, 4) as h:
                act.wait_ge(b_e, h * NQ + g * 32 + FREE)
                nc.scalar.activation(qs_b[0:BD, :], q_b[0:BD, ds(h, 1), :].rearrange("p k n -> p (k n)"), ACT.Copy)\
                    .then_inc(qb_staged, 1)

                def take_transposes(qt):
                    for j, (k0, k1, t0) in enumerate(((1024, 1280, (2 + 3 * (qt % 2)) * BANK + 256),
                                                      (0, 512, 6 * BANK), (512, 1024, 7 * BANK))):
                        act.wait_ge(b_turned, h * 24 + g * 96 + qt * 3 + j + 1)
                        nc.scalar.activation(pt_b[:, k0:k1], ps[:, t0:t0 + k1 - k0], ACT.Copy).then_inc((b_pt2, b_pt0, b_pt1)[j], 1)

                for qt in range(NQ):
                    n = h * NQ + g * 32 + qt
                    b = 3 * (qt % 2)
                    if qt:
                        take_transposes(qt - 1)
                    act.wait_ge(b_maxed, n + 1)
                    nc.scalar.activation(e_b[:, qt % 2, :], bank(b, TOK), ACT.Exp, bias=st_b[:, qt % 2, 0:1],
                                         scale=SCALE_B, accum_out=st_b[:, qt % 2, 1:2]).then_inc(b_e, 1)
                take_transposes(NQ - 1)
            meet(act, f"attn_b{g}")
        act_link(nc.scalar.activation(st_a[:, :], st_a[:, :], ACT.Ln, bias=eps_col[:, 0:1], scale=1.0 / P))
        nc.scalar.activation(st_a[:, :], st_a[:, :], ACT.Exp, scale=-0.5).then_inc(cat_scaled, 1)
        for f in range(KT):
            s = f % 2
            act.wait_ge(cat_taken[s], f // 2 + 1)
            nc.scalar.activation(cat_hi[:, f, :], cat_t[:, s, :], ACT.Copy).then_inc(cat_rounded[s], 1)
        meet(act, "cat")
        meet(act, "out1")
        norm2_act(act)
        meet(act, "norm2")
        def gate_and_round(i):
            for s in range(2):
                act.wait_ge(w_done[s], i * 2 + M_FFN + 1)
                act.wait_ge(up_mixed[s], i)
                nc.scalar.activation(gate_s[:, s, :], bank(2 * s, LAT), ACT.Silu).then_inc(gated[s], 1)
            for s in range(2):
                act.wait_ge(wd_done[1], i)
                act.wait_ge(up_mixed[s], i + 1)
                nc.scalar.activation(hid_hi[:, s, :], hid[:, s, :], ACT.Copy).then_inc(hid_rounded[s], 1)

        gate_and_round(0)
        with act.Fori(1, FT // 2) as i:
            gate_and_round(i)
        meet(act, "ffn")
        norm_f_act(act)
        act.wait_ge(norm_finished, norm_f_before + 2)
        norm3_act(act)
        meet(act, "norm3")
        act.wait_ge(spilled2, 16)
        with act.Fori(0, 6) as i:
            for s in range(2):
                act.wait_ge(w_done[s], i + M_DN + 1)
                act.wait_ge(conv_done[s], i + CAT_PAIRS)
                nc.scalar.activation(conv_in[:, s, PAD:PAD + LAT], bank(2 * s, LAT), ACT.Copy).then_inc(conv_full[s], 1)
            for s in range(2):
                act.wait_ge(conv_done[s], i + 1 + CAT_PAIRS)
                y = qkv[:, ds(i * 2 + s, 1), :].rearrange("p k n -> p (k n)")
                nc.scalar.activation(y, y, ACT.Silu)
        with act.Fori(0, 2) as i:
            for s in range(2):
                act.wait_ge(w_done[s], i + M_DN + 7)
                nc.scalar.activation(dn[:, ds(i * 2 + s, 1), :].rearrange("p k n -> p (k n)"), bank(2 * s, LAT), ACT.Silu)\
                    .then_inc(z_kept[s], 1)
        act.wait_ge(ba_in, 16)
        nc.scalar.activation(w_ba_hi[:, :, :], w_ba[:, :, :], ACT.Copy).then_inc(ba_hi, 1)
        meet(act, "dn_proj")
        def square_pair(i):
            for s in range(2):
                act.wait_ge(d_summed[s], i + V_PAIRS)
                nc.scalar.activation(sq_d[:, s, :], qkv[:, i * 2 + s, :], ACT.Square).then_inc(d_squared[s], 1)

        square_pair(0)
        for i in range(4):
            for s in range(2):
                act.wait_ge(d_summed[s], i + 1 + V_PAIRS)
                act.wait_ge(d_scaled[s], i + ROPES)
                act_did(nc.scalar.activation(rs_d[:, s, :], bank(2 * s, LAT), ACT.Ln, bias=eps_col[:, 0:1], scale=float(P)))
            if i < 3:
                square_pair(i + 1)
            act.wait_ge(act_step, act_count())
            for s in range(2):
                nc.scalar.activation(rs_d[:, s, :], rs_d[:, s, :], ACT.Exp, scale=-0.5).then_inc(d_rooted[s], 1)
        act.wait_ge(ba_kept, 1)
        nc.scalar.activation(beta[:, :, :], gb[:, :, 0:4], ACT.Exp, scale=-1.0)
        nc.scalar.activation(ealog[:, :], alog[:, :], ACT.Exp)
        act.wait_ge(g_abs, 1)
        nc.scalar.activation(g_e[:, :, :], g_e[:, :, :], ACT.Exp, scale=-1.0).then_inc(gb_exp, 1)
        act.wait_ge(g_one, 1)
        nc.scalar.activation(g_e[:, :, :], g_e[:, :, :], ACT.Ln).then_inc(gb_exp, 1)
        meet(act, "dn_l2")
        flat = lambda a: a[:, :, :].rearrange("p h n -> p (h n)")

        def root_output(c):
            act.wait_ge(od_mm, c)
            for h in range(DN):
                last = nc.scalar.activation(u_s[:, h, :], bank(6)[:, h * P:(h + 1) * P], ACT.Square, accum_out=o_ss[:, h:h + 1])
            act_link(last)
            act_link(nc.scalar.activation(o_ss[:, :], o_ss[:, :], ACT.Ln, bias=eps_col[:, 0:1], scale=1.0 / P))
            nc.scalar.activation(o_ss[:, :], o_ss[:, :], ACT.Exp, scale=-0.5).then_inc(od_rooted, 1)

        def delta_chunk(c, first):
            act.wait_ge(kv_turned, c + FREE)
            act.wait_ge(ops_ready, c + FREE)
            nc.scalar.activation(st_qkv[:, :, :], qkv[:, :, ds(c * P, P)], ACT.Copy).then_inc(staged, 1)
            if not first:
                root_output(c)
            act.wait_ge(gx_ready, c + 1)
            nc.scalar.activation(flat(eg), bank(0), ACT.Exp)
            nc.scalar.activation(e_gc[:, :], g_c[:, :], ACT.Exp)
            nc.scalar.activation(tail[:, :], tail[:, :], ACT.Exp)
            nc.scalar.activation(flat(dc), flat(gx), ACT.Exp).then_inc(e_done, 1)
            act.wait_ge(t_turned, c + 1)
            nc.scalar.activation(flat(tm), bank(7), ACT.Copy).then_inc(t_kept, 1)
            act.wait_ge(uw_mm, c + 1)
            nc.scalar.activation(flat(u_s), bank(3), ACT.Copy)
            nc.scalar.activation(flat(w_t), bank(4), ACT.Copy).then_inc(uw_kept, 1)

        delta_chunk(0, True)
        with act.Fori(1, NQ) as c:
            act_enter(c - 1, 2)
            delta_chunk(c, False)
            act_leave(2, NQ - 1)
        root_output(NQ)
        meet(act, "delta")
        with act.Fori(0, DN) as h:
            act_enter(h, 6)

            def root(j):
                act.wait_ge(qk_mm, h * 6 + j + 1 + B_HEADS)
                act.wait_ge(qk_done, h * 6 + j + B_HEADS)
                act_link(nc.scalar.activation(rs_s[:, :], bank(4, LAT), ACT.Ln, bias=eps_col[:, 0:1]))
                nc.scalar.activation(rs_s[:, :], rs_s[:, :], ACT.Exp, scale=-0.5).then_inc(qk_rooted, 1)

            act.wait_ge(so_kept, h * NQ + B_TILES + FREE)
            for c in range(10):
                s = c % 2
                act.wait_ge(w_done[s], h * 5 + M_SWA + c // 2 + 1)
                if c < 6:
                    if c >= 2:
                        act.wait_ge(qk_done, h * 6 + c - 1 + B_HEADS)
                    norm_w = ROW_AT["q_norm_w_2"] + c
                    nc.scalar.activation(tmp_s[:, s, :], bank(2 * s, LAT), ACT.Copy, scale=pcol[:, norm_w:norm_w + 1])
                    nc.scalar.activation(sq_s[:, s, :], bank(2 * s, LAT), ACT.Square).then_inc(qk_in, 1)
                elif c < 9:
                    if c < 8:
                        act.wait_ge(qk_done, h * 6 + c - 1 + B_HEADS)
                    else:
                        act.wait_ge(vs_turned, h * 3 + 1 + B_HEADS)
                    nc.scalar.activation(tmp_s[:, s, :], bank(2 * s, LAT), ACT.Copy).then_inc(vs_in, 1)
                else:
                    nc.scalar.activation(z_s[:, :], bank(2 * s, LAT), ACT.Silu).then_inc(zs_in, 1)
                if 1 <= c <= 6:
                    root(c - 1)
            act.wait_ge(vs_done, h * 3 + 3 + B_HEADS)
            for n in range(NQ):
                s = n % 2
                width = len(window_tiles(n)) * P
                act.wait_ge(s_masked, h * NQ + n + 1 + B_TILES)
                nc.scalar.activation(s_m[:, s, 0:width], s_m[:, s, 0:width], ACT.Exp, bias=st_w[:, s, 4:5],
                                     accum_out=st_w[:, s, 5:6]).then_inc(s_exp, 1)
                for b in range(1, BATCHES[n], 2):
                    act.wait_ge(s_turned, h * ALL_BATCHES + sum(BATCHES[:n]) + b + 1 + B_TILES)
                    w = min(BANK, width - b * BANK)
                    nc.scalar.activation(pt_s[:, 1, 0:w], bank(5, w), ACT.Copy).then_inc(pt_odd, 1)
            act_leave(6, DN)
        meet(act, "swa")
        with act.Fori(0, 8) as i:
            for s in range(2):
                act.wait_ge(w_done[s], i + M_GATE + 1)
                nc.scalar.activation(gates[:, ds(i * 2 + s, 1), :].rearrange("p k n -> p (k n)"), bank(2 * s, LAT), ACT.Sigmoid)\
                    .then_inc(gate_kept[s], 1)
        meet(act, "gates")
        nc.scalar.activation(dn_hi[:, :, :], dn[:, :, :], ACT.Copy).then_inc(split_hi, 1)
        nc.scalar.activation(sw_hi[:, :, :], sw[:, :, :], ACT.Copy).then_inc(split_hi, 1)
        meet(act, "split2")
        with act.Fori(0, 4) as i:
            for s in range(2):
                act.wait_ge(merged[s], i + 1 + FFN_PAIRS)
                nc.scalar.activation(m_hi[:, ds(i * 2 + s, 1), :].rearrange("p k n -> p (k n)"), m_t[:, s, :], ACT.Copy)\
                    .then_inc(merged_hi[s], 1)
        meet(act, "branch")
        out_v = t["out"].rearrange("b (q p) n -> p (b q) n", p=P)
        with act.Fori(0, 4) as i:
            for s in range(2):
                act.wait_ge(y_turned[s], i + 1 + DOWNS)
                act.wait_ge(y_stored[s], i * 16 + FREE)
                nc.scalar.activation(y_t[:, s, :, :].rearrange("p q n -> p (q n)"), bank(4 + 2 * s, LAT), ACT.Copy)\
                    .then_inc(y_kept[s], 1)
                act.wait_ge(y_kept[s], i + 1 + FFN_PAIRS)
                act.dma_start(out_v[:, :, ds(i * 256 + s * P, P)], y_t[:, s, :, :]).then_inc(y_stored[s], 16)
        for s in range(2):
            act.wait_ge(y_stored[s], 64 + FREE)

    @block.vector
    def _(dve):
        nc.vector.memset(eps_col[:, :], EPS)
        dve.wait_ge(small_in, 48)
        dve_link(nc.vector.tensor_tensor(lam_prod[:, :, :], lam_in[:, :, 0, :], lam_in[:, :, 1, :], ALU.mult))
        nc.vector.tensor_reduce(lam_e[:, :], lam_prod[:, :, :], AX_X, ALU.add).then_inc(lam_summed, 1)
        with dve.Fori(0, 5) as i:
            for s in range(2):
                dve.wait_ge(x_turned[s], i + 1)
                nc.vector.tensor_copy(xt5[:, 4:8, ds(i * 256 + s * P, P)],
                                      bank(2 * s + 1).rearrange("p (k n) -> p k n", k=4)).then_inc(xt_dve[s], 1)
        dve.wait_ge(ada_mm, 1)
        dve.wait_ge(pcol_ready, 1)

        def add_ada_bias(m0, m1, products):
            dve_link(nc.vector.tensor_tensor(ada[:, m0:m1, :], products.rearrange("p (m w) -> p m w", w=2),
                                             pcol[:, m0:m1].rearrange("p (m w) -> p m w", w=1).broadcast_to([P, m1 - m0, 2]),
                                             ALU.add))
            nc.vector.tensor_scalar(ada_1[:, m0:m1, :], ada[:, m0:m1, :], 1.0, None, ALU.add)

        add_ada_bias(0, 16, bank(6, 32))
        nc.vector.tensor_scalar(subln[:, :], pcol[:, ROW_AT["diff_subln"]:ROW_AT["diff_subln"] + 1], 1.0 - LAM_INIT, None, ALU.mult)
        meet(dve, "input")
        norm1_dve(dve)
        meet(dve, "norm1")
        dve.wait_ge(trig_in, 32)
        for m, dst, n0 in ((M_Q, q_a, 0), (M_K, k_a, 2)):
            with dve.Fori(0, 2) as i:
                dve_enter(i, 4)
                for s in range(2):
                    out = dst[:, ds(i * 2 + s, 1), 0:LAT].rearrange("p k n -> p (k n)")
                    dve.wait_ge(tmp_full[s], i + n0 + 1)
                    dve_link(nc.vector.tensor_tensor(out, rope_tmp[:, s, :], cos_a[:, :], ALU.mult))
                    dve.wait_ge(rot_done[s], i + n0 + 1)
                    dve_link(nc.vector.tensor_tensor(rope_tmp[:, s, :], bank(3 * s, LAT), sin_a[:, :], ALU.mult))
                    nc.vector.tensor_tensor(out, out, rope_tmp[:, s, :], ALU.add).then_inc(rope_done[s], 1)
                dve_leave(4, 2)
        meet(dve, "proj_q")
        with dve.Fori(0, 2) as i:
            for s in range(2):
                dve.wait_ge(v_turned[s], i + 1)
                nc.vector.tensor_copy(v_a[:, :, ds(i * 256 + s * P, P)],
                                      bank(3 * s, TOK).rearrange("p (t n) -> p t n", n=P)).then_inc(v_kept[s], 1)
        meet(dve, "proj_v")
        dve.wait_ge(lam_exp, 1)
        nc.vector.scalar_tensor_tensor(minus_lam[:, :], lam_e[:, 1:2], -LAM_INIT, lam_e[:, 0:1], ALU.add, ALU.subtract)
        meet(dve, "proj_c")
        nc.vector.memset(qs[64:128, 0, :], 0.0)
        nc.vector.memset(qs[0:64, 1, :], 0.0)
        with dve.Fori(0, A_HEADS) as h:
            dve_enter(h, 4 * NQ)
            dve.wait_ge(o_mm, h * NQ + FREE)
            for w in range(2):
                a, b = 64 * w, 64 * w + 64
                last = nc.vector.tensor_copy(qs[a:b, w, :], q_a[a:b, ds(h, 1), :].rearrange("p k n -> p (k n)"))
            last.then_inc(q_staged, 1)

            def take_output(qt):
                dve.wait_ge(o_mm, h * NQ + qt + 1 + FREE)
                nc.vector.tensor_scalar(att[:, qt, ds(h * P, P)], ps[:, 7 * BANK + 256:7 * BANK + 384], st_r[:, qt % 2, 0:1],
                                        None, ALU.mult).then_inc(o_kept, 1)

            for qt in range(NQ):
                s, n = qt % 2, h * NQ + qt
                for w in range(2):
                    dve.wait_ge(scores_ready, h * 2 * NQ + 2 * qt + w + 1)
                    dve_link(nc.vector.tensor_reduce(st_x[:, s, w:w + 1], ps[:, w * TOK:(w + 1) * TOK], AX_X, ALU.max))
                nc.vector.tensor_scalar(st_m[:, s, :], st_x[:, s, :], -SCALE_A, None, ALU.mult).then_inc(maxed, 1)
                dve.wait_ge(e_ready, n + 1 + FREE)
                dve_link(nc.vector.reciprocal(st_r[:, s, :], st_s[:, s, :]))
                dve_link(nc.vector.tensor_scalar(st_c[:, s, :], st_r[:, s, 1:2], st_s[:, s, 0:1], minus_lam[:, 0:1], ALU.mult, ALU.mult))
                nc.vector.scalar_tensor_tensor(prob[:, s, :], e_a[:, s, 1, :], st_c[:, s, :], e_a[:, s, 0, :],
                                               ALU.mult, ALU.add).then_inc(mixed, 1)
                if qt:
                    take_output(qt - 1)
            take_output(NQ - 1)
            dve_leave(4 * NQ, A_HEADS)
        meet(dve, "attn_a")
        add_ada_bias(16, 48, ps[:, 7 * BANK + 384:7 * BANK + 448])
        norm_cq_dve(dve)
        norm_kv_dve(dve)
        dve.wait_ge(up_in, 64)
        dve.wait_ge(up_hi, 1)
        nc.vector.tensor_tensor(qup_lo[:, :, :], qup_raw[:, :, :], qup_hi[:, :, :].bitcast(F32), ALU.subtract)
        nc.vector.tensor_tensor(kvup_lo[:, :], kvup_raw[:, :], kvup_hi[:, :].bitcast(F32), ALU.subtract).then_inc(up_split, 1)
        dve.wait_ge(kr_rot, 1)
        r = slice(NOPE, BD)
        dve_did(nc.vector.tensor_tensor(tmp_b[r, 0, :], ps[r, 4 * BANK:6 * BANK], sin_b[r, :], ALU.mult))
        dve_link(nc.vector.tensor_tensor(kr[r, 0:LAT], kr[r, 0:LAT], cos_b[r, :], ALU.mult))
        dve_link(nc.vector.tensor_tensor(kr[r, 0:LAT], kr[r, 0:LAT], tmp_b[r, 0, :], ALU.add))
        for kt in range(NKEY):
            dve.wait_ge(vb_mm, kt + 1)
            nc.vector.tensor_copy(v_b[:, kt, :], bank(kt % 2)).then_inc(vb_kept, 1)
        meet(dve, "prep_b")
        for g in range(2):
            for h in range(4):
                n = g * 4 + h
                nc.vector.tensor_copy(k_b[r, h, :], kr[r, :])
                dve.wait_ge(qb_tmp, n + 1)
                dve_link(nc.vector.tensor_tensor(q_b[0:BD, h, :], tmp_b[0:BD, h % 2, :], cos_b[0:BD, :], ALU.mult))
                dve.wait_ge(qb_rot, n + 1)
                dve_link(nc.vector.tensor_tensor(tmp_b[0:BD, h % 2, :], ps[0:BD, 2 * BANK:4 * BANK], sin_b[0:BD, :], ALU.mult))
                nc.vector.tensor_tensor(q_b[0:BD, h, :], q_b[0:BD, h, :], tmp_b[0:BD, h % 2, :], ALU.add).then_inc(qb_done, 1)
            meet(dve, f"heads_b{g}")
            with dve.Fori(0, 4) as h:
                dve_enter(h, 2 * NQ)

                def take_output(qt):
                    s = qt % 2
                    dve.wait_ge(b_e, h * NQ + g * 32 + qt + 1 + FREE)
                    dve_link(nc.vector.reciprocal(st_b[:, s, 3:4], st_b[:, s, 1:2]))
                    dve.wait_ge(b_av, h * NQ + g * 32 + qt + 1)
                    t0 = (2 + 3 * s) * BANK
                    nc.vector.tensor_scalar(att[:, qt, ds(h * 64 + 512 + g * 256, 64)], ps[:, t0:t0 + 64], st_b[:, s, 3:4], None, ALU.mult)\
                        .then_inc(b_kept, 1)

                for qt in range(NQ):
                    s, n = qt % 2, h * NQ + g * 32 + qt
                    dve.wait_ge(b_scores, n + 1)
                    dve_link(nc.vector.tensor_reduce(st_b[:, s, 2:3], bank(3 * s, TOK), AX_X, ALU.max))
                    nc.vector.tensor_scalar(st_b[:, s, 0:1], st_b[:, s, 2:3], -SCALE_B, None, ALU.mult).then_inc(b_maxed, 1)
                    if qt:
                        take_output(qt - 1)
                take_output(NQ - 1)
                dve_leave(2 * NQ, 4)
            meet(dve, f"attn_b{g}")
        dve.wait_ge(cat_scaled, 1)
        for qt in range(NQ):
            a = att[:, qt, 0:512].rearrange("p (h n) -> p h n", h=A_HEADS)
            last = nc.vector.tensor_tensor(a, a, st_a[:, :].rearrange("p (h q w) -> p h q w", q=NQ, w=1)[:, :, qt, :]
                                           .broadcast_to([P, A_HEADS, P]), ALU.mult)
        last.then_inc(att_ready, 1)
        for f in range(KT):
            s = f % 2
            dve.wait_ge(cat_turned[s], f // 2 + 1)
            if f < 4:
                nc.vector.tensor_scalar(cat_t[:, s, :], bank(2 * s, LAT), subln[:, 0:1], None, ALU.mult).then_inc(cat_taken[s], 1)
            else:
                nc.vector.tensor_copy(cat_t[:, s, :], bank(2 * s, LAT)).then_inc(cat_taken[s], 1)
            dve.wait_ge(cat_rounded[s], f // 2 + 1)
            nc.vector.tensor_tensor(cat_lo[:, f, :], cat_t[:, s, :], cat_hi[:, f, :].bitcast(F32), ALU.subtract)
        meet(dve, "cat")
        dve.wait_ge(xt_back, 16)
        with dve.Fori(0, 4) as i:
            for s in range(2):
                dve.wait_ge(w_done[s], i + M_OUT + 1)
                x = xt[:, ds(i * 2 + s, 1), :].rearrange("p k n -> p (k n)")
                nc.vector.scalar_tensor_tensor(x, bank(2 * s, LAT), ada[:, ds(i * 2 + s + 16, 1), 0], x, ALU.mult, ALU.add)\
                    .then_inc(added[s], 1)
        meet(dve, "out1")
        norm2_dve(dve)
        meet(dve, "norm2")

        def add_down(i):
            for f in range(KT):
                s = f % 2
                if f == KT - 1:
                    dve.wait_ge(wd_done[1], i + 1)
                else:
                    dve.wait_ge(down_mm[s], i * (4 - s) + f // 2 + 1)
                nc.vector.scalar_tensor_tensor(xt[:, f, :], bank(4 + 2 * s, LAT), ada[:, 40 + f, 0:1], xt[:, f, :],
                                               ALU.mult, ALU.add).then_inc(down_added[s], 1)

        def mix_up(i):
            for s in range(2):
                dve.wait_ge(gated[s], i + 1)
                dve.wait_ge(w_done[s], i * 2 + M_FFN + 2)
                nc.vector.tensor_tensor(hid[:, s, :], bank(4 + 2 * s, LAT), gate_s[:, s, :], ALU.mult).then_inc(up_mixed[s], 1)
            for s in range(2):
                dve.wait_ge(hid_rounded[s], i + 1)
                nc.vector.tensor_tensor(hid_lo[:, s, :], hid[:, s, :], hid_hi[:, s, :].bitcast(F32), ALU.subtract)\
                    .then_inc(hid_split[s], 1)

        mix_up(0)
        with dve.Fori(1, FT // 2) as i:
            add_down(i - 1)
            mix_up(i)
        add_down(FT // 2 - 1)
        meet(dve, "ffn")
        norm_f_dve(dve)
        dve.wait_ge(norm_finished, norm_f_before + 2)
        norm3_dve(dve)
        meet(dve, "norm3")
        dve.wait_ge(spilled2, 16)
        for s in range(2):
            last = nc.vector.memset(conv_in[:, s, 0:PAD], 0.0)
        dve_link(last)
        with dve.Fori(0, 6) as i:
            dve_enter(i, 6)
            for s in range(2):
                y = qkv[:, ds(i * 2 + s, 1), :].rearrange("p k n -> p (k n)")
                dve.wait_ge(conv_full[s], i + 1 + CAT_PAIRS)
                tap = lambda j: pcol[:, ds(i * 2 + s + CONV_AT + 12 * j, 1)]
                dve_link(nc.vector.tensor_scalar(y, conv_in[:, s, PAD - 3:PAD - 3 + LAT], tap(0), None, ALU.mult))
                for j in (1, 2, 3):
                    ins = nc.vector.scalar_tensor_tensor(y, conv_in[:, s, PAD - 3 + j:PAD - 3 + j + LAT], tap(j), y, ALU.mult, ALU.add)
                    if j < 3:
                        dve_link(ins)
                    else:
                        ins.then_inc(conv_done[s], 1)
            dve_leave(6, 6)
        dve.wait_ge(ba_hi, 1)
        nc.vector.tensor_tensor(w_ba_lo[:, :, :], w_ba[:, :, :], w_ba_hi[:, :, :].bitcast(F32), ALU.subtract).then_inc(ba_split, 1)
        dve.wait_ge(ba_mm, 1)
        nc.vector.tensor_copy(gb[:, :, :], bank(7, 64).rearrange("p (c n) -> p c n", n=8)).then_inc(ba_kept, 1)
        meet(dve, "dn_proj")
        for f0, scale in ((0, SCALE_S), (2, 1.0)):
            with dve.Fori(0, 2) as i:
                for s in range(2):
                    dve.wait_ge(d_rooted[s], i + f0 + 1 + V_PAIRS + FREE)
                    x = qkv[:, ds(i * 2 + 2 * f0 + s, 1), :].rearrange("p k n -> p (k n)")
                    nc.vector.scalar_tensor_tensor(x, x, scale, rs_d[:, s, :], ALU.mult, ALU.mult).then_inc(d_scaled[s], 1)
        per_head = lambda a: a[:, :].rearrange("p (c n) -> p c n", c=1).broadcast_to([P, 8, 4])
        dve.wait_ge(ba_kept, 1)
        dve_link(nc.vector.tensor_tensor(g_x[:, :, :], gb[:, :, 4:8], per_head(dtb), ALU.add))
        nc.vector.scalar_tensor_tensor(g_e[:, :, :], g_x[:, :, :], -1.0, g_x[:, :, :], ALU.mult, ALU.max).then_inc(g_abs, 1)
        dve.wait_ge(gb_exp, 1)
        nc.vector.tensor_scalar(g_e[:, :, :], g_e[:, :, :], 1.0, None, ALU.add).then_inc(g_one, 1)
        dve_link(nc.vector.tensor_scalar(beta[:, :, :], beta[:, :, :], 1.0, None, ALU.add))
        nc.vector.reciprocal(beta[:, :, :], beta[:, :, :])
        dve.wait_ge(gb_exp, 2)
        dve_link(nc.vector.scalar_tensor_tensor(g_x[:, :, :], g_x[:, :, :], 0.0, g_e[:, :, :], ALU.max, ALU.add))
        nc.vector.scalar_tensor_tensor(g_log[:, :, :], g_x[:, :, :], -1.0, per_head(ealog), ALU.mult, ALU.mult)
        nc.vector.memset(state[:, :, :], 0.0)
        meet(dve, "dn_l2")
        flat = lambda a: a[:, :, :].rearrange("p h n -> p (h n)")
        over_heads = lambda m: m.rearrange("p (h n) -> p h n", h=1).broadcast_to([P, DN, P])
        over_cols = lambda a: a.rearrange("p (h n) -> p h n", n=1).broadcast_to([P, DN, P])
        in_heads = lambda b: bank(b).rearrange("p (h n) -> p h n", h=DN)
        tt_ = nc.vector.tensor_tensor

        def normalise_output(c):
            dve.wait_ge(od_rooted, c)
            tt_(o_n[:, :, :], in_heads(6), over_cols(o_ss[:, :]), ALU.mult).then_inc(on_ready, 1)

        def gate_output(c):
            dve.wait_ge(on_turned, c)
            z = dn[:, :, ds(c * P - P, P)]
            norm_w = pcol[:, ROW_AT["dn_norm_w_2"]:ROW_AT["dn_norm_w_2"] + 1]
            nc.vector.scalar_tensor_tensor(z, in_heads(7), norm_w, z, ALU.mult, ALU.mult).then_inc(dn_kept, 1)

        def delta_chunk(c, first):
            dve.wait_ge(kv_turned, c + FREE)
            nc.vector.tensor_copy(g_st[:, 0:4], g_log[:, ds(c, 1), :].rearrange("p c n -> p (c n)"))
            nc.vector.tensor_copy(g_st[:, 4:8], beta[:, ds(c, 1), :].rearrange("p c n -> p (c n)")).then_inc(g_staged, 1)
            dve.wait_ge(gc_mm, c + 1)
            dve_link(nc.vector.tensor_copy(g_c[:, :], bank(2, 4)))
            dve_did(tt_(tail[:, :], in_heads(0)[:, :, P - 1], g_c[:, :], ALU.subtract))
            dve_link(tt_(gx[:, :, :], over_cols(g_c[:, :]), in_heads(0), ALU.subtract))
            nc.vector.tensor_scalar(flat(gx), flat(gx), 0.0, -1.0, ALU.max, ALU.mult).then_inc(gx_ready, 1)
            if not first:
                normalise_output(c)
            dve.wait_ge(e_done, c + 1)
            dve_link(tt_(dc[:, :, :], dc[:, :, :], over_heads(tri), ALU.mult))
            dve_did(tt_(beta_eg[:, :], g_st[:, 4:8], e_gc[:, :], ALU.mult))
            dve_link(tt_(flat(db), bank(1), flat(dc), ALU.mult))
            dve.wait_ge(kk_mm, c + 1)
            dve_link(tt_(flat(u_t), bank(3), flat(db), ALU.mult))
            dve_link(tt_(ym[:, :, :], u_t[:, :, :], over_heads(level[0]), ALU.mult))
            tt_(tt[:, :, :], over_heads(ident), ym[:, :, :], ALU.subtract).then_inc(tt_first, 1)
            if not first:
                gate_output(c)
            tt_(flat(a_t), bank(4), flat(dc), ALU.mult)
            dve.wait_ge(kv_turned, c + 1 + FREE)
            tt_(kbg[:, :, :], in_heads(5), over_cols(beta_eg[:, :]), ALU.mult)
            tt_(ktail[:, :, :], in_heads(5), over_cols(tail[:, :]), ALU.mult)
            tt_(vbeta[:, :, :], in_heads(6), over_cols(g_st[:, 4:8]), ALU.mult)
            tt_(qg[:, :, :], st_qkv[:, 0:4, :], eg[:, :, :], ALU.mult).then_inc(ops_ready, 1)
            tt_(s_dec[:, :, :], state[:, :, :], over_cols(eg[:, :, P - 1]), ALU.mult)
            for lv in range(1, LEVELS):
                n = c * 2 * (LEVELS - 1) + 2 * (lv - 1)
                two_heads = lambda a, g: a[:, 2 * g:2 * g + 2, :]
                product = lambda b, g: bank(b)[:, 2 * g * P:(2 * g + 2) * P].rearrange("p (h n) -> p h n", h=2)
                for g in range(2):
                    dve.wait_ge(y_mm, n + g + 1 + 2 * A_TILES)
                    tt_(two_heads(ym, g), product(3 * g, g), level[lv].rearrange("p (h n) -> p h n", h=1).broadcast_to([P, 2, P]),
                        ALU.mult).then_inc(y_masked, 1)
                for g in range(2):
                    dve.wait_ge(z_mm, n + g + 1 + A_TILES + FREE)
                    if lv < LEVELS - 1:
                        tt_(two_heads(tm, g), two_heads(tm, g), product(3 * g + 2, g), ALU.subtract).then_inc(t_new, 1)
                    tt_(two_heads(tt, g), two_heads(tt, g), product(3 * g + 1, g), ALU.subtract).then_inc(tt_new, 1)
            dve.wait_ge(uw_kept, c + 1 + A_TILES)
            dve.wait_ge(ws_mm, c + 1 + A_TILES + FREE)
            tt_(flat(v_new), flat(u_s), bank(5), ALU.subtract).then_inc(v_new_ready, 1)
            dve.wait_ge(state_mm, c + 1)
            tt_(flat(state), flat(s_dec), bank(7), ALU.add).then_inc(state_new, 1)

        delta_chunk(0, True)
        with dve.Fori(1, NQ) as c:
            dve_enter(c - 1, 8)
            delta_chunk(c, False)
            dve_leave(8, NQ - 1)
        normalise_output(NQ)
        gate_output(NQ)
        meet(dve, "delta")
        dve.wait_ge(win_in, 48)
        with dve.Fori(0, DN) as h:
            dve_enter(h, 6 * 3 + NQ * 3)

            def rotate(j):
                dst, s = (q_s if j < 3 else k_s)[:, j % 3, :], j % 2
                dve.wait_ge(qk_mm, h * 6 + j + 1 + B_HEADS)
                dve_link(nc.vector.tensor_tensor(dst, tmp_s[:, s, :], cos_s[:, :], ALU.mult))
                dve_link(nc.vector.tensor_tensor(sq_s[:, s, :], bank(6, LAT), sin_s[:, :], ALU.mult))
                dve_link(nc.vector.tensor_tensor(dst, dst, sq_s[:, s, :], ALU.add))
                dve.wait_ge(qk_rooted, h * 6 + j + 1 + B_HEADS)
                nc.vector.tensor_tensor(dst, dst, rs_s[:, :], ALU.mult).then_inc(qk_done, 1)

            for j in range(6):
                rotate(j)
            for j in range(3):
                dve.wait_ge(vs_turned, h * 3 + j + 1 + B_HEADS)
                nc.vector.tensor_copy(v_s[:, j, :, :].rearrange("p q n -> p (q n)"), bank(4, LAT)).then_inc(vs_done, 1)

            def take_output(n):
                s, m = n % 2, h * NQ + n
                dve.wait_ge(s_exp, m + 1 + B_TILES + FREE)
                dve_link(nc.vector.reciprocal(st_w[:, s, 6:7], st_w[:, s, 5:6]))
                dve.wait_ge(so_mm, m + 1 + B_TILES)
                nc.vector.tensor_scalar(on_s[:, s, :], bank(6, P), st_w[:, s, 6:7], None, ALU.mult).then_inc(so_scaled, 1)

            def gate_output(n):
                m = h * NQ + n
                dve.wait_ge(so_turned, m + 1 + B_TILES)
                nc.vector.tensor_tensor(sw[:, ds(h, 1), n * P:(n + 1) * P].rearrange("p h n -> p (h n)"), bank(7, P),
                                        z_s[:, n * P:(n + 1) * P], ALU.mult).then_inc(so_kept, 1)

            dve.wait_ge(zs_in, h + 1)
            for n in range(NQ):
                s, width = n % 2, len(window_tiles(n)) * P
                dve.wait_ge(s_mm, h * NQ + n + 1 + B_TILES)
                nc.vector.memset(st_w[:, s, 7:8], 0.0)
                col = 0
                for g in range(3):
                    w = min(n + 1, SPAN[g]) * P
                    m0 = STRIP[g] + SPAN[g] * P - w
                    last = nc.vector.tensor_tensor_reduce(
                        out=s_m[:, s, col:col + w], in0=ps[:, col:col + w], in1=mask[:, m0:m0 + w], scale=SCALE_S,
                        scalar=-3.0e38, op0=ALU.add, op1=ALU.max, accum_out=st_w[:, s, g:g + 1])
                    col += w
                dve_link(last)
                dve_link(nc.vector.tensor_reduce(st_w[:, s, 3:4], st_w[:, s, 0:3], AX_X, ALU.max))
                nc.vector.tensor_scalar(st_w[:, s, 4:5], st_w[:, s, 3:4], -1.0, None, ALU.mult).then_inc(s_masked, 1)
                if n:
                    take_output(n - 1)
                for b in range(0, BATCHES[n], 2):
                    if b == 2:
                        gate_output(n - 1)
                    dve.wait_ge(s_turned, h * ALL_BATCHES + sum(BATCHES[:n]) + b + 1 + B_TILES)
                    w = min(BANK, width - b * BANK)
                    nc.vector.tensor_copy(pt_s[:, 0, 0:w], bank(4, w)).then_inc(pt_even, 1)
                if n and BATCHES[n] <= 2:
                    gate_output(n - 1)
            take_output(NQ - 1)
            gate_output(NQ - 1)
            dve_leave(6 * 3 + NQ * 3, DN)
        meet(dve, "swa")
        meet(dve, "gates")
        for k, (lo, src, hi) in enumerate(((dn_lo, dn, dn_hi), (sw_lo, sw, sw_hi))):
            dve.wait_ge(split_hi, k + 1)
            nc.vector.tensor_tensor(lo[:, :, :], src[:, :, :], hi[:, :, :].bitcast(F32), ALU.subtract)
        meet(dve, "split2")
        row = lambda a, i: a[:, ds(i, 1), :].rearrange("p k n -> p (k n)")
        with dve.Fori(0, 4) as i:
            dve_enter(i, 4)
            for s in range(2):
                f = i * 2 + s
                dve.wait_ge(w_done[s], i + M_BRANCH + 1)
                dve_did(nc.vector.tensor_tensor(m_t[:, s, :], bank(4 * s, LAT), row(gates, f), ALU.mult))
                dve_link(nc.vector.tensor_tensor(row(gates, f + 8), bank(4 * s + 2, LAT), row(gates, f + 8), ALU.mult))
                nc.vector.tensor_tensor(m_t[:, s, :], m_t[:, s, :], row(gates, f + 8), ALU.add).then_inc(merged[s], 1)
                dve.wait_ge(merged_hi[s], i + 1 + FFN_PAIRS)
                nc.vector.tensor_tensor(row(m_lo, f), m_t[:, s, :], row(m_hi, f).bitcast(F32), ALU.subtract)
            dve_leave(4, 4)
        meet(dve, "branch")
        with dve.Fori(0, 4) as i:
            for s in range(2):
                dve.wait_ge(w_done[s], i + M_OUT2 + 1)
                dve.wait_ge(xp_in[s], i * 16 + 16)
                dve.wait_ge(y_turned[s], i + DOWNS)
                nc.vector.tensor_tensor(y_f[:, s, :], bank(2 * s, LAT), x_piece[:, s, :], ALU.add).then_inc(y_added[s], 1)

    @block.tensor
    def _(pe):
        def turn(dst, src, n=P):
            return nc.tensor.transpose(dst, src, ident[0:n, 0:n])

        pe.wait_ge(consts_in, 16)
        pe.wait_ge(params_in, 16 * (len(ROWS) + 1))
        turn(bank(6, N_ROWS), param_rows[0:N_ROWS, 0, :], N_ROWS).then_inc(params_turned, 1)
        turn(bank(7, 48), param_rows[0:48, 1, :], 48).then_inc(params_turned, 1)

        def turn_x(i):
            for s in range(2):
                pe.wait_ge(x_in[s], i * 16 + 16)
                pe.wait_ge(xt_act[s], i)
                pe.wait_ge(xt_dve[s], i)
                for k in range(KT):
                    last = turn(ps[:, 2 * s * BANK + k * P:2 * s * BANK + (k + 1) * P], x_tile[:, s, k * P:(k + 1) * P])
                last.then_inc(x_turned[s], 1)

        turn_x(0)
        pe.wait_ge(silu_ready, 1)
        for s in range(4):
            pe.wait_ge((*ada_in, *ada_in_2)[s], 16)
            for m in range(4):
                for k in range(KT):
                    last = nc.tensor.matmul(ps[:, 6 * BANK + s * 8 + m * 2:6 * BANK + s * 8 + m * 2 + 2],
                                            ada_w[:, s, k, m * P:(m + 1) * P], silu_c[:, k, :], start=k == 0, stop=k == KT - 1)
            last.then_inc(ada_used[s % 2], 1)
            turn_x(s + 1)
        pe.wait_ge(ada_used[1], 2)
        nc.tensor.matmul(bank(7, 2), ident, ident[:, 0:2], start=True, stop=True).then_inc(ada_mm, 1)
        meet(pe, "input")
        norm1_pe(pe)
        meet(pe, "norm1")
        for m, pieces, n0 in ((M_Q, two, 0), (M_K, three, 2)):
            with pe.Fori(0, 2) as i:
                for s in range(2):
                    pe.wait_ge(rope_done[s], i + n0 + FREE)
                    gemm(pe, i + m, s, h_hi, h_lo, pieces(3 * s))
                for s in range(2):
                    pe.wait_ge(tmp_full[s], i + n0 + 1)
                    for b in range(2):
                        last = nc.tensor.matmul(bank(3 * s + b), rot_a, rope_tmp[:, s, b * BANK:(b + 1) * BANK], start=True, stop=True)
                    last.then_inc(rot_done[s], 1)
        meet(pe, "proj_q")
        with pe.Fori(0, 2) as i:
            for s in range(2):
                pe.wait_ge(v_kept[s], i + FREE)
                gemm(pe, i + M_V, s, h_hi, h_lo, three(3 * s))
            for s in range(2):
                pe.wait_ge(v_full[s], i + 1)
                for kt in range(NKEY):
                    last = turn(ps[:, 3 * s * BANK + kt * P:3 * s * BANK + (kt + 1) * P], v_tmp[:, s, kt * P:(kt + 1) * P])
                last.then_inc(v_turned[s], 1)
        meet(pe, "proj_v")
        for s in range(2):
            gemm(pe, M_C, s, h_hi, h_lo, two(3 * s))
        pe.wait_ge(c_kept, 2)
        for s in range(2):
            gemm(pe, M_C + 1, s, h_hi, h_lo, three(3 * s))
        meet(pe, "proj_c")
        with pe.Fori(0, A_HEADS) as h:
            FIRST, SECOND = ((0, 0, 512), (0, 512, 512), (0, 1024, 256), (1, 0, 256)), ((1, 256, 512), (1, 768, 512))

            def scores(qt, pieces):
                for w, o, n in pieces:
                    last = nc.tensor.matmul(ps[:, w * TOK + o:w * TOK + o + n], qs[:, w, qt * P:(qt + 1) * P],
                                            k_a[:, ds(h, 1), o:o + n], start=True, stop=True)
                last.then_inc(scores_ready, 1)

            def turn_weights(qt):
                pe.wait_ge(mixed, h * NQ + qt + 1)
                pe.wait_ge(o_kept, h * NQ + qt + FREE)
                for kt in range(NKEY):
                    last = turn(ps[:, 5 * BANK + kt * P:5 * BANK + (kt + 1) * P], prob[:, qt % 2, kt * P:(kt + 1) * P])
                last.then_inc(turned, 1)

            def weigh(qt):
                pe.wait_ge(pt_act, h * NQ + qt + 1)
                pe.wait_ge(ada_in[qt % 2], h * 64 + (qt // 2 + 2) * 16)
                for k in range(KT):
                    last = nc.tensor.matmul(ps[:, ds(h * 16 + 7 * BANK + 384 + qt * 2, 2)], ada_w2[:, qt % 2, k, :],
                                            silu_c[:, k, :], start=k == 0, stop=k == KT - 1)
                last.then_inc(ada_used[qt % 2], 1)
                for kt in range(NKEY):
                    last = nc.tensor.matmul(ps[:, 7 * BANK + 256:7 * BANK + 384], pt[:, kt * P:(kt + 1) * P],
                                            v_a[:, kt, ds(h * P, P)], start=kt == 0, stop=kt == NKEY - 1)
                last.then_inc(o_mm, 1)

            pe.wait_ge(q_staged, h + 1)
            for qt in range(NQ):
                pe.wait_ge(e_ready, h * NQ + qt + FREE)
                scores(qt, FIRST)
                if qt:
                    turn_weights(qt - 1)
                scores(qt, SECOND)
                if qt:
                    weigh(qt - 1)
            turn_weights(NQ - 1)
            weigh(NQ - 1)
        meet(pe, "attn_a")
        norm_cq_pe(pe)
        pe.wait_ge(norm_rooted, norm_cq_before + 2)
        norm_kv_pe(pe)
        for b in range(2):
            last = nc.tensor.matmul(ps[0:BD, (4 + b) * BANK:(5 + b) * BANK], rot_b[0:BD, 0:BD], kr[0:BD, b * BANK:(b + 1) * BANK],
                                    start=True, stop=True)
        last.then_inc(kr_rot, 1)
        pe.wait_ge(up_split, 1)
        pe.wait_ge(norm_finished, norm_kv_before + 3)
        kv_v = lambda w: w[:, :].rearrange("p (h a n) -> p h a n", h=B_HEADS, a=2)[:, :, 1, :]
        for kt in range(NKEY):
            if kt >= 2:
                pe.wait_ge(vb_kept, kt - 1)
            for n_pass, (a, w) in enumerate(((ckv_hi, kvup_hi), (ckv_lo, kvup_hi), (ckv_hi, kvup_lo))):
                last = nc.tensor.matmul(bank(kt % 2), a[:, kt * P:(kt + 1) * P], kv_v(w), start=n_pass == 0, stop=n_pass == 2)
            last.then_inc(vb_mm, 1)
        meet(pe, "prep_b")
        for g in range(2):
            for h in range(4):
                n = g * 4 + h
                if n:
                    pe.wait_ge(qb_tmp, n)
                for k in range(2):
                    for n_pass, (w, a) in enumerate(((qup_hi, cq_hi), (qup_hi, cq_lo), (qup_lo, cq_hi))):
                        for b in range(2):
                            last = nc.tensor.matmul(ps[0:BD, b * BANK:(b + 1) * BANK], w[:, k, n * BD:(n + 1) * BD],
                                                    a[:, k, b * BANK:(b + 1) * BANK],
                                                    start=k == 0 and n_pass == 0, stop=k == 1 and n_pass == 2)
                last.then_inc(qb_mm, 1)
                if n:
                    pe.wait_ge(kb_kept, n)
                for n_pass, (w, a) in enumerate(((kvup_hi, ckv_hi), (kvup_hi, ckv_lo), (kvup_lo, ckv_hi))):
                    for b, o, w_n in three(4):
                        last = nc.tensor.matmul(bank(b, w_n), w[:, n * P:(n + 1) * P], a[:, o:o + w_n],
                                                start=n_pass == 0, stop=n_pass == 2)
                last.then_inc(kb_mm, 1)
                pe.wait_ge(qb_tmp, n + 1)
                if n:
                    pe.wait_ge(qb_done, n)
                for b in range(2):
                    last = nc.tensor.matmul(ps[0:BD, (2 + b) * BANK:(3 + b) * BANK], rot_b[0:BD, 0:BD],
                                            tmp_b[0:BD, h % 2, b * BANK:(b + 1) * BANK], start=True, stop=True)
                last.then_inc(qb_rot, 1)
            meet(pe, f"heads_b{g}")
            with pe.Fori(0, 4) as h:
                def scores_b(qt):
                    pe.wait_ge(b_e, h * NQ + g * 32 + max(qt - 1, 0) + FREE)
                    for b, o in enumerate(range(0, TOK, BANK)):
                        n = min(BANK, TOK - o)
                        if b == 2:
                            pe.wait_ge(b_kept, h * NQ + g * 32 + max(qt - 1, 0) + FREE)
                        last = nc.tensor.matmul(bank(3 * (qt % 2) + b, n), qs_b[0:BD, qt * P:(qt + 1) * P],
                                                k_b[0:BD, ds(h, 1), o:o + n], start=True, stop=True)
                    last.then_inc(b_scores, 1)

                def attend_b(qt):
                    n = h * NQ + g * 32 + qt
                    own = (2 + 3 * (qt % 2)) * BANK
                    pe.wait_ge(b_e, n + 1 + FREE)
                    for t0, k0, k1 in ((own + 256, 8, 10), (6 * BANK, 0, 4), (7 * BANK, 4, 8)):
                        for kt in range(k0, k1):
                            last = turn(ps[:, t0 + (kt - k0) * P:t0 + (kt - k0 + 1) * P],
                                        e_b[:, qt % 2, kt * P:(kt + 1) * P])
                        last.then_inc(b_turned, 1)
                    for kt in (8, 9, *range(8)):
                        if kt % 4 == 0:
                            pe.wait_ge((b_pt0, b_pt1, b_pt2)[kt // 4], n + 1)
                        last = nc.tensor.matmul(ps[:, own:own + 64], pt_b[:, kt * P:(kt + 1) * P],
                                                v_b[:, kt, ds(h * 64 + g * 256, 64)], start=kt == 8, stop=kt == 7)
                    last.then_inc(b_av, 1)

                pe.wait_ge(qb_staged, h + g * 4 + 1)
                scores_b(0)
                for qt in range(1, NQ):
                    scores_b(qt)
                    attend_b(qt - 1)
                attend_b(NQ - 1)
            meet(pe, f"attn_b{g}")
        pe.wait_ge(att_ready, 1)
        for f in range(KT):
            s = f % 2
            pe.wait_ge(cat_taken[s], f // 2)
            for qt in range(NQ):
                last = turn(ps[:, 2 * s * BANK + qt * P:2 * s * BANK + (qt + 1) * P], att[:, qt, f * P:(f + 1) * P])
            last.then_inc(cat_turned[s], 1)
        meet(pe, "cat")
        with pe.Fori(0, 4) as i:
            for s in range(2):
                pe.wait_ge(added[s], i + FREE)
                gemm(pe, i + M_OUT, s, cat_hi, cat_lo, two(2 * s))
        meet(pe, "out1")
        norm2_pe(pe)
        meet(pe, "norm2")

        def gate(i, m):
            for s in range(2):
                pe.wait_ge(gated[s], i)
                gemm(pe, m, s, h2_hi, h2_lo, two(2 * s))

        def up(i, m):
            for s in range(2):
                pe.wait_ge(down_added[s], i * 4)
                gemm(pe, m, s, h2_hi, h2_lo, two(4 + 2 * s))

        def down(i):
            for s in range(2):
                pe.wait_ge(hid_split[s], i + 1)
                pe.wait_ge(wd_split[s], i + 1)
            for f in range(KT):
                fs = f % 2
                pe.wait_ge(down_added[fs], i * 4 + f // 2)
                for s in range(2):
                    for n_pass, (w, a) in enumerate(((wd_hi, hid_hi), (wd_hi, hid_lo), (wd_lo, hid_hi))):
                        for b in range(2):
                            last = nc.tensor.matmul(bank(4 + 2 * fs + b), w[:, s, f, :], a[:, s, b * BANK:(b + 1) * BANK],
                                                    start=s == 0 and n_pass == 0, stop=s == 1 and n_pass == 2)
                    if f == KT - 1:
                        last.then_inc(wd_done[s], 1)
                    elif s == 1:
                        last.then_inc(down_mm[fs], 1)

        gate(0, M_FFN)
        up(0, M_FFN + 1)
        with pe.Fori(1, FT // 2) as i:
            gate(i, i * 2 + M_FFN)
            down(i - 1)
            up(i, i * 2 + M_FFN + 1)
        down(FT // 2 - 1)
        meet(pe, "ffn")
        norm_f_pe(pe)
        pe.wait_ge(norm_rooted, norm_f_before + 2)
        norm3_pe(pe)
        meet(pe, "norm3")
        pe.wait_ge(norm_finished, norm3_before + 2)
        with pe.Fori(0, 6) as i:
            for s in range(2):
                pe.wait_ge(conv_full[s], i + CAT_PAIRS)
                gemm(pe, i + M_DN, s, h2_hi, h2_lo, two(2 * s))
        with pe.Fori(0, 2) as i:
            for s in range(2):
                pe.wait_ge(conv_full[s], CAT_PAIRS + 6)
                pe.wait_ge(z_kept[s], i + CAT_PAIRS)
                gemm(pe, i + M_DN + 6, s, h2_hi, h2_lo, two(2 * s))
        pe.wait_ge(ba_split, 1)
        for qt in range(NQ):
            for k in range(KT):
                for n_pass, (w, a) in enumerate(((w_ba_hi, h2_hi), (w_ba_hi, h2_lo), (w_ba_lo, h2_hi))):
                    last = nc.tensor.matmul(ps[:, 7 * BANK + qt * 8:7 * BANK + qt * 8 + 8], a[:, k, qt * P:(qt + 1) * P],
                                            w[:, k, :], start=k == 0 and n_pass == 0, stop=k == KT - 1 and n_pass == 2)
        last.then_inc(ba_mm, 1)
        meet(pe, "dn_proj")
        with pe.Fori(0, 4) as i:
            for s in range(2):
                pe.wait_ge(d_squared[s], i + 1 + V_PAIRS)
                pe.wait_ge(d_rooted[s], i + V_PAIRS + FREE)
                for b in range(2):
                    last = nc.tensor.matmul(bank(2 * s + b), ones_mean, sq_d[:, s, b * BANK:(b + 1) * BANK], start=True, stop=True)
                last.then_inc(d_summed[s], 1)
        meet(pe, "dn_l2")

        def per_head(b, lhs, rhs, which=range(DN)):
            for h in which:
                last = nc.tensor.matmul(bank(b)[:, h * P:(h + 1) * P], lhs(h), rhs(h), start=True, stop=True)
            return last

        pairs = (range(0, 2), range(2, 4))

        of = lambda a: lambda h: a[:, h, :]

        def turn_output(c):
            pe.wait_ge(on_ready, c)
            pe.wait_ge(state_new, c + FREE)
            for h in range(DN):
                last = turn(bank(7)[:, h * P:(h + 1) * P], o_n[:, h, :])
            last.then_inc(on_turned, 1)

        def delta_chunk(c, first):
            pe.wait_ge(g_staged, c + 1)
            per_head(0, lambda h: g_st[:, h:h + 1].broadcast_to([P, P]), lambda h: tri)
            per_head(1, lambda h: g_st[:, 4 + h:5 + h].broadcast_to([P, P]), lambda h: ident)
            nc.tensor.matmul(bank(2, 4), tri, g_st[:, 0:4], start=True, stop=True).then_inc(gc_mm, 1)
            pe.wait_ge(staged, c + 1)
            key = lambda h: st_qkv[:, 4 + h, :]
            per_head(3, key, key)
            per_head(4, key, lambda h: st_qkv[:, h, :]).then_inc(kk_mm, 1)
            if not first:
                turn_output(c)
            for b, g in ((5, 4), (6, 8)):
                for h in range(DN):
                    last = turn(bank(b)[:, h * P:(h + 1) * P], st_qkv[:, g + h, :])
            last.then_inc(kv_turned, 1)
            pe.wait_ge(tt_first, c + 1)
            pe.wait_ge(dn_kept, c + FREE)
            for h in range(DN):
                last = turn(bank(7)[:, h * P:(h + 1) * P], tt[:, h, :])
            last.then_inc(t_turned, 1)
            pe.wait_ge(t_kept, c + 1)
            pe.wait_ge(ops_ready, c + 1 + FREE)
            for lv in range(1, LEVELS):
                for g in range(2):
                    if lv > 1:
                        pe.wait_ge(t_new, c * 2 * (LEVELS - 2) + 2 * (lv - 2) + g + 1 + A_TILES)
                    per_head(3 * g, of(u_t), of(tm), pairs[g]).then_inc(y_mm, 1)
                for g in range(2):
                    pe.wait_ge(y_masked, c * 2 * (LEVELS - 1) + 2 * (lv - 1) + g + 1 + A_TILES)
                    last = per_head(3 * g + 1, of(ym), of(tt), pairs[g])
                    if lv < LEVELS - 1:
                        last = per_head(3 * g + 2, of(tt), of(ym), pairs[g])
                    last.then_inc(z_mm, 1)
            pe.wait_ge(tt_new, c * 2 * (LEVELS - 1) + 2 * (LEVELS - 1) + A_TILES)
            per_head(3, of(tt), of(vbeta))
            per_head(4, of(kbg), of(tt)).then_inc(uw_mm, 1)
            pe.wait_ge(uw_kept, c + 1 + A_TILES)
            pe.wait_ge(state_new, c + FREE)
            per_head(5, of(w_t), of(state)).then_inc(ws_mm, 1)
            pe.wait_ge(v_new_ready, c + 1 + A_TILES + FREE)
            for h in range(DN):
                nc.tensor.matmul(bank(6)[:, h * P:(h + 1) * P], qg[:, h, :], state[:, h, :], start=True, stop=False)
                last = nc.tensor.matmul(bank(6)[:, h * P:(h + 1) * P], a_t[:, h, :], v_new[:, h, :], start=False, stop=True)
            last.then_inc(od_mm, 1)
            per_head(7, of(ktail), of(v_new)).then_inc(state_mm, 1)

        delta_chunk(0, True)
        with pe.Fori(1, NQ) as c:
            delta_chunk(c, False)
        turn_output(NQ)
        meet(pe, "delta")
        with pe.Fori(0, DN) as h:
            def after(c):
                s = c % 2
                if c < 6:
                    pe.wait_ge(qk_in, h * 6 + c + 1 + B_HEADS)
                    pe.wait_ge(qk_done, h * 6 + c + B_HEADS)
                    for b in range(2):
                        nc.tensor.matmul(bank(4 + b), ones_mean, sq_s[:, s, b * BANK:(b + 1) * BANK], start=True, stop=True)
                    for b in range(2):
                        last = nc.tensor.matmul(bank(6 + b), rot_s, tmp_s[:, s, b * BANK:(b + 1) * BANK], start=True, stop=True)
                    last.then_inc(qk_mm, 1)
                elif c < 9:
                    pe.wait_ge(vs_in, h * 3 + c - 5 + B_HEADS)
                    pe.wait_ge(qk_done, h * 6 + 6 + B_HEADS)
                    pe.wait_ge(vs_done, h * 3 + c - 6 + B_HEADS)
                    for q in range(NQ):
                        last = turn(ps[:, 4 * BANK + q * P:4 * BANK + (q + 1) * P], tmp_s[:, s, q * P:(q + 1) * P])
                    last.then_inc(vs_turned, 1)

            pe.wait_ge(s_masked, h * NQ + B_TILES)
            for c in range(10):
                if 2 <= c < 8:
                    pe.wait_ge(qk_in, h * 6 + c - 1 + B_HEADS)
                elif c >= 8:
                    pe.wait_ge(vs_in, h * 3 + c - 7 + B_HEADS)
                gemm(pe, h * 5 + M_SWA + c // 2, c % 2, h2_hi, h2_lo, two(2 * (c % 2)))
                if c:
                    after(c - 1)

            def scores(n):
                pe.wait_ge(s_masked, h * NQ + n + B_TILES)
                for g, kt, col in window_tiles(n):
                    last = nc.tensor.matmul(ps[:, col:col + P], q_s[:, g, n * P:(n + 1) * P], k_s[:, g, kt * P:(kt + 1) * P],
                                            start=True, stop=True)
                last.then_inc(s_mm, 1)

            def attend(n):
                m, tiles = h * NQ + n, window_tiles(n)
                pe.wait_ge(s_exp, m + 1 + B_TILES + FREE)

                def turn_batch(b):
                    for j in range(4 * b, min(4 * b + 4, len(tiles))):
                        last = turn(ps[:, (4 + b % 2) * BANK + (j % 4) * P:(4 + b % 2) * BANK + (j % 4 + 1) * P],
                                    s_m[:, n % 2, j * P:(j + 1) * P])
                    last.then_inc(s_turned, 1)

                def weigh_batch(b):
                    even = sum((x + 1) // 2 for x in BATCHES)
                    odd = sum(x // 2 for x in BATCHES)
                    if b % 2 == 0:
                        pe.wait_ge(pt_even, h * even + sum((x + 1) // 2 for x in BATCHES[:n]) + b // 2 + 1)
                    else:
                        pe.wait_ge(pt_odd, h * odd + sum(x // 2 for x in BATCHES[:n]) + b // 2 + 1)
                    for j in range(4 * b, min(4 * b + 4, len(tiles))):
                        g, kt, _ = tiles[j]
                        last = nc.tensor.matmul(bank(6, P), pt_s[:, b % 2, (j % 4) * P:(j % 4 + 1) * P], v_s[:, g, kt, :],
                                                start=j == 0, stop=j == len(tiles) - 1)
                    return last

                turn_batch(0)
                if n:
                    turn_output(n - 1)
                for b in range(1, BATCHES[n]):
                    turn_batch(b)
                    weigh_batch(b - 1)
                weigh_batch(BATCHES[n] - 1).then_inc(so_mm, 1)

            def turn_output(n):
                m = h * NQ + n
                pe.wait_ge(so_kept, m + B_TILES + FREE)
                pe.wait_ge(so_scaled, m + 1 + B_TILES)
                turn(bank(7, P), on_s[:, n % 2, :]).then_inc(so_turned, 1)

            pe.wait_ge(vs_done, h * 3 + 3 + B_HEADS)
            pe.wait_ge(zs_in, h + 1)
            scores(0)
            for n in range(1, NQ):
                scores(n)
                attend(n - 1)
            attend(NQ - 1)
            turn_output(NQ - 1)
        meet(pe, "swa")
        with pe.Fori(0, 8) as i:
            for s in range(2):
                pe.wait_ge(gate_kept[s], i + FFN_PAIRS)
                gemm(pe, i + M_GATE, s, h2_hi, h2_lo, two(2 * s))
        meet(pe, "gates")
        meet(pe, "split2")
        with pe.Fori(0, 4) as i:
            for s in range(2):
                pe.wait_ge(w_split[s], i + M_BRANCH + 1)
                pe.wait_ge(merged[s], i + FFN_PAIRS)
                for k in range(KT):
                    hi, lo = (dn_hi, dn_lo) if k < 4 else (sw_hi, sw_lo)
                    for n_pass, (w, a) in enumerate(((w_hi, hi), (w_hi, lo), (w_lo, hi))):
                        for b in range(2):
                            last = nc.tensor.matmul(bank(4 * s + 2 * (k // 4) + b), w[:, s, k, :], a[:, k % 4, b * BANK:(b + 1) * BANK],
                                                    start=k % 4 == 0 and n_pass == 0, stop=k % 4 == 3 and n_pass == 2)
                last.then_inc(w_done[s], 1)
        meet(pe, "branch")
        with pe.Fori(0, 4) as i:
            for s in range(2):
                pe.wait_ge(y_added[s], i + CAT_PAIRS + FREE)
                gemm(pe, i + M_OUT2, s, m_hi, m_lo, two(2 * s))
            for s in range(2):
                pe.wait_ge(y_added[s], i + 1 + CAT_PAIRS + FREE)
                pe.wait_ge(y_kept[s], i + FFN_PAIRS)
                for q in range(NQ):
                    last = turn(ps[:, (4 + 2 * s) * BANK + q * P:(4 + 2 * s) * BANK + (q + 1) * P], y_f[:, s, q * P:(q + 1) * P])
                last.then_inc(y_turned[s], 1)

    ctx.close()


_INS = ["x", "c", "ctx", "c_ctx", "w_ada", "b_ada", "w_in", "q_a_norm", "kv_a_norm", "w_q_up", "w_kv_up", "diff_lambda",
        "diff_subln", "w_out", "w_ffn_in", "w_ffn_out", "final_norm", "norm_w_2", "w_in_2", "conv_w_2", "dn_a_log_2",
        "dn_dt_bias_2", "dn_norm_w_2", "q_norm_w_2", "k_norm_w_2", "w_branch_dn_2", "w_branch_swa_2", "w_out_2"]


def kernel(**inputs):
    import concourse.bacc as bacc
    from concourse.bass_utils import run_bass_kernel_spmd

    nc = bacc.Bacc("TRN2", target_bir_lowering=False, num_devices=1)
    arrays = {name: np.ascontiguousarray(inputs[name]) for name in _INS}
    arrays["w_branch"] = np.concatenate([arrays.pop("w_branch_dn_2")[0], arrays.pop("w_branch_swa_2")[0]], axis=0)
    arrays.update(shape_tables())
    tensors = {name: nc.dram_tensor(name, a.shape, F32, kind="ExternalInput").ap() for name, a in arrays.items()}
    tensors["out"] = nc.dram_tensor("out", [1, LAT, D], F32, kind="ExternalOutput").ap()
    build(nc, tensors)
    return run_bass_kernel_spmd(nc, [arrays], core_ids=[0]).results[0]["out"]
```
